# Optimizing a Trainium2 kernel written in Bass

```python
import jax
import jax.numpy as jnp
from jax import lax
import numpy as np
import math
import jax, jax.numpy as jnp

D_MODEL = 1024
BATCH = 1
SEQ = 512
DEPTH = 1

HEAD_DIM = 64
MIX_WIDTH = D_MODEL
A_WIDTH = D_MODEL // 4
A_HEADS = A_WIDTH // HEAD_DIM
A_DK = HEAD_DIM
A_DV = HEAD_DIM
B_WIDTH = D_MODEL // 2
B_BLOCKS = B_WIDTH // HEAD_DIM
B_CONV = 4
LRU_C = 8.0
C_WIDTH = MIX_WIDTH - A_WIDTH - B_WIDTH
C_HEADS = C_WIDTH // HEAD_DIM
C_DV = HEAD_DIM
C_DK = C_DV // 2
C_GATE_RANK = 16
C_GATE_NORM = 16.0
CHUNK = 64
D_FF = 2688
FFN_CONV = 3
EPS = 1e-6
F_FLOOR = 1e-20

IN_SIZES = (A_HEADS * A_DK, A_HEADS * A_DK, A_HEADS * A_DV, A_HEADS * A_DV,
            B_WIDTH, B_WIDTH,
            C_HEADS * C_DK, C_HEADS * C_DK, C_WIDTH, C_WIDTH, C_GATE_RANK)
IN_SPLITS = tuple(int(s) for s in np.cumsum(IN_SIZES)[:-1])
IN_COLS = int(sum(IN_SIZES))


def rmsnorm(x, w):
    xf = x.astype(jnp.float32)
    y = xf * lax.rsqrt(jnp.mean(xf * xf, axis=-1, keepdims=True) + EPS)
    return (y * w.astype(jnp.float32)).astype(x.dtype)

def head_rmsnorm(o, w):
    b, t, h, d = o.shape
    return rmsnorm(o, w.reshape(h, d)).reshape(b, t, h * d)

def causal_dwconv(x, w, bias):
    k_w = w.shape[0]
    t = x.shape[1]
    xp = jnp.pad(x, ((0, 0), (k_w - 1, 0), (0, 0)))
    y = bias + xp[:, k_w - 1:k_w - 1 + t] * w[k_w - 1]
    for k in range(k_w - 1):
        y = y + xp[:, k:k + t] * w[k]
    return y

def chunked_gated_linear_attention(q, k, v, log_f):
    b_sz, t, h, dk = q.shape
    dv = v.shape[-1]
    n = t // CHUNK

    def to_chunks(a):
        return a.astype(jnp.float32).reshape(b_sz, n, CHUNK, h, a.shape[-1]).transpose(1, 0, 3, 2, 4)

    qc, kc, vc, gc = to_chunks(q), to_chunks(k), to_chunks(v), to_chunks(log_f)
    causal = jnp.tril(jnp.ones((CHUNK, CHUNK), dtype=bool))[:, :, None]

    def step(state, inp):
        qi, ki, vi, gi = inp
        cum = jnp.cumsum(gi, axis=2)
        diff = cum[:, :, :, None, :] - cum[:, :, None, :, :]
        decay = jnp.where(causal, jnp.exp(jnp.where(causal, diff, 0.0)), 0.0)
        scores = jnp.einsum('bhid,bhijd,bhjd->bhij', qi, decay, ki)
        last = cum[:, :, -1:, :]
        out = (jnp.einsum('bhij,bhjv->bhiv', scores, vi)
               + jnp.einsum('bhid,bhdv->bhiv', qi * jnp.exp(cum), state))
        state = (jnp.exp(last[:, :, 0, :, None]) * state
                 + jnp.einsum('bhjd,bhjv->bhdv', ki * jnp.exp(last - cum), vi))
        return state, out

    s0 = jnp.zeros((b_sz, h, dk, dv), jnp.float32)
    _, o = lax.scan(step, s0, (qc, kc, vc, gc))
    return o.transpose(1, 0, 3, 2, 4).reshape(b_sz, t, h, dv).astype(q.dtype)

def hgrn2_mixer(q, f_logit, i, g, lower_bound, norm_w):
    b_sz, t, _ = q.shape
    lb = lower_bound.astype(jnp.float32)
    z = f_logit.astype(jnp.float32)
    f = lb + (1.0 - lb) * jax.nn.sigmoid(z)
    log_f = jnp.log(jnp.maximum(f, F_FLOOR))
    key = (1.0 - lb) * jax.nn.sigmoid(-z)
    heads = lambda a, d: a.reshape(b_sz, t, A_HEADS, d)
    o = chunked_gated_linear_attention(heads(q, A_DK), heads(key, A_DK), heads(i, A_DV), heads(log_f, A_DK))
    return head_rmsnorm(o, norm_w) * jax.nn.silu(g)

def rglru_mixer(xb, gb, conv_w, conv_b, w_a, b_a, w_x, b_x, lam):
    b_sz, t, _ = xb.shape
    xc = causal_dwconv(xb, conv_w, conv_b)
    xh = xc.reshape(b_sz, t, B_BLOCKS, HEAD_DIM)
    r = jax.nn.sigmoid(jnp.einsum('bthi,hij->bthj', xh, w_a).reshape(b_sz, t, B_WIDTH) + b_a)
    gi = jax.nn.sigmoid(jnp.einsum('bthi,hij->bthj', xh, w_x).reshape(b_sz, t, B_WIDTH) + b_x)
    log_a = (-LRU_C * r.astype(jnp.float32)) * jax.nn.softplus(-lam.astype(jnp.float32))
    a = jnp.exp(log_a)
    u = jnp.sqrt(jnp.maximum(-jnp.expm1(2.0 * log_a), 0.0)) * (gi * xc).astype(jnp.float32)

    def combine(left, right):
        a1, u1 = left
        a2, u2 = right
        return a1 * a2, a2 * u1 + u2

    _, hs = lax.associative_scan(combine, (a, u), axis=1)
    return hs.astype(xb.dtype) * jax.nn.gelu(gb)

def gla_mixer(q, k, v, g, g_lr, w_g_up, b_g, norm_w):
    b_sz, t, _ = q.shape
    log_f = jax.nn.log_sigmoid((g_lr @ w_g_up + b_g).astype(jnp.float32)) / C_GATE_NORM
    qh = q.reshape(b_sz, t, C_HEADS, C_DK) * (C_DK ** -0.5)
    kh = k.reshape(b_sz, t, C_HEADS, C_DK)
    vh = v.reshape(b_sz, t, C_HEADS, C_DV)
    o = chunked_gated_linear_attention(qh, kh, vh, log_f.reshape(b_sz, t, C_HEADS, C_DK))
    return head_rmsnorm(o, norm_w) * jax.nn.silu(g)

def first_inputs(seed: int = 0) -> dict:
    key = jax.random.key(seed)
    ks = jax.random.split(key, 24)
    f32 = jnp.float32

    def nrm(k, shape, scale):
        return scale * jax.random.normal(k, shape, f32)

    def gain(k, shape):
        return 1.0 + 0.05 * jax.random.normal(k, shape, f32)

    a0 = jax.random.uniform(ks[11], (DEPTH, B_WIDTH), f32, 0.9, 0.999)
    sig = a0 ** (1.0 / LRU_C)
    lam = jnp.log(sig) - jnp.log1p(-sig)
    return {
        'x': jax.random.normal(ks[0], (BATCH, SEQ, D_MODEL), f32),
        'norm_mix': gain(ks[1], (DEPTH, D_MODEL)),
        'w_in': nrm(ks[2], (DEPTH, D_MODEL, IN_COLS), D_MODEL ** -0.5),
        'hgrn_lower_bounds': nrm(ks[3], (DEPTH, A_HEADS * A_DK), 0.5),
        'hgrn_norm': gain(ks[4], (DEPTH, A_HEADS * A_DV)),
        'rg_conv_w': nrm(ks[5], (DEPTH, B_CONV, B_WIDTH), B_CONV ** -0.5),
        'rg_conv_b': nrm(ks[6], (DEPTH, B_WIDTH), 0.05),
        'rg_w_a': nrm(ks[7], (DEPTH, B_BLOCKS, HEAD_DIM, HEAD_DIM), HEAD_DIM ** -0.5),
        'rg_b_a': nrm(ks[8], (DEPTH, B_WIDTH), 0.1),
        'rg_w_x': nrm(ks[9], (DEPTH, B_BLOCKS, HEAD_DIM, HEAD_DIM), HEAD_DIM ** -0.5),
        'rg_b_x': nrm(ks[10], (DEPTH, B_WIDTH), 0.1),
        'rg_lambda': lam,
        'gla_w_gate_up': nrm(ks[12], (DEPTH, C_GATE_RANK, C_HEADS * C_DK), C_GATE_RANK ** -0.5),
        'gla_b_gate': nrm(ks[13], (DEPTH, C_HEADS * C_DK), 0.1),
        'gla_norm': gain(ks[14], (DEPTH, C_WIDTH)),
        'w_out': nrm(ks[15], (DEPTH, MIX_WIDTH, D_MODEL), MIX_WIDTH ** -0.5),
        'norm_ffn': gain(ks[16], (DEPTH, D_MODEL)),
        'ffn_w_gate': nrm(ks[17], (DEPTH, D_MODEL, D_FF), D_MODEL ** -0.5),
        'ffn_w_val': nrm(ks[18], (DEPTH, D_MODEL, D_FF), D_MODEL ** -0.5),
        'ffn_conv_w': nrm(ks[19], (DEPTH, FFN_CONV, D_FF), FFN_CONV ** -0.5),
        'ffn_conv_b': nrm(ks[20], (DEPTH, D_FF), 0.05),
        'ffn_w_down': nrm(ks[21], (DEPTH, D_FF, D_MODEL), D_FF ** -0.5),
        'norm_final': gain(ks[22], (D_MODEL,)),
    }

def first_block(x, norm_mix, w_in, hgrn_lower_bounds, hgrn_norm, rg_conv_w, rg_conv_b, rg_w_a, rg_b_a,
              rg_w_x, rg_b_x, rg_lambda, gla_w_gate_up, gla_b_gate, gla_norm, w_out, norm_ffn,
              ffn_w_gate, ffn_w_val, ffn_conv_w, ffn_conv_b, ffn_w_down, norm_final):
    lb = jax.nn.softmax(hgrn_lower_bounds.astype(jnp.float32), axis=0)
    lb = jnp.cumsum(lb, axis=0) - lb[0]
    for l in range(DEPTH):
        h = rmsnorm(x, norm_mix[l])
        proj = h @ w_in[l]
        a_q, a_f, a_i, a_g, b_x, b_g, c_q, c_k, c_v, c_g, c_lr = jnp.split(proj, IN_SPLITS, axis=-1)
        o_a = hgrn2_mixer(a_q, a_f, a_i, a_g, lb[l], hgrn_norm[l])
        o_b = rglru_mixer(b_x, b_g, rg_conv_w[l], rg_conv_b[l], rg_w_a[l], rg_b_a[l],
                          rg_w_x[l], rg_b_x[l], rg_lambda[l])
        o_c = gla_mixer(c_q, c_k, c_v, c_g, c_lr, gla_w_gate_up[l], gla_b_gate[l], gla_norm[l])
        x = x + jnp.concatenate([o_a, o_b, o_c], axis=-1) @ w_out[l]
        h = rmsnorm(x, norm_ffn[l])
        gate = causal_dwconv(h @ ffn_w_gate[l], ffn_conv_w[l], ffn_conv_b[l])
        x = x + (jax.nn.gelu(gate) * (h @ ffn_w_val[l])) @ ffn_w_down[l]
    return rmsnorm(x, norm_final)


DEPTH_2 = 2

Q_BLOCK = 128
N_MIXERS = 2
DIFF_HEADS = 8
DIFF_HEAD_DIM = D_MODEL // (2 * DIFF_HEADS)
SB_HEADS = 16
SB_HEAD_DIM = D_MODEL // SB_HEADS
N_GROUPS = 4
EXPERTS_PER_GROUP = 8
N_EXPERTS = N_GROUPS * EXPERTS_PER_GROUP
TOP_K = 2
EXPERT_HIDDEN = D_MODEL // 2
MOE_BLOCK = 128
RMS_EPS = 1e-6
SUBLN_EPS = 1e-5


def rms_norm(x, g, eps=RMS_EPS):
    xf = x.astype(jnp.float32)
    y = xf * lax.rsqrt(jnp.mean(xf * xf, axis=-1, keepdims=True) + eps)
    return (y * g.astype(jnp.float32)).astype(x.dtype)

def alibi_slopes(n_heads):
    return jnp.exp2(-8.0 * jnp.arange(1, n_heads + 1, dtype=jnp.float32) / n_heads)

def diff_attention(h, w_in, w_out, lq1, lk1, lq2, lk2, subln_g, lambda_init):
    B, S, D = h.shape
    H, d = DIFF_HEADS, DIFF_HEAD_DIM
    q, k, v = jnp.split(h @ w_in, 3, axis=-1)
    q = q.reshape(B, S, H, 2, d)
    k = k.reshape(B, S, H, 2, d)
    v = v.reshape(B, S, H, 2 * d)
    lam = (jnp.exp(jnp.sum(lq1.astype(jnp.float32) * lk1.astype(jnp.float32)))
           - jnp.exp(jnp.sum(lq2.astype(jnp.float32) * lk2.astype(jnp.float32)))
           + lambda_init)
    slopes = alibi_slopes(H)[None, :, None, None, None]
    scale = 1.0 / math.sqrt(d)
    pos = jnp.arange(S, dtype=jnp.int32)
    outs = []
    for i in range(S // Q_BLOCK):
        q0, q1 = i * Q_BLOCK, (i + 1) * Q_BLOCK
        qb, kb, vb = q[:, q0:q1], k[:, :q1], v[:, :q1]
        tq, tk = pos[q0:q1], pos[:q1]
        s = jnp.einsum('bqhmd,bkhmd->bhmqk', qb, kb).astype(jnp.float32) * scale
        dist = jnp.abs(tq[:, None] - tk[None, :]).astype(jnp.float32)
        allowed = (tk[None, :] // CHUNK) <= (tq[:, None] // CHUNK)
        s = jnp.where(allowed, s - slopes * dist, -jnp.inf)
        p = jax.nn.softmax(s, axis=-1)
        a = p[:, :, 0] - lam * p[:, :, 1]
        outs.append(jnp.einsum('bhqk,bkhe->bqhe', a.astype(vb.dtype), vb))
    o = jnp.concatenate(outs, axis=1)
    o = rms_norm(o, subln_g, SUBLN_EPS) * (1.0 - lambda_init)
    return o.reshape(B, S, D) @ w_out

def stick_breaking_attention(h, w_in, w_out):
    B, S, D = h.shape
    H, d = SB_HEADS, SB_HEAD_DIM
    q, k, v = jnp.split(h @ w_in, 3, axis=-1)
    q = q.reshape(B, S, H, d)
    k = k.reshape(B, S, H, d)
    v = v.reshape(B, S, H, d)
    scale = 1.0 / math.sqrt(d)
    pos = jnp.arange(S, dtype=jnp.int32)
    outs = []
    for i in range(S // Q_BLOCK):
        q0, q1 = i * Q_BLOCK, (i + 1) * Q_BLOCK
        qb, kb, vb = q[:, q0:q1], k[:, :q1], v[:, :q1]
        tq, tk = pos[q0:q1], pos[:q1]
        z = jnp.einsum('bqhd,bkhd->bhqk', qb, kb).astype(jnp.float32) * scale
        strict = tk[None, :] < tq[:, None]
        log_fail = jnp.where(strict, jax.nn.log_sigmoid(-z), 0.0)
        between = lax.cumsum(log_fail, axis=log_fail.ndim - 1, reverse=True) - log_fail
        a = jnp.where(strict, jnp.exp(jax.nn.log_sigmoid(z) + between), 0.0)
        outs.append(jnp.einsum('bhqk,bkhd->bqhd', a.astype(vb.dtype), vb))
    o = jnp.concatenate(outs, axis=1)
    return o.reshape(B, S, D) @ w_out

def expert_dispatch(xf, expert_ids, weights, w_gate, w_up, w_down):
    N, D = xf.shape
    NK = expert_ids.shape[0]
    n_slots = NK + N_EXPERTS * MOE_BLOCK
    n_blocks = n_slots // MOE_BLOCK
    token_ids = jnp.arange(NK, dtype=jnp.int32) // TOP_K
    order = jnp.argsort(expert_ids)
    e_sorted = expert_ids[order]
    counts = jnp.zeros((N_EXPERTS,), jnp.int32).at[expert_ids].add(1)
    padded = (counts + MOE_BLOCK - 1) // MOE_BLOCK * MOE_BLOCK
    starts = jnp.cumsum(counts) - counts
    pad_ends = jnp.cumsum(padded)
    pad_starts = pad_ends - padded
    rank = jnp.arange(NK, dtype=jnp.int32) - starts[e_sorted]
    dest = pad_starts[e_sorted] + rank
    slot_tok = jnp.full((n_slots,), N, jnp.int32).at[dest].set(token_ids[order])
    slot_w = jnp.zeros((n_slots,), jnp.float32).at[dest].set(weights[order])
    block_start = jnp.arange(n_blocks, dtype=jnp.int32) * MOE_BLOCK
    block_expert = jnp.minimum(jnp.searchsorted(pad_ends, block_start, side='right'),
                               N_EXPERTS - 1).astype(jnp.int32)
    x_pad = jnp.concatenate([xf, jnp.zeros((1, D), xf.dtype)], axis=0)
    xs = x_pad[slot_tok].reshape(n_blocks, MOE_BLOCK, D)

    def run_block(args):
        xb, e = args
        hid = jax.nn.silu(xb @ w_gate[e]) * (xb @ w_up[e])
        return hid @ w_down[e]

    ys = lax.map(run_block, (xs, block_expert)).reshape(n_slots, D)
    ys = ys * slot_w[:, None].astype(ys.dtype)
    out = jnp.zeros((N + 1, D), ys.dtype).at[slot_tok].add(ys)
    return out[:N]

def hierarchical_moe(h, w_group, b_group, w_expert, b_expert, w_gate, w_up, w_down):
    B, S, D = h.shape
    N = B * S
    xf = h.reshape(N, D)
    rows = jnp.arange(N, dtype=jnp.int32)
    g_logits = (xf @ w_group).astype(jnp.float32) + b_group.astype(jnp.float32)
    g_prob = jax.nn.softmax(g_logits, axis=-1)
    g_idx = jnp.argmax(g_logits, axis=-1).astype(jnp.int32)
    g_w = g_prob[rows, g_idx][:, None]
    e_all = ((xf @ w_expert).astype(jnp.float32).reshape(N, N_GROUPS, EXPERTS_PER_GROUP)
             + b_expert.astype(jnp.float32))
    e_logits = e_all[rows, g_idx]
    top_v, top_i = lax.top_k(e_logits, TOP_K)
    e_w = jax.nn.softmax(top_v, axis=-1)
    weights = (g_w * e_w).reshape(-1)
    expert_ids = (g_idx[:, None] * EXPERTS_PER_GROUP + top_i.astype(jnp.int32)).reshape(-1)
    y = expert_dispatch(xf, expert_ids, weights, w_gate, w_up, w_down)
    return y.reshape(B, S, D)

def second_inputs(seed: int = 0) -> dict:
    key = jax.random.key(seed)
    ks = jax.random.split(key, 24)
    D, F, E = D_MODEL, EXPERT_HIDDEN, N_EXPERTS
    nA = (DEPTH_2 + 1) // 2
    nB = DEPTH_2 // 2
    dA = DIFF_HEAD_DIM
    nrm = jax.random.normal
    f32 = jnp.float32
    inv = D ** -0.5
    return {
        "x": nrm(ks[0], (BATCH, SEQ, D), f32),
        "c": nrm(ks[1], (BATCH, D), f32),
        "norm1_g": 1.0 + 0.02 * nrm(ks[2], (DEPTH_2, D), f32),
        "norm2_g": 1.0 + 0.02 * nrm(ks[3], (DEPTH_2, D), f32),
        "ada_w": 0.5 * inv * nrm(ks[4], (DEPTH_2, D, 6 * D), f32),
        "ada_b": 0.01 * nrm(ks[5], (DEPTH_2, 6 * D), f32),
        "diff_w_in": inv * nrm(ks[6], (nA, D, 3 * D), f32),
        "diff_w_out": inv * nrm(ks[7], (nA, D, D), f32),
        "diff_lambda_q1": 0.1 * nrm(ks[8], (nA, dA), f32),
        "diff_lambda_k1": 0.1 * nrm(ks[9], (nA, dA), f32),
        "diff_lambda_q2": 0.1 * nrm(ks[10], (nA, dA), f32),
        "diff_lambda_k2": 0.1 * nrm(ks[11], (nA, dA), f32),
        "diff_subln_g": 1.0 + 0.02 * nrm(ks[12], (nA, 2 * dA), f32),
        "sb_w_in": inv * nrm(ks[13], (nB, D, 3 * D), f32),
        "sb_w_out": inv * nrm(ks[14], (nB, D, D), f32),
        "router_group_w": inv * nrm(ks[15], (DEPTH_2, D, N_GROUPS), f32),
        "router_group_b": 0.01 * nrm(ks[16], (DEPTH_2, N_GROUPS), f32),
        "router_expert_w": inv * nrm(ks[17], (DEPTH_2, D, N_GROUPS * EXPERTS_PER_GROUP), f32),
        "router_expert_b": 0.01 * nrm(ks[18], (DEPTH_2, N_GROUPS, EXPERTS_PER_GROUP), f32),
        "expert_w_gate": inv * nrm(ks[19], (DEPTH_2, E, D, F), f32),
        "expert_w_up": inv * nrm(ks[20], (DEPTH_2, E, D, F), f32),
        "expert_w_down": (F ** -0.5) * nrm(ks[21], (DEPTH_2, E, F, D), f32),
        "final_norm_g": 1.0 + 0.02 * nrm(ks[22], (D,), f32),
    }

def second_block(x, c, norm1_g, norm2_g, ada_w, ada_b, diff_w_in, diff_w_out,
              diff_lambda_q1, diff_lambda_k1, diff_lambda_q2, diff_lambda_k2, diff_subln_g,
              sb_w_in, sb_w_out, router_group_w, router_group_b, router_expert_w,
              router_expert_b, expert_w_gate, expert_w_up, expert_w_down, final_norm_g):
    cond = jax.nn.silu(c)
    for i in range(DEPTH_2):
        mod = cond @ ada_w[i] + ada_b[i]
        sh1, sc1, g1, sh2, sc2, g2 = jnp.split(mod[:, None, :], 6, axis=-1)
        h = rms_norm(x, norm1_g[i]) * (1.0 + sc1) + sh1
        j = i // N_MIXERS
        if i % N_MIXERS == 0:
            lambda_init = 0.8 - 0.6 * math.exp(-0.3 * i)
            y = diff_attention(h, diff_w_in[j], diff_w_out[j], diff_lambda_q1[j],
                               diff_lambda_k1[j], diff_lambda_q2[j], diff_lambda_k2[j],
                               diff_subln_g[j], lambda_init)
        else:
            y = stick_breaking_attention(h, sb_w_in[j], sb_w_out[j])
        x = x + g1 * y
        h = rms_norm(x, norm2_g[i]) * (1.0 + sc2) + sh2
        y = hierarchical_moe(h, router_group_w[i], router_group_b[i], router_expert_w[i],
                             router_expert_b[i], expert_w_gate[i], expert_w_up[i],
                             expert_w_down[i])
        x = x + g2 * y
    return rms_norm(x, final_norm_g)


def setup_inputs(seed=0):
    out = dict(first_inputs(seed))
    for name, value in second_inputs(seed + 1).items():
        if name != "x":
            out[name + "_2"] = value
    return out


def reference(
    x, norm_mix, w_in, hgrn_lower_bounds, hgrn_norm, rg_conv_w, rg_conv_b, rg_w_a, rg_b_a,
    rg_w_x, rg_b_x, rg_lambda, gla_w_gate_up, gla_b_gate, gla_norm, w_out, norm_ffn, ffn_w_gate,
    ffn_w_val, ffn_conv_w, ffn_conv_b, ffn_w_down, norm_final, c_2, norm1_g_2, norm2_g_2,
    ada_w_2, ada_b_2, diff_w_in_2, diff_w_out_2, diff_lambda_q1_2, diff_lambda_k1_2,
    diff_lambda_q2_2, diff_lambda_k2_2, diff_subln_g_2, sb_w_in_2, sb_w_out_2, router_group_w_2,
    router_group_b_2, router_expert_w_2, router_expert_b_2, expert_w_gate_2, expert_w_up_2,
    expert_w_down_2, final_norm_g_2,
):
    x = first_block(
        x, norm_mix, w_in, hgrn_lower_bounds, hgrn_norm, rg_conv_w, rg_conv_b, rg_w_a, rg_b_a,
        rg_w_x, rg_b_x, rg_lambda, gla_w_gate_up, gla_b_gate, gla_norm, w_out, norm_ffn,
        ffn_w_gate, ffn_w_val, ffn_conv_w, ffn_conv_b, ffn_w_down, norm_final,
    )
    return second_block(
        x, c_2, norm1_g_2, norm2_g_2, ada_w_2, ada_b_2, diff_w_in_2, diff_w_out_2,
        diff_lambda_q1_2, diff_lambda_k1_2, diff_lambda_q2_2, diff_lambda_k2_2, diff_subln_g_2,
        sb_w_in_2, sb_w_out_2, router_group_w_2, router_group_b_2, router_expert_w_2,
        router_expert_b_2, expert_w_gate_2, expert_w_up_2, expert_w_down_2, final_norm_g_2,
    )


_drawn_inputs = setup_inputs


def setup_inputs(seed=0):
    import zlib

    import numpy as np

    out = dict(_drawn_inputs(seed))
    spreads = {}
    factors = {'rg_b_a': 4.77,
     'rg_b_x': 3.14,
     'gla_b_gate': 3.288,
     'gla_norm': 2.746,
     'norm1_g_2': 4.777,
     'norm2_g_2': 3.682,
     'diff_lambda_q2_2': 4.326,
     'diff_lambda_k2_2': 8.0,
     'diff_subln_g_2': 6.368,
     'router_group_b_2': 6.657,
     'router_expert_b_2': 7.187,
     'final_norm_g_2': 2.954}
    for name, (base, spread) in spreads.items():
        noise = np.random.default_rng([zlib.crc32(name.encode()), seed]).standard_normal(out[name].shape)
        drawn = base * np.exp(spread * noise) if base else spread * noise
        out[name] = jnp.asarray(drawn.astype(out[name].dtype))
    for name, factor in factors.items():
        out[name] = (out[name] * factor).astype(out[name].dtype)
    return out
```

```python
from contextlib import ExitStack, contextmanager

import concourse.bass as bass
from concourse import mybir

ALU = mybir.AluOpType
ACT = mybir.ActivationFunctionType
AX_X = mybir.AxisListType.X
F32 = mybir.dt.float32
I32 = mybir.dt.int32
U8 = mybir.dt.uint8

P = 128
T = 512
TT = T // P
D = 1024
KD = D // P
EPS = 1e-6
SUBLN_EPS = 1e-5

HEAD = 64
A_W, B_W, C_W = 256, 512, 256
A_TILES, B_TILES = A_W // P, B_W // P
C_DK = 32
B_TAPS, FFN_TAPS = 4, 3
RANK = 16
D_FF = 2688
FT = D_FF // P
F_FLOOR = 1e-20
LRU_C = 8.0
GATE_NORM = 16.0
LEVELS = (64, 32, 16, 8, 4, 2, 1)

DIFF_HEADS, SB_HEADS = 8, 16
CHUNK = 64
LAMBDA_INIT = 0.8 - 0.6
GROUPS, PER_GROUP = 4, 8
E = GROUPS * PER_GROUP
HID = 512
KH = HID // P
BLOCK = 64
MAX_BLOCKS = 2 * T // BLOCK + E
PAIRS = MAX_BLOCKS // 2
SLOTS = MAX_BLOCKS * BLOCK

RING = 6
SLOT_F = KD * 512


def head_slopes():
    return [2.0 ** (-8.0 * (h + 1) / DIFF_HEADS) for h in range(DIFF_HEADS)]


class Kit:
    pass


class Chain:

    def __init__(self, eng, sem):
        self.eng, self.sem, self.n = eng, sem, 0

    def mark(self, ins):
        self.n += 1
        ins.then_inc(self.sem, 1)
        return self.n

    def after(self, n):
        self.eng.wait_ge(self.sem, n)

    def link(self, ins):
        self.after(self.mark(ins))




def rows_strided(w):
    return w.rearrange("(p k) n -> p k n", p=P)


def rows_tiled(w):
    return w.rearrange("(k p) n -> p k n", p=P)


class Piece:

    def __init__(self, loads, group, used, used_at):
        self.loads, self.group, self.used, self.used_at = loads, group, used, used_at


class Stream:

    def __init__(self, kit, landed):
        self.kit, self.landed, self.pieces, self.count, self.at = kit, landed, [], [0] * RING, []

    def add(self, loads, group, used, used_at):
        slot = len(self.pieces) % RING
        self.count[slot] += 16 * len(loads)
        self.at.append(self.count[slot])
        self.pieces.append(Piece(loads, group, used, used_at))
        return len(self.pieces) - 1

    def view(self, n, chunks=KD, cols=512):
        flat = self.kit.ring[:, n % RING, 0:chunks * cols]
        return flat.rearrange("p (k n) -> p k n", k=chunks)

    def wait(self, eng, n):
        eng.wait_ge(self.landed[n % RING], self.at[n])

    def load(self, sp, n):
        if n >= RING:
            before = self.pieces[n - RING]
            sp.wait_ge(self.kit.used[before.group][before.used], before.used_at)
        for dst, src in self.pieces[n].loads:
            sp.dma_start(dst, src).then_inc(self.landed[n % RING], 16)




class Norm:

    def __init__(self, k, sems, counts, i):
        self.sems, self.counts, self.i = sems, counts, i
        self.ss, self.vr, self.rt, self.rstd = k.ss, k.vr, k.rt, k.rstd

    def after(self, eng, name, n):
        eng.wait_ge(self.sems[name], self.i * self.counts[name] + n)


NORM_COUNTS = {"sq_act": 2, "sq_dve": 2, "var": 1, "root": 1, "rstd_set": 1, "xn_act": 2, "xn_dve": 2, "turned": KD,
               "hT_act": KD // 2, "hT_dve": KD // 2}
ROW_NORM_COUNTS = {"sq_act": TT, "var": 1, "root": 1, "rstd_set": 1, "normed": TT}


def norm_scalar(act, k, s, x_ready):
    x_ready(act)
    for tt in (0, 1):
        act.activation(k.xn[:, tt, :], k.x[:, tt, :], ACT.Square, accum_out=s.ss[:, tt:tt + 1]).then_inc(s.sems["sq_act"], 1)
    s.after(act, "var", 1)
    act.activation(s.rt[:, :], s.vr[:, :], ACT.Sqrt).then_inc(s.sems["root"], 1)
    s.after(act, "rstd_set", 1)
    s.after(act, "sq_act", 2)
    for tt in (1, 3):
        act.activation(k.xn[:, tt, :], k.x[:, tt, :], ACT.Copy, scale=s.rstd[:, tt:tt + 1]).then_inc(s.sems["xn_act"], 1)
    for c in range(1, KD, 2):
        s.after(act, "turned", c + 1)
        act.activation(k.hT[:, c, :], k.ps[:, c, :], ACT.Identity, bias=s.shift(c), scale=s.gain(c)).then_inc(s.sems["hT_act"], 1)


def norm_vector(dve, k, s, x_ready, gains_ready):
    x_ready(dve)
    for tt in (2, 3):
        dve.tensor_tensor_reduce(k.xn[:, tt, :], k.x[:, tt, :], k.x[:, tt, :], 1.0, 0.0, ALU.mult, ALU.add,
                                 s.ss[:, tt:tt + 1]).then_inc(s.sems["sq_dve"], 1)
    s.after(dve, "sq_dve", 2)
    s.after(dve, "sq_act", 2)
    dve.tensor_scalar(s.vr[:, :], s.ss[:, :], 1.0 / D, EPS, ALU.mult, ALU.add).then_inc(s.sems["var"], 1)
    s.after(dve, "root", 1)
    dve.reciprocal(s.rstd[:, :], s.rt[:, :]).then_inc(s.sems["rstd_set"], 1)
    s.after(dve, "rstd_set", 1)
    for tt in (0, 2):
        dve.tensor_scalar(k.xn[:, tt, :], k.x[:, tt, :], s.rstd[:, tt:tt + 1], None, ALU.mult).then_inc(s.sems["xn_dve"], 1)
    gains_ready(dve)
    for c in range(0, KD, 2):
        s.after(dve, "turned", c + 1)
        dve.tensor_scalar(k.hT[:, c, :], k.ps[:, c, :], s.gain(c), s.shift(c), ALU.mult, ALU.add).then_inc(s.sems["hT_dve"], 1)


def norm_tensor(pe, k, s):
    for tt in range(TT):
        s.after(pe, "xn_act" if tt % 2 else "xn_dve", tt // 2 + 1)
        for c in range(KD):
            mm = pe.transpose(k.ps[:, c, tt * P:(tt + 1) * P], k.xn[:, tt, c::KD], k.ident[:, :])
            if tt == TT - 1:
                mm.then_inc(s.sems["turned"], 1)


def hT_ready(eng, s):
    s.after(eng, "hT_act", KD // 2)
    s.after(eng, "hT_dve", KD // 2)


def row_norm_scalar(act, k, s, x_ready):
    x_ready(act)
    for tt in range(TT):
        act.activation(k.xn[:, tt, :], k.x[:, tt, :], ACT.Square, accum_out=s.ss[:, tt:tt + 1]).then_inc(s.sems["sq_act"], 1)
    s.after(act, "var", 1)
    act.activation(s.rt[:, :], s.vr[:, :], ACT.Sqrt).then_inc(s.sems["root"], 1)


def row_norm_vector(dve, k, s, x_ready, gain, out):
    x_ready(dve)
    s.after(dve, "sq_act", TT)
    dve.tensor_scalar(s.vr[:, :], s.ss[:, :], 1.0 / D, EPS, ALU.mult, ALU.add).then_inc(s.sems["var"], 1)
    s.after(dve, "root", 1)
    dve.reciprocal(s.rstd[:, :], s.rt[:, :]).then_inc(s.sems["rstd_set"], 1)
    s.after(dve, "rstd_set", 1)
    for tt in range(TT):
        dve.scalar_tensor_tensor(out=out[:, tt, :], in0=k.x[:, tt, :], scalar=s.rstd[:, tt:tt + 1], in1=gain,
                                 op0=ALU.mult, op1=ALU.mult).then_inc(s.sems["normed"], 1)




def features(pe, out, w, cols, x, chunks=KD):
    for c in range(chunks):
        mm = pe.matmul(out, w[:, c, cols], x[:, c, :], start=(c == 0), stop=(c == chunks - 1))
    return mm


def tokens(pe, out, x, tt, w, chunks=KD):
    for c in range(chunks):
        mm = pe.matmul(out, x[:, c, tt * P:(tt + 1) * P], w[:, c, :], start=(c == 0), stop=(c == chunks - 1))
    return mm



GATE_JOB, B_GATE_JOB, ADA_JOB = 23, 24, 32
ADA_PIECES = 24
JOBS_1 = ADA_JOB + 2 * ADA_PIECES
PREPS = 2 + len(LEVELS)
N_LEVELS = len(LEVELS) + 1


def unit_of(t, kind, i=0, pair=0):
    base = 10 * t
    if kind == "turn":
        return base
    if kind == "state":
        return base + 1
    return base + 2 + (i if t < 2 else 2 * i + pair)


UNITS = unit_of(2, "level", N_LEVELS - 1, 1) + 1
A_UNITS = unit_of(2, "turn")


def tile_units(t):
    pairs = (0,) if t < 2 else (0, 1)
    out = [("turn", 0, 0), ("state", 0, 0)]
    out += [("level", i, pair) for i in range(N_LEVELS) for pair in pairs]
    return out + [("out", 0, pair) for pair in pairs]


class Tile:

    def __init__(self, k, t):
        self.t = t
        self.dk = HEAD if t < 2 else C_DK
        self.heads = P // self.dk
        self.q = k.qA[:, t, :] if t < 2 else k.qC
        self.key = k.keyA[:, t, :] if t < 2 else k.kC
        self.cum = k.lfA[:, t, :] if t < 2 else k.lfC
        self.v = k.VA if t < 2 else k.VC
        self.v0 = t * P if t < 2 else 0
        self.width = self.heads * HEAD

    def rows(self, h):
        return slice(h * self.dk, (h + 1) * self.dk)


def main_bank(k, j):
    return k.ps[:, j % 2, :]


def unit_banks(k, u):
    b = 4 + 2 * (u % 2)
    return k.ps[:, b, :], k.ps[:, b + 1, :]


def first_block_tensor(pe, k):
    s = k.s

    def free(j):
        if j >= 2:
            pe.wait_ge(s.main_emptied, j - 1)

    def w_in_job(j):
        free(j)
        bank = main_bank(k, j)
        if j < 4:
            if j == 0:
                k.stream1.wait(pe, 0)
            mm = features(pe, bank, k.w(0), slice(j * P, (j + 1) * P), k.hT)
        elif j < 8:
            if j == 4:
                k.stream1.wait(pe, 1)
            mm = tokens(pe, bank, k.hT, j - 4, k.w(1))
        elif j < 16:
            n = 2 if j < 12 else 3
            if j % 4 == 0:
                k.stream1.wait(pe, n)
            mm = features(pe, bank, k.w(n), slice(j % 4 * P, (j % 4 + 1) * P), k.hT)
        elif j < 19:
            if j == 16:
                k.stream1.wait(pe, 4)
            w = k.stream1.view(4, cols=2 * P + RANK)
            if j < 18:
                mm = features(pe, bank, w, slice((j - 16) * P, (j - 15) * P), k.hT)
            else:
                mm = features(pe, bank[0:RANK, :], w, slice(2 * P, 2 * P + RANK), k.hT)
        else:
            if j == 19:
                k.stream1.wait(pe, 5)
            mm = tokens(pe, bank, k.hT, j - 19, k.w(5))
        mm.then_inc(s.main_done, 1)

    def unit(t, kind, i, pair):
        tile = k.tiles[t]
        if kind == "out":
            return out_pair(tile, pair)
        u = unit_of(t, kind, i, pair)
        if u >= 2:
            pe.wait_ge(s.unit_emptied, u - 1)
        a, b = unit_banks(k, u)
        if kind == "turn":
            pe.wait_ge(s.prep_ready, PREPS * t + 1)
            for c in range(TT - 1):
                mm = pe.transpose(a[:, c * P:(c + 1) * P], k.kd[:, c * P:(c + 1) * P], k.ident[:, :])
        elif kind == "state":
            pe.wait_ge(s.unit_emptied, u)
            pe.wait_ge(s.main_emptied, 8 if t < 2 else GATE_JOB)
            for c in range(TT - 1):
                out = a[:, c * P:(c + 1) * P] if t < 2 else (a, b)[c // 2][:, c % 2 * 256:c % 2 * 256 + 256]
                mm = pe.matmul(out, k.kdT[:, c, :], tile.v[:, c, tile.v0:tile.v0 + tile.width], start=True, stop=True)
        else:
            if i < len(LEVELS):
                pe.wait_ge(s.prep_ready, PREPS * t + 3 + i)
                left = right = k.qk[:, i % 2, :]
            else:
                left, right = tile.key, tile.q
            for n, out in enumerate((a, b)):
                rows = tile.rows(2 * pair + n)
                for c in range(TT):
                    tok = slice(c * P, (c + 1) * P)
                    mm = pe.matmul(out[:, tok], left[rows, tok], right[rows, tok], start=True, stop=True)
        mm.then_inc(s.unit_done, 1)

    def out_pair(tile, pair):
        t = tile.t
        u = unit_of(t, "level", N_LEVELS - 1, pair)
        pe.wait_ge(s.unit_emptied, u + 1)
        pe.wait_ge(s.main_emptied, 8 if t < 2 else GATE_JOB)
        if t == 2 and pair == 0:
            pe.wait_ge(s.A_normed, 1)
            pe.wait_ge(s.A_emptied, 2)
        for c in range(TT):
            head = 2 * t if t < 2 else 2 * pair
            col = c % 2 * 256 + head * HEAD
            out = k.ps[:, 2 + c // 2, col:col + P]
            if c:
                pe.matmul(out, k.q0[:, t % 2, c * P:(c + 1) * P], k.st(t, c - 1)[:, pair * P:(pair + 1) * P],
                          start=True, stop=False, skip_group_check=True)
            for n in range(2):
                v = tile.v[:, c, (head + n) * HEAD:(head + n + 1) * HEAD]
                mm = pe.matmul(out[:, n * HEAD:(n + 1) * HEAD], k.scores(t, 2 * pair + n)[:, c * P:(c + 1) * P], v,
                               start=(c == 0), stop=True, skip_group_check=True)
        mm.then_inc(s.out_done, 1)

    def turn_outputs(ready, emptied, at):
        pe.wait_ge(ready, 1)
        for f in range(2):
            for tt in range(TT):
                mm = pe.transpose(k.ps[:, 2 + f, tt * P:(tt + 1) * P], k.onorm[:, tt, f * P:(f + 1) * P], k.ident[:, :])
            mm.then_inc(s.out_turned, 1)

    hT_ready(pe, k.norms[0])
    for j in range(11):
        w_in_job(j)
    todo = [(t, *u) for t in (0, 1) for u in tile_units(t)]
    for j in range(11, GATE_JOB):
        w_in_job(j)
        for u in todo[:2]:
            unit(*u)
        todo = todo[2:]
    for u in todo:
        unit(*u)
    free(GATE_JOB)
    pe.wait_ge(s.main_emptied, 19)
    pe.wait_ge(s.small_landed, 48)
    pe.matmul(main_bank(k, GATE_JOB), k.gate_up[:, :], k.lr[:, :], start=True, stop=True).then_inc(s.main_done, 1)
    turn_outputs(s.A_normed, s.A_emptied, 0)
    pe.wait_ge(s.bd_landed, 16 * 4)
    for t in range(B_TILES):
        for g in range(2):
            j = B_GATE_JOB + 2 * t + g
            free(j)
            pe.wait_ge(s.conv_ready, t + 1)
            pe.matmul(main_bank(k, j), k.bd[:, g, t, :], k.xc[:, t, :], start=True, stop=True).then_inc(s.main_done, 1)
    todo = [(2, *u) for u in tile_units(2)]
    pe.wait_ge(s.cond_ready, 1)
    pe.wait_ge(s.four_ready, 1)
    for a in range(ADA_PIECES):
        j = ADA_JOB + 2 * a
        free(j)
        n = k.ada_piece + a
        k.stream1.wait(pe, n)
        for c in range(KD):
            g = c % 4
            mm = pe.matmul(main_bank(k, j)[32 * g:32 * g + 32, :], k.cond[:, c, :], k.w(n)[:, c, :],
                           start=(c < 4), stop=(c >= 4), skip_group_check=True)
        mm.then_inc(s.main_done, 1)
        if a >= 2 and todo:
            unit(*todo.pop(0))
        free(j + 1)
        pe.wait_ge(s.main_emptied, j + 1)
        pe.matmul(main_bank(k, j + 1)[0:1, :], k.four[:, :], k.part[:, :], start=True, stop=True).then_inc(s.main_done, 1)
        if a >= 2 and todo:
            unit(*todo.pop(0))
    for u in todo:
        unit(*u)
    turn_outputs(s.C_normed, s.C_emptied, 1)
    pe.wait_ge(s.A_emptied, 2)
    pe.wait_ge(s.C_emptied, 2)
    pe.wait_ge(s.oT_pool, B_TILES)
    pe.wait_ge(s.unit_emptied, UNITS)
    pe.wait_ge(s.main_emptied, JOBS_1)
    for half in range(2):
        n = k.w_out_piece + half
        k.stream1.wait(pe, n)
        for tt in range(TT):
            bank = 4 * half + tt
            tokens(pe, k.ps[:, bank, :], k.oT, tt, k.w(n)).then_inc(s.w_out_done, 1)


def first_block_scalar(act, k):
    s = k.s
    items = [("kd", 0), ("q0", 0)] + [("level", i) for i in range(len(LEVELS))]

    def empty(j):
        act.wait_ge(s.main_done, j + 1)
        bank = main_bank(k, j)
        if j < 2:
            ins = act.copy(k.qA[:, j, :], bank)
        elif j < 4:
            act.activation(k.lfA[:, j - 2, :], bank, ACT.Sigmoid)
            ins = act.activation(k.keyA[:, j - 2, :], bank, ACT.Sigmoid, scale=-1.0)
        elif j < 8:
            act.copy(k.VA[:, j - 4, 0:256], bank[:, 0:256])
            ins = act.activation(k.VA[:, j - 4, 256:512], bank[:, 256:512], ACT.Silu)
        elif j < 12:
            ins = act.copy(k.xb[:, j - 8, B_TAPS - 1:], bank)
        elif j < 16:
            if j == 12:
                act.wait_ge(s.masks_ready, 1)
            ins = act.copy(k.gg[:, j - 12, :], bank)
        elif j == 16:
            ins = act.mul(k.qC, bank, C_DK ** -0.5)
        elif j == 17:
            ins = act.copy(k.kC, bank)
        elif j == 18:
            ins = act.copy(k.lr[:, :], bank[0:RANK, :])
        elif j < GATE_JOB:
            act.copy(k.VC[:, j - 19, 0:256], bank[:, 0:256])
            ins = act.activation(k.VC[:, j - 19, 256:512], bank[:, 256:512], ACT.Silu)
        elif j == GATE_JOB:
            ins = act.activation(k.lfC, bank, ACT.Identity, bias=k.col("gla_b", 0), scale=1.0)
        elif j < ADA_JOB:
            t, g = divmod(j - B_GATE_JOB, 2)
            if g == 0:
                if t == 0:
                    act.wait_ge(s.A_normed, 1)
                ins = act.activation(k.ga[:, t, :], bank, ACT.Sigmoid, bias=k.col("rg_b_a", t), scale=1.0)
            else:
                ins = act.activation(k.xb[:, t, B_TAPS - 1:], bank, ACT.Sigmoid, bias=k.col("rg_b_x", t), scale=1.0)
        else:
            a, kind = divmod(j - ADA_JOB, 2)
            if kind == 0:
                ins = act.copy(k.part[:, :], bank)
            else:
                if a:
                    act.wait_ge(s.row_out, 16 * a)
                act.copy(k.row[:, :], bank[0:1, :]).then_inc(s.main_emptied, 1)
                act.wait_ge(s.main_emptied, j + 1)
                act.dma_start(k.mod_dram[a:a + 1, :], k.row[:, :]).then_inc(s.row_out, 16)
                return
        ins.then_inc(s.main_emptied, 1)

    def prep(t, kind, i):
        tile = k.tiles[t]
        if kind == "q0":
            act.wait_ge(s.cum_ready, t + 1)
            if t == 2:
                act.wait_ge(s.out_done, 1)
            act.activation(k.q0[:, t % 2, :], tile.cum, ACT.Exp).then_inc(s.exp_ready, 1)
            return
        n = (PREPS - 1) * t + (0 if kind == "kd" else 1 + i)
        act.wait_ge(s.arg_ready, n + 1)
        arg = k.arg[:, n % 2, :]
        act.activation(arg, arg, ACT.Exp).then_inc(s.exp_ready, 1)

    def head_norm(ready, m):
        act.wait_ge(s.out_done, ready)
        if m == 1:
            act.wait_ge(s.B_sqrt_used, B_TILES)
        act.activation(k.onorm[:, :, :].rearrange("p t c -> p (t c)"), k.ps[:, 2:4, :].rearrange("p b c -> p (b c)"), ACT.Square).then_inc(s.osq[m], 1)
        act.wait_ge(s.ovar[m], 1)
        act.activation(k.hrt[:, m, :], k.hvar[:, m, :], ACT.Sqrt).then_inc(s.oroot[m], 1)

    act.wait_ge(s.cols_ready, 1)
    act.activation(k.sp_e[:, :], k.cols_of("rg_lambda"), ACT.Abs).then_inc(s.par_act, 1)
    act.wait_ge(s.par_act, 1)
    act.activation(k.sp_e[:, :], k.sp_e[:, :], ACT.Exp, scale=-1.0).then_inc(s.par_act, 1)
    act.wait_ge(s.lb_arg, 1)
    act.activation(k.lb_e[:, :], k.lb_e[:, :], ACT.Exp).then_inc(s.par_act, 1)
    act.wait_ge(s.cond_landed, 16)
    act.activation(k.cvec[:, :], k.cvec[:, :], ACT.Silu).then_inc(s.par_act, 1)
    for j in range(9):
        empty(j)
    act.wait_ge(s.f_ready, 1)
    act.activation(k.lfA[:, :, :], k.lfA[:, :, :], ACT.Ln)
    act.activation(k.f2[:, :, :], k.f2[:, :, :], ACT.Ln).then_inc(s.ln_ready, 1)
    todo = [(t, *it) for t in (0, 1) for it in items]
    for j in range(9, GATE_JOB):
        empty(j)
        for it in todo[:2]:
            prep(*it)
        todo = todo[2:]
    head_norm(2, 0)
    empty(GATE_JOB)
    for f in range(2):
        act.wait_ge(s.out_turned, f + 1)
        act.copy(k.oT[:, f, :], k.ps[:, 2 + f, :]).then_inc(s.A_emptied, 1)
    act.wait_ge(s.main_emptied, GATE_JOB + 1)
    act.activation(k.f2c, k.lfC, ACT.Abs).then_inc(s.par_act, 1)
    act.wait_ge(s.par_act, 5)
    act.activation(k.f2c, k.f2c, ACT.Exp, scale=-1.0).then_inc(s.par_act, 1)
    act.wait_ge(s.par_act, 6)
    act.activation(k.f2c, k.f2c, ACT.Ln, bias=k.one_col, scale=1.0).then_inc(s.ln_ready, 1)
    for j in range(B_GATE_JOB, ADA_JOB):
        empty(j)
    for t in range(B_TILES):
        act.activation(k.gg[:, t, :], k.gg[:, t, :], ACT.Gelu_apprx_tanh).then_inc(s.gelu_ready, 1)
    todo = [(2, *it) for it in items]
    for j in range(ADA_JOB, JOBS_1):
        empty(j)
        if todo and j > ADA_JOB + 1:
            prep(*todo.pop(0))
        t, step = divmod(j - (ADA_JOB + 12), 3)
        if 0 <= t < B_TILES and step == 0:
            act.wait_ge(s.par_pool, 1)
            if t >= 2:
                act.wait_ge(s.B_sqrt_used, t - 1)
            act.activation(k.th[:, t % 2, :], k.ga[:, t, :], ACT.Tanh, scale=k.sp8[:, t:t + 1]).then_inc(s.B_tanh, 1)
            act.wait_ge(s.B_tanh, t + 1)
            act.activation(k.ga[:, t, :], k.ga[:, t, :], ACT.Exp, scale=k.sp8n[:, t:t + 1]).then_inc(s.B_a, 1)
        if 0 <= t < B_TILES and step == 1:
            act.wait_ge(s.B_square, t + 1)
            act.activation(k.th[:, t % 2, :], k.th[:, t % 2, :], ACT.Sqrt).then_inc(s.B_sqrt, 1)
    head_norm(4, 1)
    for f in range(2):
        act.wait_ge(s.out_turned, 3 + f)
        act.copy(k.oT[:, 6 + f, :], k.ps[:, 2 + f, :]).then_inc(s.C_emptied, 1)


def first_block_vector(dve, k, ch):
    s = k.s
    n_units = [0]

    dve.wait_ge(s.cols_ready, 1)
    lb = k.cols_of("lower")
    dve.tensor_tensor(k.lb_e[:, :], lb, lb, ALU.subtract).then_inc(s.lb_arg, 1)
    dve.wait_ge(s.par_act, 3)
    ch.link(dve.reciprocal(k.lb_r[:, :], k.lb_e[:, :]))
    ch.link(dve.tensor_tensor(k.lb_e[:, :], k.lb_e[:, :], k.lb_r[:, :], ALU.mult))
    ch.link(dve.tensor_tensor(k.lb[:, :], k.lb_e[:, :], k.lb_e[:, :], ALU.subtract))
    ch.link(dve.tensor_scalar(k.lb1[:, :], k.lb[:, :], -1.0, 1.0, ALU.mult, ALU.add))
    dve.wait_ge(s.par_act, 2)
    ch.link(dve.tensor_scalar(k.sp_x[:, :], k.sp_e[:, :], 2.0, None, ALU.add))
    dve.reciprocal(k.sp_x[:, :], k.sp_x[:, :]).then_inc(s.sp_recip, 1)
    dve.wait_ge(s.par_act, 4)
    dve.tensor_copy(k.cond[:, :, :], k.cvec[:, :].unsqueeze(2).to_broadcast([P, KD, 32])).then_inc(s.cond_ready, 1)
    for t in range(A_TILES):
        dve.wait_ge(s.main_emptied, 3 + t)
        f = k.lfA[:, t, :]
        a = ch.mark(dve.tensor_scalar(f, f, k.lb1[:, t:t + 1], k.lb[:, t:t + 1], ALU.mult, ALU.add))
        ch.mark(dve.tensor_scalar(k.keyA[:, t, :], k.keyA[:, t, :], k.lb1[:, t:t + 1], None, ALU.mult))
        ch.after(a)
        ch.link(dve.tensor_scalar(k.f2[:, t, :], f, F_FLOOR, 2.0 ** 60, ALU.max, ALU.mult))
        ch.mark(dve.tensor_scalar(k.f2[:, t, :], k.f2[:, t, :], 1.0, None, ALU.min))
        ins = dve.tensor_scalar(f, f, 2.0 ** -60, None, ALU.max)
        if t == 0:
            ch.mark(ins)
        else:
            ins.then_inc(s.f_ready, 1)
    dve.wait_ge(s.ln_ready, 1)
    for t in range(A_TILES):
        ch.link(dve.tensor_tensor(k.lfA[:, t, :], k.lfA[:, t, :], k.f2[:, t, :], ALU.add))

    def cumulate(t):
        cum = k.tiles[t].cum
        for c in range(TT):
            part = cum[:, c * P:(c + 1) * P]
            ins = dve.tensor_tensor_scan(part, k.ones[:, :], part, 0.0, ALU.mult, ALU.add)
        ins.then_inc(s.cum_ready, 1)
        dve.wait_ge(s.cum_ready, t + 1)

    def prep(t, kind, i):
        tile = k.tiles[t]
        n = (PREPS - 1) * t + (0 if kind == "kd" else 1 + i)
        p = PREPS * t + {"kd": 0, "q0": 1}.get(kind, 2 + i)
        dve.wait_ge(s.exp_ready, p + 1)
        if kind == "kd":
            if t:
                dve.wait_ge(s.unit_done, unit_of(t - 1, "turn") + 1)
            ins = dve.tensor_tensor(k.kd[:, :], tile.key, k.arg[:, n % 2, :], ALU.mult)
        elif kind == "q0":
            q0 = k.q0[:, t % 2, :]
            ins = dve.tensor_tensor(q0, q0, tile.q, ALU.mult)
        else:
            if i >= 2:
                dve.wait_ge(s.unit_done, unit_of(t, "level", i - 2, 1 if t == 2 else 0) + 1)
            elif t:
                dve.wait_ge(s.unit_done, unit_of(t, "turn"))
            seg = {"l": LEVELS[i], "h": 2}
            out = k.qk[:, i % 2, :].rearrange("p (s h l) -> p s h l", **seg)
            e = k.arg[:, n % 2, :].rearrange("p (s h l) -> p s h l", **seg)
            kk = tile.key.rearrange("p (s h l) -> p s h l", **seg)
            qq = tile.q.rearrange("p (s h l) -> p s h l", **seg)
            dve.tensor_tensor(out[:, :, 0, :], kk[:, :, 0, :], e[:, :, 0, :], ALU.mult)
            ins = dve.tensor_tensor(out[:, :, 1, :], qq[:, :, 1, :], e[:, :, 1, :], ALU.mult)
        ins.then_inc(s.prep_ready, 1)

    def empty(t, kind, i=0, pair=0):
        tile = k.tiles[t]
        u = unit_of(t, kind, i, pair)
        assert u == n_units[0]
        n_units[0] += 1
        dve.wait_ge(s.unit_done, u + 1)
        a, b = unit_banks(k, u)
        if kind == "turn":
            if t:
                dve.wait_ge(s.out_done, t)
            ins = dve.tensor_copy(k.kdT[:, :, :].rearrange("p c d -> p (c d)"), a[:, 0:3 * P])
        elif kind == "state":
            for c in range(TT - 1):
                m = ch.mark(dve.memset(k.st(t, c), 0.0))
            ch.after(m)
            for c in range(TT - 1):
                for h in range(tile.heads):
                    own = slice(h * HEAD, (h + 1) * HEAD)
                    r = tile.rows(h)
                    src = (a[r, c * P + h * HEAD:c * P + (h + 1) * HEAD] if t < 2 else
                           (a, b)[c // 2][r, c % 2 * 256 + h * HEAD:c % 2 * 256 + (h + 1) * HEAD])
                    if c == 0:
                        m = dve.tensor_copy(k.st(t, 0)[r, own], src)
                    else:
                        m = dve.scalar_tensor_tensor(out=k.st(t, c)[r, own], in0=k.st(t, c - 1)[r, own], scalar=k.eL[r, c:c + 1],
                                                     in1=src, op0=ALU.mult, op1=ALU.add)
                    if c < TT - 2:
                        m = ch.mark(m)
                if c < TT - 2:
                    ch.after(m)
            ins = m
        else:
            mask = k.masks[:, i, :].unsqueeze(1).to_broadcast([P, TT, P])
            if i == 0 and pair == 0 and t:
                dve.wait_ge(s.out_done, t)
            if i == 0 and t == 0:
                dve.wait_ge(s.masks_ready, 1)
                dve.wait_ge(s.S_clear, 1)
            if i:
                dve.wait_ge(s.unit_emptied, u if t < 2 else u - 1)
            for n, bank in enumerate((a, b)):
                sc = k.scores(t, 2 * pair + n)
                ins = dve.copy_predicated(sc.rearrange("p (c i) -> p c i", c=TT), mask, bank.rearrange("p (c i) -> p c i", c=TT))
        ins.then_inc(s.unit_emptied, 1)

    def attend(t):
        cumulate(t)
        prep(t, "kd", 0)
        dve.wait_ge(s.exp_ready, PREPS * t + 2)
        ends = k.q0[:, t % 2, :].rearrange("p (c i) -> p c i", c=TT)[:, :, P - 1]
        ch.link(dve.tensor_copy(k.eL[:, :], ends))
        prep(t, "q0", 0)
        prep(t, "level", 0)
        prep(t, "level", 1)
        empty(t, "turn")
        empty(t, "state")
        for i in range(N_LEVELS):
            for pair in range(1 if t < 2 else 2):
                empty(t, "level", i, pair)
            if i + 2 < len(LEVELS):
                prep(t, "level", i + 2)
            if t == 2 and i in (2, 4, 5, 7):
                recur((2, 4, 5, 7).index(i))

    def recur(t):
        gi, a, th, xc = k.xb[:, t, B_TAPS - 1:], k.ga[:, t, :], k.th[:, t % 2, :], k.xc[:, t, :]
        dve.wait_ge(s.main_emptied, B_GATE_JOB + 2 * t + 2)
        m = ch.mark(dve.tensor_tensor(xc, gi, xc, ALU.mult))
        dve.wait_ge(s.B_a, t + 1)
        ch.after(m)
        ch.link(dve.tensor_tensor(gi, a, a, ALU.mult))
        ch.link(dve.scalar_tensor_tensor(out=th, in0=gi, scalar=1.0, in1=th, op0=ALU.add, op1=ALU.mult))
        dve.tensor_scalar(th, th, 0.0, None, ALU.max).then_inc(s.B_square, 1)
        dve.wait_ge(s.B_sqrt, t + 1)
        dve.tensor_tensor(xc, xc, th, ALU.mult).then_inc(s.B_sqrt_used, 1)
        dve.wait_ge(s.B_sqrt_used, t + 1)
        dve.tensor_tensor_scan(gi, a, xc, 0.0, ALU.mult, ALU.add).then_inc(s.B_scan, 1)

    def head_norm(m, v, normed):
        dve.wait_ge(s.osq[m], 1)
        sq = k.onorm[:, :, :].rearrange("p t (h d) -> p (t h) d", d=HEAD)
        ch.link(dve.tensor_reduce(k.hss[:, m, :], sq, AX_X, ALU.add))
        dve.tensor_scalar(k.hvar[:, m, :], k.hss[:, m, :], 1.0 / HEAD, EPS, ALU.mult, ALU.add).then_inc(s.ovar[m], 1)
        dve.wait_ge(s.oroot[m], 1)
        ch.link(dve.reciprocal(k.hrs[:, m, :], k.hrt[:, m, :]))
        ch.link(dve.tensor_tensor(sq, k.ps[:, 2:4, :].rearrange("p b (x d) -> p (b x) d", d=HEAD),
                                  k.hrs[:, m, :].unsqueeze(2).to_broadcast([P, 16, HEAD]), ALU.mult))
        dve.wait_ge(s.gw_ready, m + 1)
        dve.tensor_tensor(k.onorm[:, :, :], k.onorm[:, :, :], v[:, :, 256:512], ALU.mult).then_inc(normed, 1)

    attend(0)
    attend(1)
    head_norm(0, k.VA, s.A_normed)
    for t in range(B_TILES):
        dve.wait_ge(s.main_emptied, 9 + t)
        dve.wait_ge(s.pads_ready, 1)
        out = k.xc[:, t, :]
        ch.link(dve.tensor_scalar(out, k.xb[:, t, 3:3 + T], k.col("rg_w", 3 * B_TILES + t), k.col("rg_b", t), ALU.mult, ALU.add))
        for tap in range(B_TAPS - 1):
            ins = dve.scalar_tensor_tensor(out=out, in0=k.xb[:, t, tap:tap + T], scalar=k.col("rg_w", tap * B_TILES + t),
                                           in1=out, op0=ALU.mult, op1=ALU.add)
            if tap < B_TAPS - 2:
                ch.link(ins)
        ins.then_inc(s.conv_ready, 1)
    dve.wait_ge(s.ln_ready, 2)
    ch.link(dve.tensor_scalar(k.lfC, k.lfC, 0.0, 1.0 / GATE_NORM, ALU.min, ALU.mult))
    ch.link(dve.scalar_tensor_tensor(out=k.lfC, in0=k.f2c, scalar=-1.0 / GATE_NORM, in1=k.lfC, op0=ALU.mult, op1=ALU.add))
    dve.wait_ge(s.out_done, 2)
    dve.wait_ge(s.unit_done, A_UNITS)
    ch.link(dve.memset(k.S_late[:, :, :], 0.0))
    attend(2)
    head_norm(1, k.VC, s.C_normed)
    dve.wait_ge(s.x_again, 16)
    for half in range(2):
        for tt in range(TT):
            j = 4 * half + tt
            dve.wait_ge(s.w_out_done, j + 1)
            xs = k.x[:, tt, half * 512:(half + 1) * 512]
            dve.tensor_tensor(xs, xs, k.ps[:, j, :], ALU.add).then_inc(s.x1_ready, 1)


def first_block_gpsimd(pool, k):
    s = k.s
    ch = Chain(pool, s.pool_chain)
    make_constants(pool, k, ch)

    def prep(t, kind, i):
        tile = k.tiles[t]
        n = (PREPS - 1) * t + (0 if kind == "kd" else 1 + i)
        if n >= 2:
            t2, m = divmod(n - 2, PREPS - 1)
            pool.wait_ge(s.prep_ready, PREPS * t2 + (1 if m == 0 else 2 + m))
        arg = k.arg[:, n % 2, :]
        if kind == "kd":
            pool.wait_ge(s.cum_ready, t + 1)
            c = tile.cum.rearrange("p (c i) -> p c i", c=TT)
            ins = pool.tensor_tensor(arg.rearrange("p (c i) -> p c i", c=TT), c[:, :, P - 1:P].to_broadcast([P, TT, P]), c, ALU.subtract)
        else:
            half = LEVELS[i]
            c = tile.cum.rearrange("p (s h l) -> p s h l", h=2, l=half)
            out = arg.rearrange("p (s h l) -> p s h l", h=2, l=half)
            mid = c[:, :, 0, half - 1:half].to_broadcast([P, T // (2 * half), half])
            pool.tensor_tensor(out[:, :, 0, :], mid, c[:, :, 0, :], ALU.subtract)
            ins = pool.tensor_tensor(out[:, :, 1, :], c[:, :, 1, :], mid, ALU.subtract)
        ins.then_inc(s.arg_ready, 1)

    def gate_gain(v, cols, at):
        pool.wait_ge(s.main_emptied, at)
        pool.tensor_tensor(v[:, :, 256:512], v[:, :, 256:512], cols.unsqueeze(1).to_broadcast([P, TT, 256]), ALU.mult)\
            .then_inc(s.gw_ready, 1)

    def softplus():
        e, x, y, z = k.sp_e, k.sp_x, k.sp_y, k.sp_z
        pool.wait_ge(s.sp_recip, 1)
        ch.link(pool.tensor_tensor(x[:, :], e[:, :], x[:, :], ALU.mult))
        ch.link(pool.tensor_tensor(z[:, :], x[:, :], x[:, :], ALU.mult))
        ch.link(pool.tensor_scalar(y[:, :], z[:, :], 1.0 / 19, 1.0 / 17, ALU.mult, ALU.add))
        for n in (15, 13, 11, 9, 7, 5, 3, 1):
            ch.link(pool.tensor_tensor(y[:, :], y[:, :], z[:, :], ALU.mult))
            ch.link(pool.tensor_scalar(y[:, :], y[:, :], 1.0 / n, None, ALU.add))
        ch.link(pool.tensor_tensor(y[:, :], y[:, :], x[:, :], ALU.mult))
        ch.link(pool.tensor_scalar(z[:, :], k.cols_of("rg_lambda"), -1.0, 0.0, ALU.mult, ALU.max))
        ch.link(pool.tensor_scalar(y[:, :], y[:, :], 2.0, None, ALU.mult))
        ch.link(pool.tensor_tensor(y[:, :], y[:, :], z[:, :], ALU.add))
        ch.link(pool.tensor_scalar(k.sp8[:, :], y[:, :], LRU_C, None, ALU.mult))
        pool.tensor_scalar(k.sp8n[:, :], y[:, :], -LRU_C, None, ALU.mult).then_inc(s.par_pool, 1)

    softplus()
    pool.wait_ge(s.small_landed, 48)
    gate_gain(k.VA, k.normw[:, 0:256], 8)
    for t in (0, 1):
        for kind, i in [("kd", 0)] + [("level", i) for i in range(len(LEVELS))]:
            prep(t, kind, i)
    pool.wait_ge(s.unit_done, A_UNITS)
    pool.wait_ge(s.prep_ready, 2 * PREPS)
    pool.memset(k.bd[:, :, :, :], 0.0).then_inc(s.bd_clear, 1)
    pool.wait_ge(s.bd_clear, 1)
    for g, w in enumerate((k.rg_w_a, k.rg_w_x)):
        for b in range(2):
            rows = slice(b * HEAD, (b + 1) * HEAD)
            pool.dma_start(k.bd[rows, g, :, rows], w[0].rearrange("(t b) i j -> b i t j", b=2)[b]).then_inc(s.bd_landed, 16)
    gate_gain(k.VC, k.normw[:, 256:512], GATE_JOB)
    for kind, i in [("kd", 0)] + [("level", i) for i in range(len(LEVELS))]:
        prep(2, kind, i)
    for t in range(B_TILES):
        pool.wait_ge(s.B_scan, t + 1)
        pool.wait_ge(s.gelu_ready, t + 1)
        pool.tensor_tensor(k.oT[:, 2 + t, :], k.xb[:, t, B_TAPS - 1:], k.gg[:, t, :], ALU.mult).then_inc(s.oT_pool, 1)




def gate_tiles(c):
    return range(4 * c, min(4 * c + 4, FT))


FFN_PIECES = (FT + 3) // 4
DOWN_CHUNKS = [(0, 8), (8, 8), (16, 5)]


def ffn_tensor(pe, k):
    s = k.s
    hT_ready(pe, k.norms[1])
    for c in range(FFN_PIECES):
        cols = len(gate_tiles(c)) * P
        for val in range(2):
            n = k.ffn_piece + 2 * c + val
            k.stream1.wait(pe, n)
            for g in gate_tiles(c):
                if g >= 4:
                    pe.wait_ge(s.ffn_val_out if val else s.ffn_gate_out, g - 3)
                mm = features(pe, k.ps[:, 4 * val + g % 4, :], k.stream1.view(n, cols=cols),
                              slice(g % 4 * P, (g % 4 + 1) * P), k.hT)
                mm.then_inc(s.ffn_val if val else s.ffn_gate, 1)
    pe.wait_ge(s.ffn_gate_out, FT)
    pe.wait_ge(s.ffn_val_out, FT)
    for half in range(2):
        for r, (c0, nc_) in enumerate(DOWN_CHUNKS):
            n = k.down_piece + 3 * half + r
            k.stream1.wait(pe, n)
            w = k.stream1.view(n, chunks=nc_)
            for tt in range(TT):
                for c in range(nc_):
                    mm = pe.matmul(k.ps[:, 4 * half + tt, :], k.actT[:, c0 + c, tt * P:(tt + 1) * P], w[:, c, :],
                                   start=(c0 + c == 0), stop=(c0 + c == FT - 1))
                if r == len(DOWN_CHUNKS) - 1:
                    mm.then_inc(s.down_done, 1)
                elif tt == TT - 1:
                    mm.then_inc(s.down_piece_used, 1)


def ffn_scalar(act, k):
    s = k.s

    def gelu(g):
        act.wait_ge(s.ffn_conv, g + 1)
        if g >= 4:
            act.wait_ge(s.ffn_val_out, g - 3)
        act.activation(k.gelu[:, g % 4, :], k.conv[:, g % 2, :], ACT.Gelu_apprx_tanh).then_inc(s.ffn_gelu, 1)

    act.wait_ge(s.ffn_pads, 1)
    for g in range(FT + 1):
        if g < FT:
            act.wait_ge(s.ffn_gate, g + 1)
            if g >= 2:
                act.wait_ge(s.ffn_conv, g - 1)
            act.copy(k.gpad[:, g % 2, FFN_TAPS - 1:], k.ps[:, g % 4, :]).then_inc(s.ffn_gate_out, 1)
        if g:
            gelu(g - 1)


def ffn_vector(dve, k, ch):
    s = k.s
    hT_ready(dve, k.norms[1])
    dve.memset(k.gpad[:, :, 0:FFN_TAPS - 1], 0.0).then_inc(s.ffn_pads, 1)
    for c in range(FFN_PIECES):
        for g in gate_tiles(c):
            dve.wait_ge(s.ffn_gate_out, g + 1)
            if g >= 2:
                dve.wait_ge(s.ffn_gelu, g - 1)
            out, src = k.conv[:, g % 2, :], k.gpad[:, g % 2, :]
            ch.link(dve.tensor_scalar(out, src[:, 2:2 + T], k.col("ffn_w", 2 * FT + g), k.col("ffn_b", g), ALU.mult, ALU.add))
            ch.link(dve.scalar_tensor_tensor(out=out, in0=src[:, 0:T], scalar=k.col("ffn_w", g), in1=out,
                                             op0=ALU.mult, op1=ALU.add))
            dve.scalar_tensor_tensor(out=out, in0=src[:, 1:1 + T], scalar=k.col("ffn_w", FT + g), in1=out,
                                     op0=ALU.mult, op1=ALU.add).then_inc(s.ffn_conv, 1)
        for g in gate_tiles(c):
            dve.wait_ge(s.ffn_val, g + 1)
            dve.wait_ge(s.ffn_gelu, g + 1)
            dve.tensor_tensor(k.actT[:, g, :], k.ps[:, 4 + g % 4, :], k.gelu[:, g % 4, :], ALU.mult).then_inc(s.ffn_val_out, 1)
    for half in range(2):
        for tt in range(TT):
            dve.wait_ge(s.down_done, 4 * half + tt + 1)
            xs = k.x[:, tt, half * 512:(half + 1) * 512]
            dve.tensor_tensor(xs, xs, k.ps[:, 4 * half + tt, :], ALU.add).then_inc(s.x2_ready, 1)



QKV_JOBS = 24


def qkv_tensor(pe, k, a):
    for j in range(QKV_JOBS):
        n = a.first_piece + j // 4
        if j % 4 == 0:
            a.stream.wait(pe, n)
        if j == 0:
            hT_ready(pe, a.norm)
        if j >= 4:
            pe.wait_ge(a.proj_dve if j % 2 else a.proj_act, (j - 4) // 2 + 1)
        bank = k.ps[:, j % 4, :]
        if j < 16:
            mm = features(pe, bank, a.stream.view(n), slice(j % 4 * P, (j % 4 + 1) * P), k.hT)
        else:
            mm = tokens(pe, bank, k.hT, j % 4, a.stream.view(n))
        mm.then_inc(a.proj, 1)


def qkv_out(k, j):
    if j < 8:
        return k.q[:, j, :]
    if j < 16:
        return k.k[:, j - 8, :]
    return k.v[:, j % 4, (j - 16) // 4 * 512:((j - 16) // 4 + 1) * 512]


def qkv_scalar(act, k, a):
    for j in range(0, QKV_JOBS, 2):
        act.wait_ge(a.proj, j + 1)
        act.mul(qkv_out(k, j), k.ps[:, j % 4, :], 0.125 if j < 8 else 1.0).then_inc(a.proj_act, 1)


def qkv_vector(dve, k, a):
    for j in range(1, QKV_JOBS, 2):
        dve.wait_ge(a.proj, j + 1)
        dve.tensor_scalar(qkv_out(k, j), k.ps[:, j % 4, :], 0.125 if j < 8 else 1.0, None, ALU.mult).then_inc(a.proj_dve, 1)


def out_proj_tensor(pe, k, a):
    for half in range(2):
        n = a.first_piece + 6 + half
        a.stream.wait(pe, n)
        for tt in range(TT):
            tokens(pe, k.ps[:, 4 * half + tt, :], k.oT, tt, a.stream.view(n)).then_inc(a.out, 1)


def out_proj_vector(dve, k, a, gate, tmp):
    dve.wait_ge(a.gate_ready, 1)
    for half in range(2):
        for tt in range(TT):
            j = 4 * half + tt
            dve.wait_ge(a.out, j + 1)
            cols = slice(half * 512, (half + 1) * 512)
            dve.tensor_tensor(tmp[:, j % 2, :], k.ps[:, j, :], gate[:, cols], ALU.mult).then_inc(a.gated, 1)
            dve.wait_ge(a.gated, j + 1)
            dve.tensor_tensor(k.x[:, tt, cols], k.x[:, tt, cols], tmp[:, j % 2, :], ALU.add).then_inc(a.x_ready, 1)



DIFF_UNITS = DIFF_HEADS * TT


def diff_tensor(pe, k, a):
    def scores(i):
        h, qt = divmod(i, TT)
        if i >= 2:
            pe.wait_ge(a.biased, 2 * i - 2)
        for m in range(2):
            r = slice(m * HEAD, (m + 1) * HEAD)
            mm = pe.matmul(k.ps[:, 2 * (i % 2) + m, 0:(qt + 1) * P], k.q[r, h, qt * P:(qt + 1) * P],
                           k.k[r, h, 0:(qt + 1) * P], start=True, stop=True)
        mm.then_inc(a.scored, 1)

    def turn(i):
        pe.wait_ge(a.weighed, i + 1)
        if i >= 2:
            pe.wait_ge(a.turned_out, i - 1)
        for kt in range(i % TT + 1):
            cols = slice(kt * P, (kt + 1) * P)
            mm = pe.transpose(k.ps[:, 4 + i % 2, cols], k.sm[:, i % 2, 0, cols], k.ident[:, :])
        mm.then_inc(a.turned, 1)

    def values(i):
        h, qt = divmod(i, TT)
        pe.wait_ge(a.turned_out, i + 1)
        if h >= 2 and qt == 0:
            pe.wait_ge(a.oT_out, h - 1)
        for kt in range(qt + 1):
            mm = pe.matmul(k.ps[:, 6 + h % 2, qt * P:(qt + 1) * P], k.aT[:, i % 2, kt * P:(kt + 1) * P],
                           k.v[:, kt, h * P:(h + 1) * P], start=(kt == 0), stop=(kt == qt))
        mm.then_inc(a.valued, 1)

    def turn_head(h):
        pe.wait_ge(a.head_normed, h + 1)
        for tt in range(TT):
            mm = pe.transpose(k.ps[:, 6 + h % 2, tt * P:(tt + 1) * P], k.hd[:, tt * P:(tt + 1) * P], k.ident[:, :])
        mm.then_inc(a.head_turned, 1)

    pe.wait_ge(a.proj_act, QKV_JOBS // 2)
    pe.wait_ge(a.proj_dve, QKV_JOBS // 2)
    for i in range(DIFF_UNITS + 4):
        if i < DIFF_UNITS:
            scores(i)
        if 1 <= i <= DIFF_UNITS:
            turn(i - 1)
        if 2 <= i <= DIFF_UNITS + 1:
            values(i - 2)
        if i >= 7 and (i - 7) % TT == 0:
            turn_head((i - 7) // TT)
    pe.wait_ge(a.oT_out, DIFF_HEADS)


def diff_scalar(act, k, a):
    for i in range(DIFF_UNITS + 5):
        if i < DIFF_UNITS:
            kw = (i % TT + 1) * P
            act.wait_ge(a.maxed, i + 1)
            for m in range(2):
                buf = k.sm[:, i % 2, m, 0:kw]
                act.activation(buf, buf, ACT.Exp, bias=k.nmax[:, i % 2, m:m + 1], scale=1.0,
                               accum_out=k.esum[:, i % 2, m:m + 1]).then_inc(a.exped, 1)
        if 1 <= i <= DIFF_UNITS:
            u = i - 1
            kw = (u % TT + 1) * P
            act.wait_ge(a.turned, u + 1)
            if u >= 2:
                act.wait_ge(a.valued, u - 1)
            act.copy(k.aT[:, u % 2, 0:kw], k.ps[:, 4 + u % 2, 0:kw]).then_inc(a.turned_out, 1)
        if i >= 6 and (i - 6) % TT == 0 and (i - 6) // TT < DIFF_HEADS:
            h = (i - 6) // TT
            act.wait_ge(a.valued, TT * h + TT)
            if h:
                act.wait_ge(a.head_turned, h)
            act.activation(k.hd[:, :], k.ps[:, 6 + h % 2, :], ACT.Square).then_inc(a.squared, 1)
            act.wait_ge(a.var, h + 1)
            act.activation(k.hsmall[:, 2, :], k.hsmall[:, 1, :], ACT.Sqrt).then_inc(a.rooted, 1)
        if i >= 8 and (i - 8) % TT == 0:
            h = (i - 8) // TT
            act.wait_ge(a.head_turned, h + 1)
            act.activation(k.oT[:, h, :], k.ps[:, 6 + h % 2, :], ACT.Copy, scale=k.subln[:, 0:1]).then_inc(a.oT_out, 1)


def diff_vector(dve, k, a, ch):
    slopes = head_slopes()

    def front(i):
        h, qt = divmod(i, TT)
        kw = (qt + 1) * P
        dve.wait_ge(a.scored, i + 1)
        if i >= 2:
            dve.wait_ge(a.turned, i - 1)
        for m in range(2):
            dve.scalar_tensor_tensor(out=k.sm[:, i % 2, m, 0:kw], in0=k.dist[:, (TT - 1 - qt) * P:TT * P],
                                     scalar=-slopes[h], in1=k.ps[:, 2 * (i % 2) + m, 0:kw],
                                     op0=ALU.mult, op1=ALU.add).then_inc(a.biased, 1)
        dve.wait_ge(a.biased, 2 * i + 2)
        ch.link(dve.tensor_reduce(k.nmax[:, i % 2, 2:4], k.sm[:, i % 2, :, 0:kw], AX_X, ALU.max))
        dve.tensor_scalar(k.nmax[:, i % 2, 0:2], k.nmax[:, i % 2, 2:4], -1.0, None, ALU.mult).then_inc(a.maxed, 1)

    def back(i):
        kw = (i % TT + 1) * P
        dve.wait_ge(a.exped, 2 * i + 2)
        r = k.esum[:, i % 2, 2:4]
        ch.link(dve.reciprocal(r, k.esum[:, i % 2, 0:2]))
        m = ch.mark(dve.tensor_scalar(k.esum[:, i % 2, 4:5], r[:, 1:2], k.lam_neg[:, 0:1], None, ALU.mult))
        p0, p1 = k.sm[:, i % 2, 0, 0:kw], k.sm[:, i % 2, 1, 0:kw]
        ch.link(dve.tensor_scalar(p0, p0, r[:, 0:1], None, ALU.mult))
        dve.scalar_tensor_tensor(out=p0, in0=p1, scalar=k.esum[:, i % 2, 4:5], in1=p0,
                                 op0=ALU.mult, op1=ALU.add).then_inc(a.weighed, 1)

    def head_norm(h):
        sm = k.hsmall
        dve.wait_ge(a.squared, h + 1)
        hd = k.hd[:, :].rearrange("p (t d) -> p t d", t=TT)
        ch.link(dve.tensor_reduce(sm[:, 0, :], hd, AX_X, ALU.add))
        dve.tensor_scalar(sm[:, 1, :], sm[:, 0, :], 1.0 / P, SUBLN_EPS, ALU.mult, ALU.add).then_inc(a.var, 1)
        dve.wait_ge(a.rooted, h + 1)
        ch.link(dve.reciprocal(sm[:, 3, :], sm[:, 2, :]))
        dve.tensor_tensor(hd, k.ps[:, 6 + h % 2, :].rearrange("p (t d) -> p t d", t=TT),
                          sm[:, 3, :].unsqueeze(2).to_broadcast([P, TT, P]), ALU.mult).then_inc(a.head_normed, 1)

    dve.wait_ge(k.s.dist_ready, 1)
    for i in range(DIFF_UNITS + 3):
        if i < DIFF_UNITS:
            front(i)
        if 1 <= i <= DIFF_UNITS:
            back(i - 1)
        if i >= 6 and (i - 6) % TT == 0:
            head_norm((i - 6) // TT)



SB_AT = (0, 512, 1024, 896)
SB_W = 1280


def sb_cols(kt, frm=None):
    frm = kt if frm is None else frm
    return slice(SB_AT[kt] + (frm - kt) * P, SB_AT[kt] + (TT - kt) * P)


def sb_tensor(pe, k, a):
    z, between = k.ps[:, 0:3, :].rearrange("p b n -> p (b n)"), k.ps[:, 3:6, :].rearrange("p b n -> p (b n)")

    def scores(h):
        if h:
            pe.wait_ge(a.log_sig, h)
        r = slice(h % 2 * HEAD, (h % 2 + 1) * HEAD)
        for kt in range(TT):
            mm = pe.matmul(z[:, sb_cols(kt)], k.k[r, h // 2, kt * P:(kt + 1) * P], k.q[r, h // 2, kt * P:T],
                           start=True, stop=True)
        mm.then_inc(a.scored, 1)

    def sums(h):
        pe.wait_ge(a.sp_masked, h + 1)
        if h:
            pe.wait_ge(a.arg, h)
        for kt in range(TT):
            for st in range(kt, TT):
                lhs = k.later[:, :] if st == kt else k.ones[:, :]
                mm = pe.matmul(between[:, sb_cols(kt, st)], lhs, k.sp[:, sb_cols(st)],
                               start=(st == kt), stop=(st == TT - 1))
        mm.then_inc(a.summed, 1)

    def values(h):
        pe.wait_ge(a.a_masked, h + 1)
        if h % 2 == 0 and h >= 4:
            pe.wait_ge(a.oT_out, h // 2 - 1)
        out = k.ps[h % 2 * HEAD:(h % 2 + 1) * HEAD, 6 + h // 2 % 2, :]
        for kt in range(TT):
            mm = pe.matmul(out[:, kt * P:T], k.v[:, kt, h * HEAD:(h + 1) * HEAD], k.tt[:, h % 2, sb_cols(kt)],
                           start=(kt == 0), stop=(kt == TT - 1))
        mm.then_inc(a.valued, 1)

    pe.wait_ge(a.proj_act, QKV_JOBS // 2)
    pe.wait_ge(a.proj_dve, QKV_JOBS // 2)
    for h in range(SB_HEADS + 2):
        if h < SB_HEADS:
            scores(h)
        if 1 <= h <= SB_HEADS:
            sums(h - 1)
        if h >= 2:
            values(h - 2)
    pe.wait_ge(a.oT_out, SB_HEADS // 2)


def sb_scalar(act, k, a):
    z = k.ps[:, 0:3, :].rearrange("p b n -> p (b n)")[:, 0:SB_W]
    for h in range(SB_HEADS + 2):
        if h < SB_HEADS:
            act.wait_ge(a.scored, h + 1)
            if h:
                act.wait_ge(a.softplus, h)
            act.activation(k.ln[:, :], z, ACT.Abs).then_inc(a.steps, 1)
            act.wait_ge(a.steps, 2 * h + 1)
            act.activation(k.ln[:, :], k.ln[:, :], ACT.Exp, scale=-1.0).then_inc(a.steps, 1)
            act.wait_ge(a.steps, 2 * h + 2)
            act.activation(k.ln[:, :], k.ln[:, :], ACT.Ln, bias=k.one_col, scale=1.0).then_inc(a.logged, 1)
        if 1 <= h <= SB_HEADS:
            act.wait_ge(a.arg, h)
            buf = k.tt[:, (h - 1) % 2, :]
            act.activation(buf, buf, ACT.Exp).then_inc(a.exped, 1)
        if h >= 3 and h % 2 == 1:
            pair = (h - 3) // 2
            act.wait_ge(a.valued, 2 * pair + 2)
            act.copy(k.oT[:, pair, :], k.ps[:, 6 + pair % 2, :]).then_inc(a.oT_out, 1)


def sb_vector(dve, k, a):
    z = k.ps[:, 0:3, :].rearrange("p b n -> p (b n)")[:, 0:SB_W]
    between = k.ps[:, 3:6, :].rearrange("p b n -> p (b n)")[:, 0:SB_W]
    for h in range(SB_HEADS + 1):
        if h:
            buf = k.tt[:, (h - 1) % 2, :]
            dve.wait_ge(a.summed, h)
            dve.tensor_tensor(buf, buf, between, ALU.subtract).then_inc(a.arg, 1)
        if h < SB_HEADS:
            dve.wait_ge(a.logged, h + 1)
            dve.scalar_tensor_tensor(out=k.sp[:, :], in0=z, scalar=0.0, in1=k.ln[:, :], op0=ALU.max, op1=ALU.add)\
                .then_inc(a.softplus, 1)
            dve.wait_ge(a.softplus, h + 1)
            if h >= 2:
                dve.wait_ge(a.valued, h - 1)
            dve.tensor_tensor(k.tt[:, h % 2, :], z, k.sp[:, :], ALU.subtract).then_inc(a.log_sig, 1)


def sb_gpsimd(pool, k, a):
    for h in range(SB_HEADS + 1):
        if h < SB_HEADS:
            pool.wait_ge(a.log_sig, h + 1)
            for kt in range(TT):
                diag = k.sp[:, SB_AT[kt]:SB_AT[kt] + P]
                ins = pool.tensor_tensor(diag, diag, k.before[:, :], ALU.mult)
            ins.then_inc(a.sp_masked, 1)
        if h:
            pool.wait_ge(a.exped, h)
            for kt in range(TT):
                diag = k.tt[:, (h - 1) % 2, SB_AT[kt]:SB_AT[kt] + P]
                ins = pool.tensor_tensor(diag, diag, k.before[:, :], ALU.mult)
            ins.then_inc(a.a_masked, 1)




def router_tensor(pe, k, m):
    hT_ready(pe, m.norm)
    pe.wait_ge(m.router_landed, 64)
    for tt in range(TT):
        for c in range(KD):
            mm = pe.matmul(k.ps[:, 0, tt * 36:(tt + 1) * 36], k.hT[:, c, tt * P:(tt + 1) * P], k.rw[:, c, :],
                           start=(c == 0), stop=(c == KD - 1))
    mm.then_inc(m.logits, 1)
    pe.wait_ge(m.chosen, 1)
    for tt in range(TT):
        for src in range(tt + 1):
            lhs = k.before if src == tt else k.ones
            pe.matmul(k.ps[:, 1, tt * E:(tt + 1) * E], lhs[:, :], k.sel[:, src, :], start=(src == 0), stop=(src == tt))
    for src in range(TT):
        mm = pe.matmul(k.ps[:, 2, 0:E], k.ones[:, :], k.sel[:, src, :], start=(src == 0), stop=(src == TT - 1))
    mm.then_inc(m.ranked, 1)


def router_vector(dve, k, m, ch):
    f = k.route

    def first_of(out, values, top, order, n, scratch):
        ch.link(dve.tensor_tensor(scratch, values, top.to_broadcast([P, TT, n]), ALU.is_equal))
        ch.link(dve.tensor_tensor(scratch, scratch, order.unsqueeze(1).to_broadcast([P, TT, n]), ALU.mult))
        ch.link(dve.tensor_reduce(f("top_order")[:, :, 0], scratch, AX_X, ALU.max))
        ch.link(dve.tensor_tensor(out, scratch, f("top_order").to_broadcast([P, TT, n]), ALU.is_equal))

    dve.wait_ge(m.logits, 1)
    lg = f("logits")
    ch.link(dve.tensor_tensor(lg, k.ps[:, 0, 0:TT * 36].rearrange("p (t n) -> p t n", t=TT),
                              k.rb[:, :].unsqueeze(1).to_broadcast([P, TT, 36]), ALU.add))
    g, e = lg[:, :, 0:GROUPS], lg[:, :, GROUPS:36]
    gm = f("g_max")
    ch.link(dve.tensor_reduce(gm[:, :, 0], g, AX_X, ALU.max))
    dve.tensor_tensor(f("g_exp"), g, gm.to_broadcast([P, TT, GROUPS]), ALU.subtract).then_inc(m.g_diff, 1)
    first_of(f("g_hot"), g, gm, k.iota[:, 0:GROUPS], GROUPS, f("g_tmp"))
    hot = f("g_hot")
    ch.link(dve.tensor_scalar(f("g_tmp"), hot, -1.0, 1e30, ALU.add, ALU.mult))
    em = f("e_mask")
    for tt in range(TT):
        shape = [P, GROUPS, PER_GROUP]
        ee = e[:, tt, :].rearrange("p (g e) -> p g e", g=GROUPS)
        out = em[:, tt, :].rearrange("p (g e) -> p g e", g=GROUPS)
        ch.link(dve.tensor_tensor(out, ee, hot[:, tt, :].unsqueeze(2).to_broadcast(shape), ALU.mult))
        ch.link(dve.tensor_tensor(out, out, f("g_tmp")[:, tt, :].unsqueeze(2).to_broadcast(shape), ALU.add))
    v1, v2 = f("v1"), f("v2")
    ch.link(dve.tensor_reduce(v1[:, :, 0], em, AX_X, ALU.max))
    first_of(f("hot1"), em, v1, k.iota[:, 4:36], E, f("e_tmp"))
    ch.link(dve.scalar_tensor_tensor(out=em, in0=f("hot1"), scalar=-1e38, in1=em, op0=ALU.mult, op1=ALU.add))
    ch.link(dve.tensor_reduce(v2[:, :, 0], em, AX_X, ALU.max))
    first_of(f("hot2"), em, v2, k.iota[:, 4:36], E, f("e_tmp"))
    dve.tensor_tensor(k.sel[:, :, :], f("hot1"), f("hot2"), ALU.add).then_inc(m.chosen, 1)
    dve.tensor_tensor(f("e2")[:, :, 0], v2[:, :, 0], v1[:, :, 0], ALU.subtract).then_inc(m.e_diff, 1)
    dve.wait_ge(m.exps, 2)
    ch.link(dve.tensor_reduce(f("g_sum")[:, :, 0], f("g_exp"), AX_X, ALU.add))
    ch.link(dve.tensor_scalar(f("w1"), f("e2"), 1.0, None, ALU.add))
    ch.link(dve.tensor_tensor(f("w1"), f("w1"), f("g_sum"), ALU.mult))
    ch.link(dve.reciprocal(f("w1"), f("w1")))
    ch.mark(dve.tensor_tensor(f("w2"), f("w1"), f("e2"), ALU.mult))
    dve.wait_ge(m.ranked, 1)
    ch.link(dve.tensor_copy(f("count"), k.ps[:, 2, 0:E]))
    ch.link(dve.tensor_tensor(f("cmp"), f("count").unsqueeze(2).to_broadcast([P, E, 8]),
                              k.iota[:, 36:44].unsqueeze(1).to_broadcast([P, E, 8]), ALU.is_gt))
    ch.link(dve.tensor_reduce(f("blocks"), f("cmp"), AX_X, ALU.add))
    ch.link(dve.tensor_tensor_scan(f("end"), k.ones[:, 0:E], f("blocks"), 0.0, ALU.mult, ALU.add))
    ch.link(dve.tensor_tensor(f("start"), f("end"), f("blocks"), ALU.subtract))
    ch.link(dve.tensor_scalar(f("start"), f("start"), float(BLOCK), None, ALU.mult))
    rank = f("e_mask")
    ch.link(dve.tensor_tensor(rank, k.ps[:, 1, 0:TT * E].rearrange("p (t e) -> p t e", t=TT),
                              f("start").unsqueeze(1).to_broadcast([P, TT, E]), ALU.add))
    for n, hot in enumerate(("hot1", "hot2")):
        ch.link(dve.tensor_tensor(f("e_tmp"), rank, f(hot), ALU.mult))
        ch.link(dve.tensor_reduce(f("slot_f"), f("e_tmp"), AX_X, ALU.add))
        ch.link(dve.tensor_copy(k.slot[:, n, :], f("slot_f")))
    ends = f("end")[0:1, :].unsqueeze(1).to_broadcast([1, MAX_BLOCKS, E])
    block = k.iota[0:1, 68:68 + MAX_BLOCKS].unsqueeze(2).to_broadcast([1, MAX_BLOCKS, E])
    ch.link(dve.tensor_tensor(k.big[0:1, :].rearrange("p (b e) -> p b e", e=E), ends, block, ALU.is_le))
    ch.link(dve.tensor_reduce(f("owner")[0:1, :], k.big[0:1, :].rearrange("p (b e) -> p b e", e=E), AX_X, ALU.add))
    ch.link(dve.tensor_scalar(f("owner")[0:1, :], f("owner")[0:1, :], float(E - 1), None, ALU.min))
    ch.link(dve.tensor_copy(k.meta[0:1, 1:1 + MAX_BLOCKS], f("owner")[0:1, :]))
    ch.link(dve.tensor_scalar(f("owner")[0:1, 0:PAIRS], k.iota[0:1, 44:44 + PAIRS], f("end")[0:1, E - 1:E], None, ALU.is_lt))
    ch.link(dve.tensor_reduce(f("slot_f")[0:1, 0:1], f("owner")[0:1, 0:PAIRS], AX_X, ALU.add))
    dve.tensor_copy(k.meta[0:1, 0:1], f("slot_f")[0:1, 0:1]).then_inc(m.routed, 1)


def router_scalar(act, k, m):
    act.wait_ge(m.g_diff, 1)
    act.activation(k.route("g_exp"), k.route("g_exp"), ACT.Exp).then_inc(m.exps, 1)
    act.wait_ge(m.e_diff, 1)
    act.activation(k.route("e2"), k.route("e2"), ACT.Exp).then_inc(m.exps, 1)


def pair_count(eng, k, m):
    eng.wait_ge(m.routed, 1)
    return eng.value_load(k.meta[0:1, 0:1], min_val=1, max_val=PAIRS)


def moe_sync(sp, k, m):
    n = pair_count(sp, k, m)
    sp.wait_ge(m.scattered, 16 * 2 * TT)
    with sp.Fori(0, n) as i:
        sp.wait_ge(m.x_turned, i + 1)
        sp.dma_start(k.xg[:, :], k.x_slots[bass.ds(i * P, P), :]).then_inc(m.x_landed, 16)
        first = sp.value_load(k.meta[0:1, bass.ds(i * 2 + 1, 1)], min_val=0, max_val=E - 1)
        second = sp.value_load(k.meta[0:1, bass.ds(i * 2 + 2, 1)], min_val=0, max_val=E - 1)
        for kind, (w, landed, used) in enumerate(((m.w_gate, m.gate_landed, m.gated), (m.w_up, m.up_landed, m.upped),
                                                  (m.w_down, m.down_landed, m.downed))):
            sp.wait_ge(used, i + 1)
            for b, expert in enumerate((first, second)):
                src = w[bass.ds(expert, 1), :, :].rearrange("a (p k) n -> p (a k n)", p=P)
                sp.dma_start(k.ring[:, 2 * kind + b, :], src).then_inc(landed, 16)
    sp.wait_ge(m.downed, n + 1)


def moe_tensor(pe, k, m):
    n = pair_count(pe, k, m)
    for opened in (m.x_turned, m.gated, m.upped, m.downed, m.h_turned):
        pe.sem_inc(opened, 1)
    halves = (slice(0, BLOCK), slice(BLOCK, P))
    with pe.Fori(0, n) as i:
        pe.wait_ge(m.x_landed, i * 16 + 16)
        for c in range(KD):
            mm = pe.transpose(k.ps[:, c // 4, c % 4 * P:(c % 4 + 1) * P], k.xg[:, c::KD], k.ident[:, :])
        mm.then_inc(m.x_turned, 1)
        pe.wait_ge(m.xT_act, i + 1)
        pe.wait_ge(m.xT_dve, i + 1)
        pe.wait_ge(m.hidden, i + 1)
        for kind, (landed, done) in enumerate(((m.gate_landed, m.gated), (m.up_landed, m.upped))):
            pe.wait_ge(landed, i * 32 + 32)
            for c in range(KD):
                for b, slots in enumerate(halves):
                    w = k.ring[:, 2 * kind + b, :].rearrange("p (k n) -> p k n", k=KD)
                    mm = pe.matmul(k.ps[slots, 2 + kind, :], k.xT[:, c, slots], w[:, c, :],
                                   start=(c == 0), stop=(c == KD - 1))
            mm.then_inc(done, 1)
        pe.wait_ge(m.hidden, i + 2)
        for c in range(KH):
            mm = pe.transpose(k.ps[:, 4, c * P:(c + 1) * P], k.hid[:, c::KH], k.ident[:, :])
        mm.then_inc(m.h_turned, 1)
        pe.wait_ge(m.hT_out, i + 1)
        pe.wait_ge(m.down_landed, i * 32 + 32)
        pe.wait_ge(m.y_act, i + 1)
        pe.wait_ge(m.y_dve, i + 1)
        for half in range(2):
            for c in range(KH):
                for b, slots in enumerate(halves):
                    w = k.ring[:, 4 + b, :].rearrange("p (k n) -> p k n", k=KH)
                    mm = pe.matmul(k.ps[slots, 5 + half, :], k.hTt[:, c, slots], w[:, c, half * 512:(half + 1) * 512],
                                   start=(c == 0), stop=(c == KH - 1))
        mm.then_inc(m.downed, 1)


def moe_scalar(act, k, m):
    n = pair_count(act, k, m)
    act.sem_inc(m.y_act, 1)
    act.sem_inc(m.y_stored, 1)
    with act.Fori(0, n) as i:
        act.wait_ge(m.x_turned, i + 2)
        act.wait_ge(m.upped, i + 1)
        for c in range(KD // 2):
            ins = act.activation(k.xT[:, c, :], k.ps[:, 0, c * P:(c + 1) * P], ACT.Identity,
                                 bias=m.norm.shift(c), scale=m.norm.gain(c))
        ins.then_inc(m.xT_act, 1)
        act.wait_ge(m.gated, i + 2)
        act.wait_ge(m.hidden, i + 1)
        act.activation(k.sg[:, :], k.ps[:, 2, :], ACT.Silu).then_inc(m.silu, 1)
        act.wait_ge(m.h_turned, i + 2)
        act.copy(k.hTt[:, :, :].rearrange("p c s -> p (c s)"), k.ps[:, 4, :]).then_inc(m.hT_out, 1)
        act.wait_ge(m.downed, i + 2)
        act.wait_ge(m.y_stored, i * 16 + 1)
        act.copy(k.ys[:, 0:512], k.ps[:, 5, :]).then_inc(m.y_act, 1)
        act.wait_ge(m.y_act, i + 2)
        act.wait_ge(m.y_dve, i + 2)
        act.dma_start(k.y_slots[bass.ds(i * P, P), :], k.ys[:, :]).then_inc(m.y_stored, 16)


def moe_vector(dve, k, m):
    n = pair_count(dve, k, m)
    dve.sem_inc(m.y_dve, 1)
    dve.sem_inc(m.hidden, 1)
    with dve.Fori(0, n) as i:
        dve.wait_ge(m.x_turned, i + 2)
        dve.wait_ge(m.upped, i + 1)
        for c in range(KD // 2, KD):
            ins = dve.tensor_scalar(k.xT[:, c, :], k.ps[:, 1, (c - 4) * P:(c - 3) * P], m.norm.gain(c), m.norm.shift(c),
                                    ALU.mult, ALU.add)
        ins.then_inc(m.xT_dve, 1)
        dve.wait_ge(m.upped, i + 2)
        dve.wait_ge(m.silu, i + 1)
        dve.wait_ge(m.h_turned, i + 1)
        dve.tensor_tensor(k.hid[:, :], k.ps[:, 3, :], k.sg[:, :], ALU.mult).then_inc(m.hidden, 1)
        dve.wait_ge(m.downed, i + 2)
        dve.wait_ge(m.y_stored, i * 16 + 1)
        dve.tensor_copy(k.ys[:, 512:1024], k.ps[:, 6, :]).then_inc(m.y_dve, 1)
    dve.wait_ge(m.y_stored, n * 16 + 1)
    dve.memset(k.all_stored[:, :], 0.0).then_inc(m.all_stored, 1)


def moe_gpsimd(pool, k, m):
    pool.wait_ge(m.routed, 1)
    m.norm.after(pool, "xn_act", 2)
    m.norm.after(pool, "xn_dve", 2)
    for tt in range(TT):
        for c in range(2):
            pool.indirect_dma_start(k.x_slots, bass.IndirectOffsetOnAxis(ap=k.slot[:, c, tt:tt + 1], axis=0),
                                    k.xn[:, tt, :], None).then_inc(m.scattered, 16)
    pool.wait_ge(m.all_stored, 1)
    pool.wait_ge(m.scattered, 16 * 2 * TT)
    for tt in range(TT):
        for c in range(2):
            pool.indirect_dma_start(k.yg[:, 2 * tt + c, :], None, k.y_slots,
                                    bass.IndirectOffsetOnAxis(ap=k.slot[:, c, tt:tt + 1], axis=0)).then_inc(m.gathered[tt], 16)


def combine_vector(dve, k, m, ch):
    dve.wait_ge(m.gate_ready, 1)
    for tt in range(TT):
        dve.wait_ge(m.gathered[tt], 32)
        y1, y2 = k.yg[:, 2 * tt, :], k.yg[:, 2 * tt + 1, :]
        ch.link(dve.tensor_scalar(y1, y1, k.route("w1")[:, tt, :], None, ALU.mult))
        ch.link(dve.scalar_tensor_tensor(out=y1, in0=y2, scalar=k.route("w2")[:, tt, :], in1=y1, op0=ALU.mult, op1=ALU.add))
        ch.link(dve.tensor_tensor(y1, y1, k.gate_m[:, :], ALU.mult))
        dve.tensor_tensor(k.x[:, tt, :], k.x[:, tt, :], y1, ALU.add).then_inc(m.x_ready, 1)




PARAM_ROWS = [("ffn_w", FFN_TAPS * FT), ("ffn_b", FT), ("rg_w", B_TAPS * B_TILES), ("rg_b", B_TILES), ("rg_b_a", B_TILES),
              ("rg_b_x", B_TILES), ("rg_lambda", B_TILES), ("lower", A_TILES), ("gla_b", 1), ("subln", 1)]
PARAM_AT = {name: sum(n for _, n in PARAM_ROWS[:i]) for i, (name, _) in enumerate(PARAM_ROWS)}
PARAMS = sum(n for _, n in PARAM_ROWS)

ROUTE = [("logits", 36), ("g_max", 1), ("g_exp", 4), ("g_hot", 4), ("g_tmp", 4), ("top_order", 1), ("e_mask", 32),
         ("e_tmp", 32), ("v1", 1), ("v2", 1), ("hot1", 32), ("hot2", 32), ("e2", 1), ("g_sum", 1), ("w1", 1), ("w2", 1)]


def make_constants(pool, k, ch):
    s = k.s
    pool.memset(k.ones[:, :], 1.0)
    ch.link(pool.memset(k.ident[:, :], 0.0))
    pool.affine_select(out=k.ident[:, :], in_=k.ident[:, :], compare_op=ALU.not_equal, fill=1.0, base=0,
                       pattern=[[-1, P]], channel_multiplier=1).then_inc(s.ident_ready, 1)
    pool.wait_ge(s.ident_ready, 1)
    pool.affine_select(out=k.before[:, :], in_=k.ones[:, :], compare_op=ALU.is_gt, fill=0.0, base=0,
                       pattern=[[1, P]], channel_multiplier=-1)
    pool.memset(k.xb[:, :, 0:B_TAPS - 1], 0.0).then_inc(s.pads_ready, 1)
    ch.link(pool.memset(k.mask_f[:, :, :], 0.0))
    for i, half in enumerate(LEVELS):
        m = k.mask_f[:, i, :].rearrange("p (s h l) -> p s h l", h=2, l=half)[:, :, 1, :]
        n = P // (2 * half)
        ch.link(pool.memset(m, 1.0))
        ch.link(pool.affine_select(out=m, in_=m, compare_op=ALU.is_ge, fill=0.0, base=0,
                                   pattern=[[-2 * half, n], [0, half]], channel_multiplier=1))
        ch.link(pool.affine_select(out=m, in_=m, compare_op=ALU.is_ge, fill=0.0, base=half - 1,
                                   pattern=[[2 * half, n], [0, half]], channel_multiplier=-1))
    ch.link(pool.tensor_copy(k.mask_f[:, N_LEVELS - 1, :], k.ident[:, :]))
    pool.tensor_copy(k.masks[:, :, :], k.mask_f[:, :, :]).then_inc(s.masks_ready, 1)
    it = k.iota_i
    for c0, cn, step, base in ((0, GROUPS, -1, GROUPS), (4, E, -1, E), (36, 8, BLOCK, 0), (44, PAIRS, 2, 0), (68, MAX_BLOCKS, 1, 0)):
        ins = pool.iota(it[:, c0:c0 + cn], pattern=[[step, cn]], base=base, channel_multiplier=0)
    ch.link(ins)
    pool.tensor_copy(k.iota[:, :], it[:, :]).then_inc(s.iota_ready, 1)
    pool.wait_ge(s.iota_ready, 1)
    pool.memset(k.S[:, :, :], 0.0).then_inc(s.S_clear, 1)


def parameters_vector(dve, k):
    s = k.s
    dve.wait_ge(s.ident_ready, 1)
    dve.tensor_reduce(k.four[:, :], k.ident[:, 0:P:32], AX_X, ALU.add).then_inc(s.four_ready, 1)
    dve.wait_ge(s.rows_turned, 1)
    dve.tensor_copy(k.cols[:, :], k.ps[:, 0, 0:PARAMS]).then_inc(s.cols_ready, 1)
    dve.wait_ge(s.lam_landed, 64)
    dve.tensor_tensor(k.lprod[:, :], k.lvec[:, 0:4:2], k.lvec[:, 1:4:2], ALU.mult).then_inc(s.lam_prod, 1)
    dve.wait_ge(s.lam_exp, 1)
    dve.tensor_tensor(k.lam_neg[:, :], k.lexp[:, 1:2], k.lexp[:, 0:1], ALU.subtract).then_inc(s.lam_diff, 1)
    dve.wait_ge(s.lam_diff, 1)
    dve.tensor_scalar(k.lam_neg[:, :], k.lam_neg[:, :], -LAMBDA_INIT, None, ALU.add)
    dve.wait_ge(s.cols_ready, 1)
    dve.tensor_scalar(k.subln[:, :], k.col("subln", 0), 1.0 - LAMBDA_INIT, None, ALU.mult).then_inc(s.lam_ready, 1)


def parameters_tensor(pe, k):
    s = k.s
    pe.wait_ge(s.ident_ready, 1)
    pe.wait_ge(s.rows_landed, 16 * len(PARAM_ROWS))
    pe.transpose(k.ps[:, 0, 0:PARAMS], k.rows[0:PARAMS, :], k.ident[0:PARAMS, 0:PARAMS]).then_inc(s.rows_turned, 1)
    pe.wait_ge(s.lam_prod, 1)
    pe.matmul(k.ps[:, 1, 0:2], k.ones[0:HEAD, :], k.lprod[:, :], start=True, stop=True).then_inc(s.lam_sum, 1)
    pe.wait_ge(s.cols_ready, 1)
    pe.wait_ge(s.lam_exp, 1)


def modulation_gpsimd(pool, k):
    s = k.s
    pool.wait_ge(s.row_out, 16 * ADA_PIECES)
    for l in range(2):
        for i, v in enumerate((0, 1, 3, 4)):
            pool.dma_start(k.mod[:, l, i, :], k.mod_rows[l, v, :].rearrange("(p k) -> p k", p=P)).then_inc(s.mod_landed, 16)
            pool.dma_start(k.modb[:, l, i, :], k.ada_b[l, v * D:(v + 1) * D].rearrange("(p k) -> p k", p=P)).then_inc(s.mod_landed, 16)
    pool.wait_ge(s.mod_landed, 16 * 16)
    pool.tensor_tensor(k.mod[:, :, :, :], k.mod[:, :, :, :], k.modb[:, :, :, :], ALU.add).then_inc(s.mod_steps, 1)
    pool.wait_ge(s.mod_steps, 1)
    for l in range(2):
        for i in (1, 3):
            pool.tensor_scalar(k.mod[:, l, i, :], k.mod[:, l, i, :], 1.0, None, ALU.add).then_inc(s.mod_steps, 1)
    pool.wait_ge(s.mod_steps, 5)
    pool.wait_ge(s.gains_landed, 16 * 6)
    for l in range(2):
        for i, g in ((1, 2 + 2 * l), (3, 3 + 2 * l)):
            ins = pool.tensor_tensor(k.mod[:, l, i, :], k.mod[:, l, i, :], k.gains[:, g, :], ALU.mult)
    ins.then_inc(s.mod_ready, 1)


def distances_gpsimd(pool, k):
    steps = k.s.dist_steps
    pool.iota(k.dist_i, pattern=[[1, T]], base=-(T - P), channel_multiplier=-1).then_inc(steps, 1)
    pool.wait_ge(steps, 1)
    pool.tensor_copy(k.dist, k.dist_i).then_inc(steps, 1)
    pool.wait_ge(steps, 2)
    pool.tensor_scalar(k.sm[:, 0, 0, :], k.dist, -2.0, 0.0, ALU.mult, ALU.max).then_inc(steps, 1)
    pool.wait_ge(steps, 3)
    pool.tensor_tensor(k.dist, k.dist, k.sm[:, 0, 0, :], ALU.add).then_inc(steps, 1)
    pool.wait_ge(steps, 4)
    pool.memset(k.dist[0:CHUNK, T - CHUNK:T], F_SLOPE_MASK).then_inc(steps, 1)
    pool.wait_ge(steps, 5)


def gate_rows(pool, k, l, v, out, tmp, landed, ready):
    pool.dma_start(out, k.mod_rows[l, v:v + 1, :].to_broadcast([P, D])).then_inc(landed, 16)
    pool.dma_start(tmp, k.ada_b[l:l + 1, v * D:(v + 1) * D].to_broadcast([P, D])).then_inc(landed, 16)
    pool.wait_ge(landed, 32)
    pool.tensor_tensor(out, out, tmp, ALU.add).then_inc(ready, 1)



ARENA = 18124
F_SLOPE_MASK = 1e32


def place(k, nc, ctx):

    def sb(name, shape, dt=F32):
        return ctx.enter_context(nc.sbuf_tensor(name, shape, dt))

    k.ring = sb("ring", [P, RING, SLOT_F])
    xbuf = sb("x", [P, TT * D])
    k.x = xbuf[:, :].rearrange("p (t d) -> p t d", t=TT)
    k.hT = sb("hT", [P, KD, T])
    k.oT = k.hT
    arena = sb("arena", [P, ARENA])
    k.ps = ctx.enter_context(nc.psum_tensor("ps", [P, 8, 512], F32))

    def at(off, *shape, base=arena):
        n = 1
        for d in shape:
            n *= d
        flat = base[:, off:off + n]
        if len(shape) == 2:
            return flat.rearrange("p (a b) -> p a b", b=shape[1])
        if len(shape) == 3:
            return flat.rearrange("p (a b c) -> p a b c", b=shape[1], c=shape[2])
        return flat

    k.ident, k.ones, k.before = sb("ident", [P, P]), sb("ones", [P, P]), sb("before", [P, P])
    k.masks = sb("masks", [P, N_LEVELS, P], U8)
    k.cols = sb("cols", [P, PARAMS])
    k.col = lambda name, i: k.cols[:, PARAM_AT[name] + i:PARAM_AT[name] + i + 1]
    k.cols_of = lambda name: k.cols[:, PARAM_AT[name]:PARAM_AT[name] + dict(PARAM_ROWS)[name]]
    k.gains = sb("gains", [P, 6, KD])
    k.mod, k.modb = sb("mod", [P, 2, 4, KD]), at(16500, 8, KD).rearrange("p (l v) k -> p l v k", l=2)
    k.iota = sb("iota", [P, 68 + MAX_BLOCKS])
    k.one_col = k.ones[:, 0:1]
    k.subln, k.lam_neg, k.lvec, k.lprod, k.lexp = (sb("subln", [P, 1]), sb("lam_neg", [P, 1]), sb("lvec", [HEAD, 4]),
                                                   sb("lprod", [HEAD, 2]), sb("lexp", [P, 2]))
    k.ss, k.vr, k.rt, k.rstd = (sb(n, [P, TT]) for n in ("ss", "vr", "rt", "rstd"))
    k.all_stored = sb("all_stored", [1, 1])
    k.slot = sb("slot", [P, 2, TT], I32)
    k.meta = sb("meta", [1, 2 + MAX_BLOCKS], I32)
    k.xn = at(0, TT, D)

    k.cvec, k.cond, k.four = sb("cvec", [P, KD]), sb("cond", [P, KD, 32]), sb("four", [P, 1])
    k.gate_up, k.normw = sb("gate_up", [RANK, P]), sb("normw", [P, 512])
    k.sp_e, k.sp_x, k.sp_y, k.sp_z, k.sp8, k.sp8n = (sb(n, [P, B_TILES]) for n in ("sp_e", "sp_x", "sp_y", "sp_z", "sp8", "sp8n"))
    k.lb_e, k.lb_r, k.lb, k.lb1 = (sb(n, [P, A_TILES]) for n in ("lb_e", "lb_r", "lb", "lb1"))
    k.eL = sb("eL", [P, TT])
    k.hss, k.hvar, k.hrt, k.hrs = (sb(n, [P, 2, 16]) for n in ("hss", "hvar", "hrt", "hrs"))
    k.arg, k.qk = at(0, 2, T, base=xbuf), at(1024, 2, T, base=xbuf)
    k.kd, k.q0, k.kdT = at(2048, T, base=xbuf), at(2560, 2, T, base=xbuf), at(3584, 3, P, base=xbuf)
    k.f2 = k.qk
    k.qA, k.S_late, k.keyA, k.lfA, k.VA = at(0, 2, T), at(0, 2, T), at(1024, 2, T), at(2048, 2, T), at(3072, TT, 512)
    k.bd = at(1024, 8, P).rearrange("p (g t) c -> p g t c", g=2)
    k.ga = at(3072, B_TILES, T)
    k.qC, k.kC, k.lfC, k.VC = at(5120, T), at(5632, T), at(6144, T), at(6656, TT, 512)
    k.xb, k.xc, k.gg = at(8704, B_TILES, T + B_TAPS - 1), at(10764, B_TILES, T), at(12812, B_TILES, T)
    k.S = at(14860, 2, T)
    k.onorm, k.th, k.part = at(15884, TT, 256), at(15884, 2, T), at(16908, T)
    k.f2c = k.th[:, 0, :]
    k.lr = k.part[0:RANK, :]
    k.row = at(17420, 512)[0:1, :]
    k.st = lambda t, c: at(3584 + c * P, P, base=xbuf) if t < 2 else at((3584, 3840, 2048)[c], 2 * P, base=xbuf)
    k.rows, k.mask_f = at(17420, P), at(12812, N_LEVELS, P)
    k.iota_i = at(14860, 68 + MAX_BLOCKS).bitcast(I32)
    k.scores = lambda t, h: k.S[:, h % 2, :] if t < 2 or h < 2 else k.S_late[:, h - 2, :]
    k.tiles = [Tile(k, t) for t in range(3)]

    k.actT, k.gpad, k.conv, k.gelu = at(0, FT, T), at(10752, 2, T + FFN_TAPS - 1), at(11780, 2, T), at(12804, 4, T)
    k.gain_1, k.zero = at(14852, D), at(15876, 512)

    k.q, k.k, k.v = at(0, KD, T), at(4096, KD, T), at(8192, TT, D)
    k.dist, k.sm, k.aT, k.hd = at(12288, T), at(12800, 2, 2, T), at(14848, 2, T), at(15872, T)
    k.dist_i = at(12800, T).bitcast(I32)
    k.nmax, k.esum, k.hsmall = at(17408, 2, 4), at(17416, 2, 5), at(17426, 4, TT)
    k.gate_diff, k.gate_diff_b, k.tmp_diff = at(16384, D), at(12800, D), at(12800, 2, 512)
    k.ln, k.sp, k.tt, k.later = at(12288, SB_W), at(13568, SB_W), at(14848, 2, SB_W), at(17408, P)
    k.gate_sb, k.gate_sb_b, k.tmp_sb = at(12288, D), at(13568, D), at(14848, 2, 512)

    k.big = at(4096, MAX_BLOCKS * E)
    k.xg, k.xT, k.sg, k.hid, k.hTt, k.ys = (at(8192, D), at(9216, KD, P), at(10240, HID), at(10752, HID), at(11264, KH, P),
                                            at(11776, D))
    route_at, off = {}, 12800
    for name, n in ROUTE:
        route_at[name] = at(off, TT, n)
        off += TT * n
    for name, n in (("count", E), ("blocks", E), ("end", E), ("start", E), ("owner", MAX_BLOCKS), ("slot_f", TT)):
        route_at[name] = at(off, n)
        off += n
    route_at["cmp"] = at(off, E, 8)
    off += E * 8
    k.sel = at(off, TT, E)
    off += TT * E
    k.route = lambda name: route_at[name]
    k.rw = at(off, KD, 36)
    off += KD * 36
    k.rb = at(off, 36)
    off += 36
    k.gate_m, k.gate_m_b = at(off, D), at(off + D, D)
    off += 2 * D
    assert off + D <= ARENA, off
    k.gain_2 = at(off, D)
    k.yg = at(0, 2 * TT, D)


def semaphores(nc, prefix, names):
    return [nc.alloc_semaphore(name=prefix + n) for n in names.split()]


@contextmanager
def part(nc):
    before = nc.snapshot_sems()
    yield
    nc.all_engine_barrier()
    nc.clear_and_free_semaphores(nc.allocated_since(before))
    nc.all_engine_barrier()


def norm_group(nc, k, where, n, rows):
    norm, row = ({name: nc.alloc_semaphore(name=where + prefix + name) for name in counts}
                 for prefix, counts in (("norm_", NORM_COUNTS), ("row_norm_", ROW_NORM_COUNTS)))
    return [Norm(k, norm, NORM_COUNTS, i) for i in range(n)], [Norm(k, row, ROW_NORM_COUNTS, i) for i in range(rows)]


def piece(st, src, c0, n, at=0, width=512, chunks=KD):
    view = st.view(len(st.pieces), chunks, width)
    return view[:, :, at:at + n], src[:, :, c0:c0 + n]


def plan_first_block(k, w):
    s, st = "first", k.stream1
    k.w = st.view
    w_in = rows_strided(w["w_in"][0])
    for n, used in enumerate((4, 8, 12, 16)):
        st.add([piece(st, w_in, 512 * n, 512)], s, "main_done", used)
    st.add([piece(st, w_in, 2048, 256, 0, 272), piece(st, w_in, 2816, RANK, 256, 272)], s, "main_done", 19)
    st.add([piece(st, w_in, 2304, 512)], s, "main_done", 23)
    k.ada_piece = len(st.pieces)
    for a in range(ADA_PIECES):
        l, c = divmod(a, ADA_PIECES // 2)
        st.add([piece(st, rows_strided(w["ada_w"][l]), c * 512, 512)], s, "main_done", ADA_JOB + 2 * a + 1)
    k.w_out_piece = len(st.pieces)
    for half in range(2):
        st.add([piece(st, rows_tiled(w["w_out"][0]), half * 512, 512)], s, "w_out_done", TT * (half + 1))
    k.ffn_piece = len(st.pieces)
    for c in range(FFN_PIECES):
        tiles = gate_tiles(c)
        n = len(tiles) * P
        for name, used in (("ffn_w_gate", "ffn_gate"), ("ffn_w_val", "ffn_val")):
            st.add([piece(st, rows_strided(w[name][0]), c * 512, n, 0, n)], s, used, tiles[-1] + 1)
    k.down_piece = len(st.pieces)
    down = rows_tiled(w["ffn_w_down"][0])
    for half in range(2):
        for r, (c0, n) in enumerate(DOWN_CHUNKS):
            used = ("down_done", TT * (half + 1)) if r == len(DOWN_CHUNKS) - 1 else ("down_piece_used", 2 * half + r + 1)
            st.add([piece(st, down[:, c0:c0 + n, :], half * 512, 512, chunks=n)], s, *used)


def plan_attention(st, a, w_in, w_out):
    for n in range(6):
        st.add([piece(st, rows_strided(w_in), n * 512, 512)], a, "proj", 4 * (n + 1))
    for half in range(2):
        st.add([piece(st, rows_tiled(w_out), half * 512, 512)], a, "out", TT * (half + 1))


def first_block(nc, k, w):
    s = k.s = Kit()
    (s.S_clear, s.four_ready, s.ident_ready, s.pads_ready, s.masks_ready, s.iota_ready, s.pool_chain, s.dve_chain,
     s.rows_landed, s.rows_turned, s.cols_ready, s.lam_landed, s.lam_prod, s.lam_sum, s.lam_exp, s.lam_diff,
     s.lam_ready, s.gains_landed, s.cond_landed, s.small_landed, s.x_landed, s.main_done, s.main_emptied,
     s.unit_done, s.unit_emptied, s.out_done, s.out_turned, s.par_act, s.par_pool, s.sp_recip, s.lb_arg,
     s.cond_ready, s.f_ready, s.ln_ready, s.cum_ready, s.arg_ready, s.exp_ready, s.prep_ready, s.A_normed,
     s.A_emptied, s.C_normed, s.C_emptied, s.gw_ready, s.bd_clear, s.bd_landed, s.conv_ready, s.gelu_ready, s.B_tanh,
     s.B_a, s.B_square, s.B_sqrt, s.B_sqrt_used, s.B_scan, s.oT_pool, s.row_out, s.w_out_done, s.x_again, s.x1_ready,
     s.ffn_pads, s.ffn_gate, s.ffn_gate_out, s.ffn_val, s.ffn_val_out, s.ffn_conv, s.ffn_gelu, s.down_piece_used,
     s.down_done, s.x2_ready, s.zero_ready, s.slots_clear, s.mod_landed, s.mod_steps, s.mod_ready, s.gain_landed) = semaphores(
        nc, "", """S_clear four_ready ident_ready pads_ready masks_ready iota_ready pool_chain dve_chain rows_landed
        rows_turned cols_ready lam_landed lam_prod lam_sum lam_exp lam_diff lam_ready gains_landed
        cond_landed small_landed x_landed main_done main_emptied unit_done unit_emptied out_done out_turned
        par_act par_pool sp_recip lb_arg cond_ready f_ready ln_ready cum_ready arg_ready exp_ready
        prep_ready A_normed A_emptied C_normed C_emptied gw_ready bd_clear bd_landed conv_ready gelu_ready
        B_tanh B_a B_square B_sqrt B_sqrt_used B_scan oT_pool row_out w_out_done x_again x1_ready ffn_pads
        ffn_gate ffn_gate_out ffn_val ffn_val_out ffn_conv ffn_gelu down_piece_used down_done x2_ready
        zero_ready slots_clear mod_landed mod_steps mod_ready gain_landed""")
    k.used["first"] = {"main_done": s.main_done, "w_out_done": s.w_out_done, "ffn_gate": s.ffn_gate, "ffn_val": s.ffn_val,
                       "down_piece_used": s.down_piece_used, "down_done": s.down_done}
    s.osq, s.ovar, s.oroot = ([nc.alloc_semaphore(name=f"{n}{i}") for i in range(2)] for n in ("osq", "ovar", "oroot"))
    k.norms, (last,) = norm_group(nc, k, "first_", 2, 1)
    for i, n in enumerate(k.norms):
        n.gain, n.shift = (lambda c, i=i: k.gains[:, i, c:c + 1]), (lambda c: 0.0)

    def x_landed(eng):
        eng.wait_ge(s.x_landed, 16)

    def x1(eng):
        eng.wait_ge(s.x1_ready, 8)

    def x2(eng):
        eng.wait_ge(s.x2_ready, 8)

    def gains(eng):
        eng.wait_ge(s.gains_landed, 16 * 6)

    with nc.Block() as block:
        @block.sync
        def _(sp):
            sp.dma_start(k.x, w["x"][0].rearrange("(t p) d -> p t d", p=P)).then_inc(s.x_landed, 16)
            for n in range(k.diff_piece + RING):
                k.stream1.load(sp, n)

        @block.gpsimd
        def _(pool):
            first_block_gpsimd(pool, k)
            pool.wait_ge(s.prep_ready, 3 * PREPS)
            pool.wait_ge(s.out_done, 4)
            pool.dma_start(k.x, w["x"][0].rearrange("(t p) d -> p t d", p=P)).then_inc(s.x_again, 16)
            pool.wait_ge(s.ffn_pads, 1)
            pool.memset(k.zero, 0.0).then_inc(s.zero_ready, 1)
            pool.dma_start(k.gain_1, w["norm_final"].rearrange("(a d) -> a d", a=1).to_broadcast([P, D])).then_inc(s.gain_landed, 16)
            pool.wait_ge(s.zero_ready, 1)
            for slots in (k.x_slots, k.y_slots):
                dst = slots.rearrange("(p r) (h n) -> p (r h) n", p=P, h=2)
                pool.dma_start(dst, k.zero.unsqueeze(1).to_broadcast([P, 2 * SLOTS // P, 512])).then_inc(s.slots_clear, 16)
            modulation_gpsimd(pool, k)
            pool.wait_ge(s.slots_clear, 32)

        @block.scalar
        def _(act):
            act.dma_start(k.cvec[:, :], w["c"][0].rearrange("(p k) -> p k", p=P)).then_inc(s.cond_landed, 16)
            for name, n in PARAM_ROWS:
                r = k.rows[PARAM_AT[name]:PARAM_AT[name] + n, :]
                act.dma_start(r, w["row_" + name]).then_inc(s.rows_landed, 16)
            for i, name in enumerate(("norm_mix", "norm_ffn")):
                act.dma_start(k.gains[:, i, :], w[name][0].rearrange("(p k) -> p k", p=P)).then_inc(s.gains_landed, 16)
            for l in range(2):
                for i, name in enumerate(("norm1_g", "norm2_g")):
                    act.dma_start(k.gains[:, 2 + 2 * l + i, :], w[name][l].rearrange("(p k) -> p k", p=P)).then_inc(s.gains_landed, 16)
            for i, name in enumerate(("q1", "k1", "q2", "k2")):
                act.dma_start(k.lvec[:, i:i + 1], w["lambda_" + name][0].rearrange("(d a) -> d a", a=1)).then_inc(s.lam_landed, 16)
            act.dma_start(k.gate_up[:, :], w["gla_w_gate_up"][0]).then_inc(s.small_landed, 16)
            act.dma_start(k.normw[:, 0:256], w["hgrn_norm"].to_broadcast([P, 256])).then_inc(s.small_landed, 16)
            act.dma_start(k.normw[:, 256:512], w["gla_norm"].to_broadcast([P, 256])).then_inc(s.small_landed, 16)
            act.wait_ge(s.lam_sum, 1)
            act.activation(k.lexp[:, :], k.ps[:, 1, 0:2], ACT.Exp).then_inc(s.lam_exp, 1)
            gains(act)
            norm_scalar(act, k, k.norms[0], x_landed)
            first_block_scalar(act, k)
            norm_scalar(act, k, k.norms[1], x1)
            ffn_scalar(act, k)
            row_norm_scalar(act, k, last, x2)

        @block.tensor
        def _(pe):
            parameters_tensor(pe, k)
            norm_tensor(pe, k, k.norms[0])
            first_block_tensor(pe, k)
            norm_tensor(pe, k, k.norms[1])
            ffn_tensor(pe, k)

        @block.vector
        def _(dve):
            ch = Chain(dve, s.dve_chain)
            parameters_vector(dve, k)
            norm_vector(dve, k, k.norms[0], x_landed, gains)
            first_block_vector(dve, k, ch)
            norm_vector(dve, k, k.norms[1], x1, gains)
            ffn_vector(dve, k, ch)
            dve.wait_ge(s.gain_landed, 16)
            row_norm_vector(dve, k, last, x2, k.gain_1, k.x)


def second_block_layer(nc, k, w, out, l):
    s, a, m = Kit(), Kit(), Kit()
    k.s, a.stream, a.first_piece = s, (k.stream1, k.stream2)[l], (k.diff_piece, 0)[l]
    (s.dve_chain, s.dist_steps, s.dist_ready, s.later_ready, s.gain_landed, s.stored) = semaphores(
        nc, f"layer{l}_", """dve_chain dist_steps dist_ready later_ready gain_landed stored""")
    (a.proj, a.proj_act, a.proj_dve, a.out, a.gated, a.x_ready, a.gate_landed, a.gate_ready, a.scored, a.valued,
     a.exped, a.oT_out) = semaphores(
        nc, f"attention{l}_", """proj proj_act proj_dve out gated x_ready gate_landed gate_ready scored valued exped oT_out""")
    if l == 0:
        (a.biased, a.maxed, a.weighed, a.turned, a.turned_out, a.squared, a.var, a.rooted, a.head_normed, a.head_turned) = semaphores(
            nc, "diff_", """biased maxed weighed turned turned_out squared var rooted head_normed head_turned""")
    else:
        (a.steps, a.logged, a.softplus, a.log_sig, a.sp_masked, a.summed, a.arg, a.a_masked) = semaphores(
            nc, "sb_", """steps logged softplus log_sig sp_masked summed arg a_masked""")
    k.used[("diff", "sb")[l]] = {"proj": a.proj, "out": a.out}
    (m.router_landed, m.logits, m.g_diff, m.e_diff, m.exps, m.chosen, m.ranked, m.routed, m.scattered, m.x_landed,
     m.x_turned, m.xT_act, m.xT_dve, m.gate_landed, m.up_landed, m.down_landed, m.gated, m.upped, m.downed, m.hidden,
     m.silu, m.h_turned, m.hT_out, m.y_act, m.y_dve, m.y_stored, m.all_stored, m.gate_rows, m.gate_ready, m.x_ready) = semaphores(
        nc, f"moe{l}_", """router_landed logits g_diff e_diff exps chosen ranked routed scattered x_landed x_turned xT_act
        xT_dve gate_landed up_landed down_landed gated upped downed hidden silu h_turned hT_out y_act y_dve
        y_stored all_stored gate_rows gate_ready x_ready""")
    m.gathered = [nc.alloc_semaphore(name=f"moe{l}_gathered{t}") for t in range(TT)]
    m.w_gate, m.w_up, m.w_down = (w[n][l] for n in ("expert_w_gate", "expert_w_up", "expert_w_down"))
    (norm1, m.norm), (last,) = norm_group(nc, k, f"layer{l}_", 2, 1)
    a.norm = norm1
    for v, n in enumerate((norm1, m.norm)):
        n.gain = lambda c, v=v: k.mod[:, l, 2 * v + 1, c:c + 1]
        n.shift = lambda c, v=v: k.mod[:, l, 2 * v, c:c + 1]
    gate, gate_b, tmp = (k.gate_diff, k.gate_diff_b, k.tmp_diff) if l == 0 else (k.gate_sb, k.gate_sb_b, k.tmp_sb)

    def from_before(eng):
        pass

    def after_attention(eng):
        eng.wait_ge(a.x_ready, 8)

    def after_moe(eng):
        eng.wait_ge(m.x_ready, TT)

    with nc.Block() as block:
        @block.sync
        def _(sp):
            for n in range(a.first_piece + RING, a.first_piece + 8):
                a.stream.load(sp, n)
            sp.wait_ge(a.out, 8)
            moe_sync(sp, k, m)
            if l == 0:
                for n in range(RING):
                    k.stream2.load(sp, n)
            else:
                last.after(sp, "normed", TT)
                sp.dma_start(out[0].rearrange("(t p) d -> p t d", p=P), k.x).then_inc(s.stored, 16)
                sp.wait_ge(s.stored, 16)

        @block.gpsimd
        def _(pool):
            if l == 0:
                distances_gpsimd(pool, k)
                a.norm.after(pool, "turned", KD)
                gate_rows(pool, k, l, 2, gate, gate_b, a.gate_landed, a.gate_ready)
                pool.wait_ge(a.gate_ready, 1)
                pool.memset(k.sm[:, 0, 0, 0:1], 0.0).then_inc(s.dist_ready, 1)
            else:
                pool.affine_select(out=k.later, in_=k.ones[:, :], compare_op=ALU.is_gt, fill=0.0, base=0,
                                   pattern=[[-1, P]], channel_multiplier=1).then_inc(s.later_ready, 1)
                sb_gpsimd(pool, k, a)
                pool.wait_ge(a.softplus, SB_HEADS)
                pool.wait_ge(a.summed, SB_HEADS)
                gate_rows(pool, k, l, 2, gate, gate_b, a.gate_landed, a.gate_ready)
            pool.wait_ge(m.routed, 1)
            gate_rows(pool, k, l, 5, k.gate_m, k.gate_m_b, m.gate_rows, m.gate_ready)
            if l == 1:
                gain = w["final_norm_g"].rearrange("(a d) -> a d", a=1).to_broadcast([P, D])
                pool.wait_ge(m.gate_ready, 1)
                pool.dma_start(k.gain_2, gain).then_inc(s.gain_landed, 16)
            moe_gpsimd(pool, k, m)

        @block.scalar
        def _(act):
            norm_scalar(act, k, norm1, from_before)
            qkv_scalar(act, k, a)
            (diff_scalar, sb_scalar)[l](act, k, a)
            after_attention(act)
            act.dma_start(k.rw[:, :, 0:GROUPS], rows_strided(w["router_group_w"][l])).then_inc(m.router_landed, 16)
            act.dma_start(k.rw[:, :, GROUPS:36], rows_strided(w["router_expert_w"][l])).then_inc(m.router_landed, 16)
            act.dma_start(k.rb[:, 0:GROUPS], w["router_group_b"][l:l + 1].to_broadcast([P, GROUPS])).then_inc(m.router_landed, 16)
            act.dma_start(k.rb[:, GROUPS:36], w["router_expert_b"][l:l + 1].rearrange("a g e -> a (g e)").to_broadcast([P, E]))                .then_inc(m.router_landed, 16)
            norm_scalar(act, k, m.norm, after_attention)
            router_scalar(act, k, m)
            moe_scalar(act, k, m)
            if l == 1:
                row_norm_scalar(act, k, last, after_moe)

        @block.tensor
        def _(pe):
            norm_tensor(pe, k, norm1)
            qkv_tensor(pe, k, a)
            if l == 1:
                pe.wait_ge(s.later_ready, 1)
            (diff_tensor, sb_tensor)[l](pe, k, a)
            out_proj_tensor(pe, k, a)
            norm_tensor(pe, k, m.norm)
            router_tensor(pe, k, m)
            moe_tensor(pe, k, m)

        @block.vector
        def _(dve):
            ch = Chain(dve, s.dve_chain)
            norm_vector(dve, k, norm1, from_before, from_before)
            qkv_vector(dve, k, a)
            if l == 0:
                diff_vector(dve, k, a, ch)
            else:
                sb_vector(dve, k, a)
            out_proj_vector(dve, k, a, gate, tmp)
            norm_vector(dve, k, m.norm, after_attention, from_before)
            router_vector(dve, k, m, ch)
            moe_vector(dve, k, m)
            combine_vector(dve, k, m, ch)
            if l == 1:
                dve.wait_ge(s.gain_landed, 16)
                row_norm_vector(dve, k, last, after_moe, k.gain_2, k.x)


def two_block_kernel(nc, w, out):
    with ExitStack() as ctx:
        k = Kit()
        place(k, nc, ctx)
        k.mod_dram = nc.dram_tensor("modulation", [ADA_PIECES, 512], F32).ap()
        k.mod_rows = k.mod_dram.rearrange("(l v h) n -> l v (h n)", l=2, v=6)
        k.x_slots = nc.dram_tensor("token_slots", [SLOTS, D], F32).ap()
        k.y_slots = nc.dram_tensor("output_slots", [SLOTS, D], F32).ap()
        k.ada_b, k.rg_w_a, k.rg_w_x = w["ada_b"], w["rg_w_a"], w["rg_w_x"]
        k.used = {}
        k.stream1, k.stream2 = (Stream(k, [ctx.enter_context(nc.semaphore(f"ring{i}_{n}")) for n in range(RING)]) for i in range(2))
        plan_first_block(k, w)
        k.diff_piece = len(k.stream1.pieces)
        plan_attention(k.stream1, "diff", w["diff_w_in"][0], w["diff_w_out"][0])
        plan_attention(k.stream2, "sb", w["sb_w_in"][0], w["sb_w_out"][0])
        with part(nc):
            first_block(nc, k, w)
        for l in range(2):
            with part(nc):
                second_block_layer(nc, k, w, out, l)


_INS = {
    "x": ("x", None), "norm_mix": ("norm_mix", None), "w_in": ("w_in", None), "hgrn_norm": ("hgrn_norm", None),
    "rg_w_a": ("rg_w_a", None), "rg_w_x": ("rg_w_x", None), "gla_w_gate_up": ("gla_w_gate_up", None),
    "gla_norm": ("gla_norm", None), "w_out": ("w_out", None), "norm_ffn": ("norm_ffn", None),
    "ffn_w_gate": ("ffn_w_gate", None), "ffn_w_val": ("ffn_w_val", None), "ffn_w_down": ("ffn_w_down", None),
    "norm_final": ("norm_final", None),
    "row_ffn_w": ("ffn_conv_w", (-1, P)), "row_ffn_b": ("ffn_conv_b", (-1, P)), "row_rg_w": ("rg_conv_w", (-1, P)),
    "row_rg_b": ("rg_conv_b", (-1, P)), "row_rg_b_a": ("rg_b_a", (-1, P)), "row_rg_b_x": ("rg_b_x", (-1, P)),
    "row_rg_lambda": ("rg_lambda", (-1, P)), "row_lower": ("hgrn_lower_bounds", (-1, P)),
    "row_gla_b": ("gla_b_gate", (-1, P)), "row_subln": ("diff_subln_g_2", (-1, P)),
    "c": ("c_2", None), "norm1_g": ("norm1_g_2", None), "norm2_g": ("norm2_g_2", None), "ada_w": ("ada_w_2", None),
    "ada_b": ("ada_b_2", None), "diff_w_in": ("diff_w_in_2", None), "diff_w_out": ("diff_w_out_2", None),
    "lambda_q1": ("diff_lambda_q1_2", None), "lambda_k1": ("diff_lambda_k1_2", None),
    "lambda_q2": ("diff_lambda_q2_2", None), "lambda_k2": ("diff_lambda_k2_2", None),
    "sb_w_in": ("sb_w_in_2", None), "sb_w_out": ("sb_w_out_2", None), "router_group_w": ("router_group_w_2", None),
    "router_group_b": ("router_group_b_2", None), "router_expert_w": ("router_expert_w_2", None),
    "router_expert_b": ("router_expert_b_2", None), "expert_w_gate": ("expert_w_gate_2", None),
    "expert_w_up": ("expert_w_up_2", None), "expert_w_down": ("expert_w_down_2", None),
    "final_norm_g": ("final_norm_g_2", None),
}


def kernel(**inputs):
    import numpy as _np
    import concourse.bacc as _bacc
    from concourse.bass_utils import run_bass_kernel_spmd as _run

    nc = _bacc.Bacc("TRN2", target_bir_lowering=False, num_devices=1)
    arrays, w = {}, {}
    for name, (source, shape) in _INS.items():
        a = _np.ascontiguousarray(inputs[source])
        if shape:
            a = a.reshape(shape)
        arrays[f"in_{name}"] = a
        w[name] = nc.dram_tensor(f"in_{name}", a.shape, mybir.dt.from_np(a.dtype), kind="ExternalInput").ap()
    out = nc.dram_tensor("out", (1, T, D), F32, kind="ExternalOutput").ap()
    two_block_kernel(nc, w, out)
    r = _run(nc, [arrays], core_ids=[0])
    return r.results[0]["out"]
```

```python
from contextlib import ExitStack, contextmanager

import concourse.bass as bass
from concourse import mybir

ALU = mybir.AluOpType
ACT = mybir.ActivationFunctionType
AX_X = mybir.AxisListType.X
F32 = mybir.dt.float32
I32 = mybir.dt.int32
U8 = mybir.dt.uint8

P = 128
T = 512
TT = T // P
D = 1024
KD = D // P
EPS = 1e-6
SUBLN_EPS = 1e-5

HEAD = 64
A_W, B_W, C_W = 256, 512, 256
A_TILES, B_TILES = A_W // P, B_W // P
C_DK = 32
B_TAPS, FFN_TAPS = 4, 3
RANK = 16
D_FF = 2688
FT = D_FF // P
F_FLOOR = 1e-20
LRU_C = 8.0
GATE_NORM = 16.0
LEVELS = (64, 32, 16, 8, 4, 2, 1)

DIFF_HEADS, SB_HEADS = 8, 16
CHUNK = 64
LAMBDA_INIT = 0.8 - 0.6
GROUPS, PER_GROUP = 4, 8
E = GROUPS * PER_GROUP
HID = 512
KH = HID // P
BLOCK = 64
EXTRA = 2 * T // BLOCK
MAX_BLOCKS = E + EXTRA
PAIRS = MAX_BLOCKS // 2
SLOTS = MAX_BLOCKS * BLOCK

RING = 6
SLOT_F = KD * 512


def head_slopes():
    return [2.0 ** (-8.0 * (h + 1) / DIFF_HEADS) for h in range(DIFF_HEADS)]


class Kit:
    pass


class Chain:

    def __init__(self, eng, sem):
        self.eng, self.sem, self.n = eng, sem, 0

    def mark(self, ins):
        self.n += 1
        ins.then_inc(self.sem, 1)
        return self.n

    def after(self, n):
        self.eng.wait_ge(self.sem, n)

    def link(self, ins):
        self.after(self.mark(ins))




def rows_strided(w):
    return w.rearrange("(p k) n -> p k n", p=P)


def rows_tiled(w):
    return w.rearrange("(k p) n -> p k n", p=P)


class Piece:

    def __init__(self, loads, group, used, used_at):
        self.loads, self.group, self.used, self.used_at = loads, group, used, used_at


class Stream:

    def __init__(self, kit, landed):
        self.kit, self.landed, self.pieces, self.count, self.at = kit, landed, [], [0] * RING, []

    def add(self, loads, group, used, used_at):
        slot = len(self.pieces) % RING
        self.count[slot] += 16 * len(loads)
        self.at.append(self.count[slot])
        self.pieces.append(Piece(loads, group, used, used_at))
        return len(self.pieces) - 1

    def view(self, n, chunks=KD, cols=512):
        flat = self.kit.ring[:, n % RING, 0:chunks * cols]
        return flat.rearrange("p (k n) -> p k n", k=chunks)

    def wait(self, eng, n):
        eng.wait_ge(self.landed[n % RING], self.at[n])

    def load(self, sp, n):
        if n >= RING:
            before = self.pieces[n - RING]
            sp.wait_ge(self.kit.used[before.group][before.used], before.used_at)
        for dst, src in self.pieces[n].loads:
            sp.dma_start(dst, src).then_inc(self.landed[n % RING], 16)




class Norm:

    def __init__(self, k, sems, counts, i):
        self.sems, self.counts, self.i = sems, counts, i
        self.ss, self.vr, self.rt, self.rstd = k.ss, k.vr, k.rt, k.rstd

    def after(self, eng, name, n):
        eng.wait_ge(self.sems[name], self.i * self.counts[name] + n)


NORM_COUNTS = {"sq_act": 2, "sq_dve": 2, "var": 1, "root": 1, "rstd_set": 1, "xn_act": 2, "xn_dve": 2, "turned": KD,
               "hT_act": KD // 2, "hT_dve": KD // 2}
ROW_NORM_COUNTS = {"sq_act": TT, "var": 1, "root": 1, "rstd_set": 1, "normed": TT}


def norm_scalar(act, k, s, x_ready):
    x_ready(act)
    for tt in (0, 1):
        act.activation(k.xn[:, tt, :], k.x[:, tt, :], ACT.Square, accum_out=s.ss[:, tt:tt + 1]).then_inc(s.sems["sq_act"], 1)
    s.after(act, "var", 1)
    act.activation(s.rt[:, :], s.vr[:, :], ACT.Sqrt).then_inc(s.sems["root"], 1)
    s.after(act, "rstd_set", 1)
    s.after(act, "sq_act", 2)
    for tt in (1, 3):
        act.activation(k.xn[:, tt, :], k.x[:, tt, :], ACT.Copy, scale=s.rstd[:, tt:tt + 1]).then_inc(s.sems["xn_act"], 1)
    for c in range(1, KD, 2):
        s.after(act, "turned", c + 1)
        act.activation(k.hT[:, c, :], k.ps[:, c, :], ACT.Identity, bias=s.shift(c), scale=s.gain(c)).then_inc(s.sems["hT_act"], 1)


def norm_vector(dve, k, s, x_ready, gains_ready):
    x_ready(dve)
    for tt in (2, 3):
        dve.tensor_tensor_reduce(k.xn[:, tt, :], k.x[:, tt, :], k.x[:, tt, :], 1.0, 0.0, ALU.mult, ALU.add,
                                 s.ss[:, tt:tt + 1]).then_inc(s.sems["sq_dve"], 1)
    s.after(dve, "sq_dve", 2)
    s.after(dve, "sq_act", 2)
    dve.tensor_scalar(s.vr[:, :], s.ss[:, :], 1.0 / D, EPS, ALU.mult, ALU.add).then_inc(s.sems["var"], 1)
    s.after(dve, "root", 1)
    dve.reciprocal(s.rstd[:, :], s.rt[:, :]).then_inc(s.sems["rstd_set"], 1)
    s.after(dve, "rstd_set", 1)
    for tt in (0, 2):
        dve.tensor_scalar(k.xn[:, tt, :], k.x[:, tt, :], s.rstd[:, tt:tt + 1], None, ALU.mult).then_inc(s.sems["xn_dve"], 1)
    gains_ready(dve)
    for c in range(0, KD, 2):
        s.after(dve, "turned", c + 1)
        dve.tensor_scalar(k.hT[:, c, :], k.ps[:, c, :], s.gain(c), s.shift(c), ALU.mult, ALU.add).then_inc(s.sems["hT_dve"], 1)


def norm_tensor(pe, k, s):
    for tt in range(TT):
        s.after(pe, "xn_act" if tt % 2 else "xn_dve", tt // 2 + 1)
        for c in range(KD):
            mm = pe.transpose(k.ps[:, c, tt * P:(tt + 1) * P], k.xn[:, tt, c::KD], k.ident[:, :])
            if tt == TT - 1:
                mm.then_inc(s.sems["turned"], 1)


def hT_ready(eng, s):
    s.after(eng, "hT_act", KD // 2)
    s.after(eng, "hT_dve", KD // 2)


def row_norm_scalar(act, k, s, x_ready):
    x_ready(act)
    for tt in range(TT):
        act.activation(k.xn[:, tt, :], k.x[:, tt, :], ACT.Square, accum_out=s.ss[:, tt:tt + 1]).then_inc(s.sems["sq_act"], 1)
    s.after(act, "var", 1)
    act.activation(s.rt[:, :], s.vr[:, :], ACT.Sqrt).then_inc(s.sems["root"], 1)


def row_norm_vector(dve, k, s, x_ready, gain, out):
    x_ready(dve)
    s.after(dve, "sq_act", TT)
    dve.tensor_scalar(s.vr[:, :], s.ss[:, :], 1.0 / D, EPS, ALU.mult, ALU.add).then_inc(s.sems["var"], 1)
    s.after(dve, "root", 1)
    dve.reciprocal(s.rstd[:, :], s.rt[:, :]).then_inc(s.sems["rstd_set"], 1)
    s.after(dve, "rstd_set", 1)
    for tt in range(TT):
        dve.scalar_tensor_tensor(out=out[:, tt, :], in0=k.x[:, tt, :], scalar=s.rstd[:, tt:tt + 1], in1=gain,
                                 op0=ALU.mult, op1=ALU.mult).then_inc(s.sems["normed"], 1)




def features(pe, out, w, cols, x, chunks=KD):
    for c in range(chunks):
        mm = pe.matmul(out, w[:, c, cols], x[:, c, :], start=(c == 0), stop=(c == chunks - 1))
    return mm


def tokens(pe, out, x, tt, w, chunks=KD):
    for c in range(chunks):
        mm = pe.matmul(out, x[:, c, tt * P:(tt + 1) * P], w[:, c, :], start=(c == 0), stop=(c == chunks - 1))
    return mm



GATE_JOB, B_GATE_JOB, ADA_JOB = 23, 24, 32
ADA_PIECES = 24
JOBS_1 = ADA_JOB + 2 * ADA_PIECES
EARLY_JOB = 11
EARLY_ADA = GATE_JOB - EARLY_JOB
LATE_JOB = ADA_JOB + 2 * EARLY_ADA


def job_order():
    order = list(range(EARLY_JOB))
    for n in range(EARLY_ADA):
        order += [EARLY_JOB + n, ADA_JOB + 2 * n, ADA_JOB + 2 * n + 1]
    return order + list(range(GATE_JOB, ADA_JOB)) + list(range(LATE_JOB, JOBS_1))


JOB_POSITION = {j: n for n, j in enumerate(job_order())}


def job_count(j):
    return JOB_POSITION[j] + 1


PREPS = 2 + len(LEVELS)
N_LEVELS = len(LEVELS) + 1


def unit_of(t, kind, i=0, pair=0):
    base = 10 * t
    if kind == "turn":
        return base
    if kind == "state":
        return base + 1
    return base + 2 + (i if t < 2 else 2 * i + pair)


UNITS = unit_of(2, "level", N_LEVELS - 1, 1) + 1
A_UNITS = unit_of(2, "turn")


def tile_units(t):
    pairs = (0,) if t < 2 else (0, 1)
    out = [("turn", 0, 0), ("state", 0, 0)]
    out += [("level", i, pair) for i in range(N_LEVELS) for pair in pairs]
    return out + [("out", 0, pair) for pair in pairs]


class Tile:

    def __init__(self, k, t):
        self.t = t
        self.dk = HEAD if t < 2 else C_DK
        self.heads = P // self.dk
        self.q = k.qA[:, t, :] if t < 2 else k.qC
        self.key = k.keyA[:, t, :] if t < 2 else k.kC
        self.cum = k.lfA[:, t, :] if t < 2 else k.lfC
        self.v = k.VA if t < 2 else k.VC
        self.v0 = t * P if t < 2 else 0
        self.width = self.heads * HEAD

    def rows(self, h):
        return slice(h * self.dk, (h + 1) * self.dk)


def main_bank(k, j):
    return k.ps[:, JOB_POSITION[j] % 2, :]


def unit_banks(k, u):
    b = 4 + 2 * (u % 2)
    return k.ps[:, b, :], k.ps[:, b + 1, :]


def first_block_tensor(pe, k):
    s = k.s

    def free(j):
        if job_count(j) > 2:
            pe.wait_ge(s.main_emptied, job_count(j) - 2)

    def w_in_job(j):
        free(j)
        bank = main_bank(k, j)
        n = k.w_in_piece[j]
        if j < 4:
            if j == 0:
                k.stream1.wait(pe, n)
            mm = features(pe, bank, k.w(n), slice(j * P, (j + 1) * P), k.hT)
        elif j < 8:
            if j == 4:
                k.stream1.wait(pe, n)
            mm = tokens(pe, bank, k.hT, j - 4, k.w(n))
        elif j < 16:
            if j % 4 == 0:
                k.stream1.wait(pe, n)
            mm = features(pe, bank, k.w(n), slice(j % 4 * P, (j % 4 + 1) * P), k.hT)
        elif j < 19:
            if j == 16:
                k.stream1.wait(pe, n)
            w = k.stream1.view(n, cols=2 * P + RANK)
            if j < 18:
                mm = features(pe, bank, w, slice((j - 16) * P, (j - 15) * P), k.hT)
            else:
                mm = features(pe, bank[0:RANK, :], w, slice(2 * P, 2 * P + RANK), k.hT)
        else:
            if j == 19:
                k.stream1.wait(pe, n)
            mm = tokens(pe, bank, k.hT, j - 19, k.w(n))
        mm.then_inc(s.main_done, 1)

    def unit(t, kind, i, pair):
        tile = k.tiles[t]
        if kind == "out":
            return out_pair(tile, pair)
        u = unit_of(t, kind, i, pair)
        if u >= 2:
            pe.wait_ge(s.unit_emptied, u - 1)
        a, b = unit_banks(k, u)
        if kind == "turn":
            pe.wait_ge(s.prep_ready, PREPS * t + 1)
            for c in range(TT - 1):
                mm = pe.transpose(a[:, c * P:(c + 1) * P], k.kd[:, c * P:(c + 1) * P], k.ident[:, :])
        elif kind == "state":
            pe.wait_ge(s.unit_emptied, u)
            pe.wait_ge(s.main_emptied, job_count(7 if t < 2 else GATE_JOB - 1))
            for c in range(TT - 1):
                out = a[:, c * P:(c + 1) * P] if t < 2 else (a, b)[c // 2][:, c % 2 * 256:c % 2 * 256 + 256]
                mm = pe.matmul(out, k.kdT[:, c, :], tile.v[:, c, tile.v0:tile.v0 + tile.width], start=True, stop=True)
        else:
            if i < len(LEVELS):
                pe.wait_ge(s.prep_ready, PREPS * t + 3 + i)
                left = right = k.qk[:, i % 2, :]
            else:
                left, right = tile.key, tile.q
            for n, out in enumerate((a, b)):
                rows = tile.rows(2 * pair + n)
                for c in range(TT):
                    tok = slice(c * P, (c + 1) * P)
                    mm = pe.matmul(out[:, tok], left[rows, tok], right[rows, tok], start=True, stop=True)
        mm.then_inc(s.unit_done, 1)

    def out_pair(tile, pair):
        t = tile.t
        u = unit_of(t, "level", N_LEVELS - 1, pair)
        pe.wait_ge(s.unit_emptied, u + 1)
        pe.wait_ge(s.main_emptied, job_count(7 if t < 2 else GATE_JOB - 1))
        if t == 2 and pair == 0:
            pe.wait_ge(s.A_normed, 1)
            pe.wait_ge(s.A_emptied, 2)
        for c in range(TT):
            head = 2 * t if t < 2 else 2 * pair
            col = c % 2 * 256 + head * HEAD
            out = k.ps[:, 2 + c // 2, col:col + P]
            if c:
                pe.matmul(out, k.q0[:, t % 2, c * P:(c + 1) * P], k.st(t, c - 1)[:, pair * P:(pair + 1) * P],
                          start=True, stop=False, skip_group_check=True)
            for n in range(2):
                v = tile.v[:, c, (head + n) * HEAD:(head + n + 1) * HEAD]
                mm = pe.matmul(out[:, n * HEAD:(n + 1) * HEAD], k.scores(t, 2 * pair + n)[:, c * P:(c + 1) * P], v,
                               start=(c == 0), stop=True, skip_group_check=True)
        mm.then_inc(s.out_done, 1)

    def turn_outputs(ready):
        pe.wait_ge(ready, 1)
        for f in range(2):
            for tt in range(TT):
                mm = pe.transpose(k.ps[:, 2 + f, tt * P:(tt + 1) * P], k.onorm[:, tt, f * P:(f + 1) * P], k.ident[:, :])
            mm.then_inc(s.out_turned, 1)

    def modulate(j):
        a, last = divmod(j - ADA_JOB, 2)
        free(j)
        if last:
            pe.wait_ge(s.main_emptied, job_count(j - 1))
            pe.matmul(main_bank(k, j)[0:1, :], k.four[:, :], k.part[:, :], start=True, stop=True).then_inc(s.main_done, 1)
            return
        n = k.ada_piece[a]
        k.stream1.wait(pe, n)
        for c in range(KD):
            g = c % 4
            mm = pe.matmul(main_bank(k, j)[32 * g:32 * g + 32, :], k.cond[:, c, :], k.w(n)[:, c, :],
                           start=(c < 4), stop=(c >= 4), skip_group_check=True)
        mm.then_inc(s.main_done, 1)

    hT_ready(pe, k.norms[0])
    for j in range(EARLY_JOB):
        w_in_job(j)
    pe.wait_ge(s.cond_ready, 1)
    pe.wait_ge(s.four_ready, 1)
    todo = [(t, *u) for t in (0, 1) for u in tile_units(t)]
    for j in range(EARLY_JOB, GATE_JOB):
        w_in_job(j)
        for u in todo[:2]:
            unit(*u)
        todo = todo[2:]
        modulate(ADA_JOB + 2 * (j - EARLY_JOB))
        modulate(ADA_JOB + 2 * (j - EARLY_JOB) + 1)
    for u in todo:
        unit(*u)
    free(GATE_JOB)
    pe.wait_ge(s.main_emptied, job_count(18))
    pe.wait_ge(s.small_landed, 48)
    pe.matmul(main_bank(k, GATE_JOB), k.gate_up[:, :], k.lr[:, :], start=True, stop=True).then_inc(s.main_done, 1)
    turn_outputs(s.A_normed)
    pe.wait_ge(s.bd_landed, 16 * 4)
    for t in range(B_TILES):
        for g in range(2):
            j = B_GATE_JOB + 2 * t + g
            free(j)
            pe.wait_ge(s.conv_ready, t + 1)
            pe.matmul(main_bank(k, j), k.bd[:, g, t, :], k.xc[:, t, :], start=True, stop=True).then_inc(s.main_done, 1)
    todo = [(2, *u) for u in tile_units(2)]
    for a in range(EARLY_ADA, ADA_PIECES):
        for j in (ADA_JOB + 2 * a, ADA_JOB + 2 * a + 1):
            modulate(j)
            if todo:
                unit(*todo.pop(0))
    for u in todo:
        unit(*u)
    pe.wait_ge(s.A_emptied, 2)
    pe.wait_ge(s.oT_pool, B_TILES)
    pe.wait_ge(s.unit_emptied, UNITS)
    first, second = k.w_out_piece, k.w_out_piece + 1
    k.stream1.wait(pe, first)

    def project(n, bank, tt, chunks):
        for c in chunks:
            mm = pe.matmul(k.ps[:, bank, :], k.oT[:, c, tt * P:(tt + 1) * P], k.w(n)[:, c, :],
                           start=(c == 0), stop=(c == KD - 1), skip_group_check=True)
        return mm

    for tt in range(TT):
        project(first, 4 + tt, tt, range(KD - C_W // P))
    turn_outputs(s.C_normed)
    pe.wait_ge(s.C_emptied, 2)
    for tt in range(TT):
        project(first, 4 + tt, tt, range(KD - C_W // P, KD)).then_inc(s.w_out_done, 1)
    pe.wait_ge(s.main_emptied, JOBS_1)
    k.stream1.wait(pe, second)
    for tt in range(TT):
        project(second, tt, tt, range(KD)).then_inc(s.w_out_done, 1)


def first_block_scalar(act, k):
    s = k.s
    items = [("kd", 0), ("q0", 0)] + [("level", i) for i in range(len(LEVELS))]

    def empty(j):
        act.wait_ge(s.main_done, job_count(j))
        bank = main_bank(k, j)
        if j < 2:
            ins = act.copy(k.qA[:, j, :], bank)
        elif j < 4:
            act.activation(k.lfA[:, j - 2, :], bank, ACT.Sigmoid)
            ins = act.activation(k.keyA[:, j - 2, :], bank, ACT.Sigmoid, scale=-1.0)
        elif j < 8:
            act.copy(k.VA[:, j - 4, 0:256], bank[:, 0:256])
            ins = act.activation(k.VA[:, j - 4, 256:512], bank[:, 256:512], ACT.Silu)
        elif j < 12:
            ins = act.copy(k.xb[:, j - 8, B_TAPS - 1:], bank)
        elif j < 16:
            if j == 12:
                act.wait_ge(s.masks_ready, 1)
            ins = act.copy(k.gg[:, j - 12, :], bank)
        elif j == 16:
            ins = act.mul(k.qC, bank, C_DK ** -0.5)
        elif j == 17:
            ins = act.copy(k.kC, bank)
        elif j == 18:
            ins = act.copy(k.lr[:, :], bank[0:RANK, :])
        elif j < GATE_JOB:
            act.copy(k.VC[:, j - 19, 0:256], bank[:, 0:256])
            ins = act.activation(k.VC[:, j - 19, 256:512], bank[:, 256:512], ACT.Silu)
        elif j == GATE_JOB:
            ins = act.activation(k.lfC, bank, ACT.Identity, bias=k.col("gla_b", 0), scale=1.0)
        elif j < ADA_JOB:
            t, g = divmod(j - B_GATE_JOB, 2)
            if g == 0:
                if t == 0:
                    act.wait_ge(s.A_normed, 1)
                ins = act.activation(k.ga[:, t, :], bank, ACT.Sigmoid, bias=k.col("rg_b_a", t), scale=1.0)
            else:
                ins = act.activation(k.xb[:, t, B_TAPS - 1:], bank, ACT.Sigmoid, bias=k.col("rg_b_x", t), scale=1.0)
        else:
            a, kind = divmod(j - ADA_JOB, 2)
            if kind == 0:
                ins = act.copy(k.part[:, :], bank)
            else:
                if a:
                    act.wait_ge(s.row_out, 16 * a)
                act.copy(k.row[:, :], bank[0:1, :]).then_inc(s.main_emptied, 1)
                act.wait_ge(s.main_emptied, job_count(j))
                act.dma_start(k.mod_dram[a:a + 1, :], k.row[:, :]).then_inc(s.row_out, 16)
                return
        ins.then_inc(s.main_emptied, 1)

    def prep(t, kind, i):
        tile = k.tiles[t]
        if kind == "q0":
            act.wait_ge(s.cum_ready, t + 1)
            if t == 2:
                act.wait_ge(s.out_done, 1)
            act.activation(k.q0[:, t % 2, :], tile.cum, ACT.Exp).then_inc(s.exp_ready, 1)
            return
        n = (PREPS - 1) * t + (0 if kind == "kd" else 1 + i)
        act.wait_ge(s.arg_ready, n + 1)
        arg = k.arg[:, n % 2, :]
        act.activation(arg, arg, ACT.Exp).then_inc(s.exp_ready, 1)

    def head_norm(ready, m):
        act.wait_ge(s.out_done, ready)
        if m == 1:
            act.wait_ge(s.B_sqrt_used, B_TILES)
        act.activation(k.onorm[:, :, :].rearrange("p t c -> p (t c)"), k.ps[:, 2:4, :].rearrange("p b c -> p (b c)"), ACT.Square).then_inc(s.osq[m], 1)
        act.wait_ge(s.ovar[m], 1)
        act.activation(k.hrt[:, m, :], k.hvar[:, m, :], ACT.Sqrt).then_inc(s.oroot[m], 1)

    act.wait_ge(s.cols_ready, 1)
    act.activation(k.sp_e[:, :], k.cols_of("rg_lambda"), ACT.Abs).then_inc(s.par_act, 1)
    act.wait_ge(s.par_act, 1)
    act.activation(k.sp_e[:, :], k.sp_e[:, :], ACT.Exp, scale=-1.0).then_inc(s.par_act, 1)
    act.wait_ge(s.lb_arg, 1)
    act.activation(k.lb_e[:, :], k.lb_e[:, :], ACT.Exp).then_inc(s.par_act, 1)
    act.wait_ge(s.cond_landed, 16)
    act.activation(k.cvec[:, :], k.cvec[:, :], ACT.Silu).then_inc(s.par_act, 1)
    for j in range(9):
        empty(j)
    act.wait_ge(s.f_ready, 1)
    act.activation(k.lfA[:, :, :], k.lfA[:, :, :], ACT.Ln)
    act.activation(k.f2[:, :, :], k.f2[:, :, :], ACT.Ln).then_inc(s.ln_ready, 1)
    todo = [(t, *it) for t in (0, 1) for it in items]
    for j in range(9, GATE_JOB):
        empty(j)
        while todo and (PREPS * 2 - len(todo)) // 2 <= j - EARLY_JOB + (len(todo) > PREPS):
            prep(*todo.pop(0))
        if j >= EARLY_JOB:
            empty(ADA_JOB + 2 * (j - EARLY_JOB))
            empty(ADA_JOB + 2 * (j - EARLY_JOB) + 1)
    head_norm(2, 0)
    empty(GATE_JOB)
    for f in range(2):
        act.wait_ge(s.out_turned, f + 1)
        act.copy(k.oT[:, f, :], k.ps[:, 2 + f, :]).then_inc(s.A_emptied, 1)
    act.wait_ge(s.main_emptied, job_count(GATE_JOB))
    act.activation(k.f2c, k.lfC, ACT.Abs).then_inc(s.par_act, 1)
    act.wait_ge(s.par_act, 5)
    act.activation(k.f2c, k.f2c, ACT.Exp, scale=-1.0).then_inc(s.par_act, 1)
    act.wait_ge(s.par_act, 6)
    act.activation(k.f2c, k.f2c, ACT.Ln, bias=k.one_col, scale=1.0).then_inc(s.ln_ready, 1)
    for j in range(B_GATE_JOB, ADA_JOB):
        empty(j)
    for t in range(B_TILES):
        act.activation(k.gg[:, t, :], k.gg[:, t, :], ACT.Gelu_apprx_tanh).then_inc(s.gelu_ready, 1)
    todo = [(2, *it) for it in items]
    prep(*todo.pop(0))
    prep(*todo.pop(0))
    for j in range(LATE_JOB, JOBS_1):
        empty(j)
        if todo:
            prep(*todo.pop(0))
        t, step = divmod(j - (LATE_JOB + 7), 3)
        if 0 <= t < B_TILES and step == 0:
            act.wait_ge(s.par_pool, 1)
            if t >= 2:
                act.wait_ge(s.B_sqrt_used, t - 1)
            act.activation(k.th[:, t % 2, :], k.ga[:, t, :], ACT.Tanh, scale=k.sp8[:, t:t + 1]).then_inc(s.B_tanh, 1)
            act.wait_ge(s.B_tanh, t + 1)
            act.activation(k.ga[:, t, :], k.ga[:, t, :], ACT.Exp, scale=k.sp8n[:, t:t + 1]).then_inc(s.B_a, 1)
        if 0 <= t < B_TILES and step == 1:
            act.wait_ge(s.B_square, t + 1)
            act.activation(k.th[:, t % 2, :], k.th[:, t % 2, :], ACT.Sqrt).then_inc(s.B_sqrt, 1)
    head_norm(4, 1)
    for f in range(2):
        act.wait_ge(s.out_turned, 3 + f)
        act.copy(k.oT[:, 6 + f, :], k.ps[:, 2 + f, :]).then_inc(s.C_emptied, 1)


def first_block_vector(dve, k, ch):
    s = k.s
    n_units = [0]

    dve.wait_ge(s.cols_ready, 1)
    lb = k.cols_of("lower")
    dve.tensor_tensor(k.lb_e[:, :], lb, lb, ALU.subtract).then_inc(s.lb_arg, 1)
    dve.wait_ge(s.par_act, 3)
    ch.link(dve.reciprocal(k.lb_r[:, :], k.lb_e[:, :]))
    ch.link(dve.tensor_tensor(k.lb_e[:, :], k.lb_e[:, :], k.lb_r[:, :], ALU.mult))
    ch.link(dve.tensor_tensor(k.lb[:, :], k.lb_e[:, :], k.lb_e[:, :], ALU.subtract))
    ch.link(dve.tensor_scalar(k.lb1[:, :], k.lb[:, :], -1.0, 1.0, ALU.mult, ALU.add))
    dve.wait_ge(s.par_act, 2)
    ch.link(dve.tensor_scalar(k.sp_x[:, :], k.sp_e[:, :], 2.0, None, ALU.add))
    dve.reciprocal(k.sp_x[:, :], k.sp_x[:, :]).then_inc(s.sp_recip, 1)
    dve.wait_ge(s.par_act, 4)
    dve.tensor_copy(k.cond[:, :, :], k.cvec[:, :].unsqueeze(2).to_broadcast([P, KD, 32])).then_inc(s.cond_ready, 1)
    for t in range(A_TILES):
        dve.wait_ge(s.main_emptied, job_count(2 + t))
        f = k.lfA[:, t, :]
        a = ch.mark(dve.tensor_scalar(f, f, k.lb1[:, t:t + 1], k.lb[:, t:t + 1], ALU.mult, ALU.add))
        ch.mark(dve.tensor_scalar(k.keyA[:, t, :], k.keyA[:, t, :], k.lb1[:, t:t + 1], None, ALU.mult))
        ch.after(a)
        ch.link(dve.tensor_scalar(k.f2[:, t, :], f, F_FLOOR, 2.0 ** 60, ALU.max, ALU.mult))
        ch.mark(dve.tensor_scalar(k.f2[:, t, :], k.f2[:, t, :], 1.0, None, ALU.min))
        ins = dve.tensor_scalar(f, f, 2.0 ** -60, None, ALU.max)
        if t == 0:
            ch.mark(ins)
        else:
            ins.then_inc(s.f_ready, 1)
    dve.wait_ge(s.ln_ready, 1)
    for t in range(A_TILES):
        ch.link(dve.tensor_tensor(k.lfA[:, t, :], k.lfA[:, t, :], k.f2[:, t, :], ALU.add))

    def cumulate(t):
        cum = k.tiles[t].cum
        for c in range(TT):
            part = cum[:, c * P:(c + 1) * P]
            ins = dve.tensor_tensor_scan(part, k.ones[:, :], part, 0.0, ALU.mult, ALU.add)
        ins.then_inc(s.cum_ready, 1)
        dve.wait_ge(s.cum_ready, t + 1)

    def prep(t, kind, i):
        tile = k.tiles[t]
        n = (PREPS - 1) * t + (0 if kind == "kd" else 1 + i)
        p = PREPS * t + {"kd": 0, "q0": 1}.get(kind, 2 + i)
        dve.wait_ge(s.exp_ready, p + 1)
        if kind == "kd":
            if t:
                dve.wait_ge(s.unit_done, unit_of(t - 1, "turn") + 1)
            ins = dve.tensor_tensor(k.kd[:, :], tile.key, k.arg[:, n % 2, :], ALU.mult)
        elif kind == "q0":
            q0 = k.q0[:, t % 2, :]
            ins = dve.tensor_tensor(q0, q0, tile.q, ALU.mult)
        else:
            if i >= 2:
                dve.wait_ge(s.unit_done, unit_of(t, "level", i - 2, 1 if t == 2 else 0) + 1)
            elif t:
                dve.wait_ge(s.unit_done, unit_of(t, "turn"))
            seg = {"l": LEVELS[i], "h": 2}
            out = k.qk[:, i % 2, :].rearrange("p (s h l) -> p s h l", **seg)
            e = k.arg[:, n % 2, :].rearrange("p (s h l) -> p s h l", **seg)
            kk = tile.key.rearrange("p (s h l) -> p s h l", **seg)
            qq = tile.q.rearrange("p (s h l) -> p s h l", **seg)
            dve.tensor_tensor(out[:, :, 0, :], kk[:, :, 0, :], e[:, :, 0, :], ALU.mult)
            ins = dve.tensor_tensor(out[:, :, 1, :], qq[:, :, 1, :], e[:, :, 1, :], ALU.mult)
        ins.then_inc(s.prep_ready, 1)

    def empty(t, kind, i=0, pair=0):
        tile = k.tiles[t]
        u = unit_of(t, kind, i, pair)
        assert u == n_units[0]
        n_units[0] += 1
        dve.wait_ge(s.unit_done, u + 1)
        a, b = unit_banks(k, u)
        if kind == "turn":
            if t:
                dve.wait_ge(s.out_done, t)
            ins = dve.tensor_copy(k.kdT[:, :, :].rearrange("p c d -> p (c d)"), a[:, 0:3 * P])
        elif kind == "state":
            for c in range(TT - 1):
                m = ch.mark(dve.memset(k.st(t, c), 0.0))
            ch.after(m)
            for c in range(TT - 1):
                for h in range(tile.heads):
                    own = slice(h * HEAD, (h + 1) * HEAD)
                    r = tile.rows(h)
                    src = (a[r, c * P + h * HEAD:c * P + (h + 1) * HEAD] if t < 2 else
                           (a, b)[c // 2][r, c % 2 * 256 + h * HEAD:c % 2 * 256 + (h + 1) * HEAD])
                    if c == 0:
                        m = dve.tensor_copy(k.st(t, 0)[r, own], src)
                    else:
                        m = dve.scalar_tensor_tensor(out=k.st(t, c)[r, own], in0=k.st(t, c - 1)[r, own], scalar=k.eL[r, c:c + 1],
                                                     in1=src, op0=ALU.mult, op1=ALU.add)
                    if c < TT - 2:
                        m = ch.mark(m)
                if c < TT - 2:
                    ch.after(m)
            ins = m
        else:
            mask = k.masks[:, i, :].unsqueeze(1).to_broadcast([P, TT, P])
            if i == 0 and pair == 0 and t:
                dve.wait_ge(s.out_done, t)
            if i == 0 and t == 0:
                dve.wait_ge(s.masks_ready, 1)
                dve.wait_ge(s.S_clear, 1)
            if i:
                dve.wait_ge(s.unit_emptied, u if t < 2 else u - 1)
            for n, bank in enumerate((a, b)):
                sc = k.scores(t, 2 * pair + n)
                ins = dve.copy_predicated(sc.rearrange("p (c i) -> p c i", c=TT), mask, bank.rearrange("p (c i) -> p c i", c=TT))
        ins.then_inc(s.unit_emptied, 1)

    def attend(t):
        cumulate(t)
        prep(t, "kd", 0)
        dve.wait_ge(s.exp_ready, PREPS * t + 2)
        ends = k.q0[:, t % 2, :].rearrange("p (c i) -> p c i", c=TT)[:, :, P - 1]
        ch.link(dve.tensor_copy(k.eL[:, :], ends))
        prep(t, "q0", 0)
        prep(t, "level", 0)
        prep(t, "level", 1)
        empty(t, "turn")
        empty(t, "state")
        for i in range(N_LEVELS):
            for pair in range(1 if t < 2 else 2):
                empty(t, "level", i, pair)
            if i + 2 < len(LEVELS):
                prep(t, "level", i + 2)
            if t == 2 and i in (2, 4, 5, 7):
                recur((2, 4, 5, 7).index(i))

    def recur(t):
        gi, a, th, xc = k.xb[:, t, B_TAPS - 1:], k.ga[:, t, :], k.th[:, t % 2, :], k.xc[:, t, :]
        dve.wait_ge(s.main_emptied, job_count(B_GATE_JOB + 2 * t + 1))
        m = ch.mark(dve.tensor_tensor(xc, gi, xc, ALU.mult))
        dve.wait_ge(s.B_a, t + 1)
        ch.after(m)
        ch.link(dve.tensor_tensor(gi, a, a, ALU.mult))
        ch.link(dve.scalar_tensor_tensor(out=th, in0=gi, scalar=1.0, in1=th, op0=ALU.add, op1=ALU.mult))
        dve.tensor_scalar(th, th, 0.0, None, ALU.max).then_inc(s.B_square, 1)
        dve.wait_ge(s.B_sqrt, t + 1)
        dve.tensor_tensor(xc, xc, th, ALU.mult).then_inc(s.B_sqrt_used, 1)
        dve.wait_ge(s.B_sqrt_used, t + 1)
        dve.tensor_tensor_scan(gi, a, xc, 0.0, ALU.mult, ALU.add).then_inc(s.B_scan, 1)

    def head_norm(m, v, normed):
        dve.wait_ge(s.osq[m], 1)
        sq = k.onorm[:, :, :].rearrange("p t (h d) -> p (t h) d", d=HEAD)
        ch.link(dve.tensor_reduce(k.hss[:, m, :], sq, AX_X, ALU.add))
        dve.tensor_scalar(k.hvar[:, m, :], k.hss[:, m, :], 1.0 / HEAD, EPS, ALU.mult, ALU.add).then_inc(s.ovar[m], 1)
        dve.wait_ge(s.oroot[m], 1)
        ch.link(dve.reciprocal(k.hrs[:, m, :], k.hrt[:, m, :]))
        ch.link(dve.tensor_tensor(sq, k.ps[:, 2:4, :].rearrange("p b (x d) -> p (b x) d", d=HEAD),
                                  k.hrs[:, m, :].unsqueeze(2).to_broadcast([P, 16, HEAD]), ALU.mult))
        dve.wait_ge(s.gw_ready, m + 1)
        dve.tensor_tensor(k.onorm[:, :, :], k.onorm[:, :, :], v[:, :, 256:512], ALU.mult).then_inc(normed, 1)

    attend(0)
    attend(1)
    head_norm(0, k.VA, s.A_normed)
    for t in range(B_TILES):
        dve.wait_ge(s.main_emptied, job_count(8 + t))
        dve.wait_ge(s.pads_ready, 1)
        out = k.xc[:, t, :]
        ch.link(dve.tensor_scalar(out, k.xb[:, t, 3:3 + T], k.col("rg_w", 3 * B_TILES + t), k.col("rg_b", t), ALU.mult, ALU.add))
        for tap in range(B_TAPS - 1):
            ins = dve.scalar_tensor_tensor(out=out, in0=k.xb[:, t, tap:tap + T], scalar=k.col("rg_w", tap * B_TILES + t),
                                           in1=out, op0=ALU.mult, op1=ALU.add)
            if tap < B_TAPS - 2:
                ch.link(ins)
        ins.then_inc(s.conv_ready, 1)
    dve.wait_ge(s.ln_ready, 2)
    ch.link(dve.tensor_scalar(k.lfC, k.lfC, 0.0, 1.0 / GATE_NORM, ALU.min, ALU.mult))
    ch.link(dve.scalar_tensor_tensor(out=k.lfC, in0=k.f2c, scalar=-1.0 / GATE_NORM, in1=k.lfC, op0=ALU.mult, op1=ALU.add))
    dve.wait_ge(s.out_done, 2)
    dve.wait_ge(s.unit_done, A_UNITS)
    ch.link(dve.memset(k.S_late[:, :, :], 0.0))
    attend(2)
    head_norm(1, k.VC, s.C_normed)
    dve.wait_ge(s.x_again, 16)
    for n, half in enumerate((1, 0)):
        for tt in range(TT):
            dve.wait_ge(s.w_out_done, TT * n + tt + 1)
            xs = k.x[:, tt, half * 512:(half + 1) * 512]
            dve.tensor_tensor(xs, xs, k.ps[:, 4 * half + tt, :], ALU.add).then_inc(s.x1_ready, 1)


def first_block_gpsimd(pool, k):
    s = k.s
    ch = Chain(pool, s.pool_chain)
    make_constants(pool, k, ch)

    def prep(t, kind, i):
        tile = k.tiles[t]
        n = (PREPS - 1) * t + (0 if kind == "kd" else 1 + i)
        if n >= 2:
            t2, m = divmod(n - 2, PREPS - 1)
            pool.wait_ge(s.prep_ready, PREPS * t2 + (1 if m == 0 else 2 + m))
        arg = k.arg[:, n % 2, :]
        if kind == "kd":
            pool.wait_ge(s.cum_ready, t + 1)
            c = tile.cum.rearrange("p (c i) -> p c i", c=TT)
            ins = pool.tensor_tensor(arg.rearrange("p (c i) -> p c i", c=TT), c[:, :, P - 1:P].to_broadcast([P, TT, P]), c, ALU.subtract)
        else:
            half = LEVELS[i]
            c = tile.cum.rearrange("p (s h l) -> p s h l", h=2, l=half)
            out = arg.rearrange("p (s h l) -> p s h l", h=2, l=half)
            mid = c[:, :, 0, half - 1:half].to_broadcast([P, T // (2 * half), half])
            pool.tensor_tensor(out[:, :, 0, :], mid, c[:, :, 0, :], ALU.subtract)
            ins = pool.tensor_tensor(out[:, :, 1, :], c[:, :, 1, :], mid, ALU.subtract)
        ins.then_inc(s.arg_ready, 1)

    def gate_gain(v, cols, at):
        pool.wait_ge(s.main_emptied, job_count(at))
        pool.tensor_tensor(v[:, :, 256:512], v[:, :, 256:512], cols.unsqueeze(1).to_broadcast([P, TT, 256]), ALU.mult)\
            .then_inc(s.gw_ready, 1)

    def softplus():
        e, x, y, z = k.sp_e, k.sp_x, k.sp_y, k.sp_z
        pool.wait_ge(s.sp_recip, 1)
        ch.link(pool.tensor_tensor(x[:, :], e[:, :], x[:, :], ALU.mult))
        ch.link(pool.tensor_tensor(z[:, :], x[:, :], x[:, :], ALU.mult))
        ch.link(pool.tensor_scalar(y[:, :], z[:, :], 1.0 / 19, 1.0 / 17, ALU.mult, ALU.add))
        for n in (15, 13, 11, 9, 7, 5, 3, 1):
            ch.link(pool.tensor_tensor(y[:, :], y[:, :], z[:, :], ALU.mult))
            ch.link(pool.tensor_scalar(y[:, :], y[:, :], 1.0 / n, None, ALU.add))
        ch.link(pool.tensor_tensor(y[:, :], y[:, :], x[:, :], ALU.mult))
        ch.link(pool.tensor_scalar(z[:, :], k.cols_of("rg_lambda"), -1.0, 0.0, ALU.mult, ALU.max))
        ch.link(pool.tensor_scalar(y[:, :], y[:, :], 2.0, None, ALU.mult))
        ch.link(pool.tensor_tensor(y[:, :], y[:, :], z[:, :], ALU.add))
        ch.link(pool.tensor_scalar(k.sp8[:, :], y[:, :], LRU_C, None, ALU.mult))
        pool.tensor_scalar(k.sp8n[:, :], y[:, :], -LRU_C, None, ALU.mult).then_inc(s.par_pool, 1)

    softplus()
    pool.wait_ge(s.small_landed, 48)
    gate_gain(k.VA, k.normw[:, 0:256], 7)
    for t in (0, 1):
        for kind, i in [("kd", 0)] + [("level", i) for i in range(len(LEVELS))]:
            prep(t, kind, i)
    pool.wait_ge(s.unit_done, A_UNITS)
    pool.wait_ge(s.prep_ready, 2 * PREPS)
    pool.memset(k.bd[:, :, :, :], 0.0).then_inc(s.bd_clear, 1)
    pool.wait_ge(s.bd_clear, 1)
    for g, w in enumerate((k.rg_w_a, k.rg_w_x)):
        for b in range(2):
            rows = slice(b * HEAD, (b + 1) * HEAD)
            pool.dma_start(k.bd[rows, g, :, rows], w[0].rearrange("(t b) i j -> b i t j", b=2)[b]).then_inc(s.bd_landed, 16)
    gate_gain(k.VC, k.normw[:, 256:512], GATE_JOB - 1)
    for kind, i in [("kd", 0)] + [("level", i) for i in range(len(LEVELS))]:
        prep(2, kind, i)
    for t in range(B_TILES):
        pool.wait_ge(s.B_scan, t + 1)
        pool.wait_ge(s.gelu_ready, t + 1)
        pool.tensor_tensor(k.oT[:, 2 + t, :], k.xb[:, t, B_TAPS - 1:], k.gg[:, t, :], ALU.mult).then_inc(s.oT_pool, 1)




def gate_tiles(c):
    return range(4 * c, min(4 * c + 4, FT))


FFN_PIECES = (FT + 3) // 4
DOWN_CHUNKS = [(0, 8), (8, 8), (16, 5)]


def ffn_tensor(pe, k):
    s = k.s
    hT_ready(pe, k.norms[1])
    for c in range(FFN_PIECES):
        cols = len(gate_tiles(c)) * P
        for val in range(2):
            n = k.ffn_piece + 2 * c + val
            k.stream1.wait(pe, n)
            for g in gate_tiles(c):
                if g >= 4:
                    pe.wait_ge(s.ffn_val_out if val else s.ffn_gate_out, g - 3)
                mm = features(pe, k.ps[:, 4 * val + g % 4, :], k.stream1.view(n, cols=cols),
                              slice(g % 4 * P, (g % 4 + 1) * P), k.hT)
                mm.then_inc(s.ffn_val if val else s.ffn_gate, 1)
    pe.wait_ge(s.ffn_gate_out, FT)
    pe.wait_ge(s.ffn_val_out, FT)
    for half in range(2):
        for r, (c0, nc_) in enumerate(DOWN_CHUNKS):
            n = k.down_piece + 3 * half + r
            k.stream1.wait(pe, n)
            w = k.stream1.view(n, chunks=nc_)
            for tt in range(TT):
                for c in range(nc_):
                    mm = pe.matmul(k.ps[:, 4 * half + tt, :], k.actT[:, c0 + c, tt * P:(tt + 1) * P], w[:, c, :],
                                   start=(c0 + c == 0), stop=(c0 + c == FT - 1))
                if r == len(DOWN_CHUNKS) - 1:
                    mm.then_inc(s.down_done, 1)
                elif tt == TT - 1:
                    mm.then_inc(s.down_piece_used, 1)


def ffn_scalar(act, k):
    s = k.s

    def gelu(g):
        act.wait_ge(s.ffn_conv, g + 1)
        if g >= 4:
            act.wait_ge(s.ffn_val_out, g - 3)
        act.activation(k.gelu[:, g % 4, :], k.conv[:, g % 2, :], ACT.Gelu_apprx_tanh).then_inc(s.ffn_gelu, 1)

    act.wait_ge(s.ffn_pads, 1)
    for g in range(FT + 1):
        if g < FT:
            act.wait_ge(s.ffn_gate, g + 1)
            if g >= 2:
                act.wait_ge(s.ffn_conv, g - 1)
            act.copy(k.gpad[:, g % 2, FFN_TAPS - 1:], k.ps[:, g % 4, :]).then_inc(s.ffn_gate_out, 1)
        if g:
            gelu(g - 1)


def ffn_vector(dve, k, ch):
    s = k.s
    hT_ready(dve, k.norms[1])
    dve.memset(k.gpad[:, :, 0:FFN_TAPS - 1], 0.0).then_inc(s.ffn_pads, 1)
    for c in range(FFN_PIECES):
        for g in gate_tiles(c):
            dve.wait_ge(s.ffn_gate_out, g + 1)
            if g >= 2:
                dve.wait_ge(s.ffn_gelu, g - 1)
            out, src = k.conv[:, g % 2, :], k.gpad[:, g % 2, :]
            ch.link(dve.tensor_scalar(out, src[:, 2:2 + T], k.col("ffn_w", 2 * FT + g), k.col("ffn_b", g), ALU.mult, ALU.add))
            ch.link(dve.scalar_tensor_tensor(out=out, in0=src[:, 0:T], scalar=k.col("ffn_w", g), in1=out,
                                             op0=ALU.mult, op1=ALU.add))
            dve.scalar_tensor_tensor(out=out, in0=src[:, 1:1 + T], scalar=k.col("ffn_w", FT + g), in1=out,
                                     op0=ALU.mult, op1=ALU.add).then_inc(s.ffn_conv, 1)
        for g in gate_tiles(c):
            dve.wait_ge(s.ffn_val, g + 1)
            dve.wait_ge(s.ffn_gelu, g + 1)
            dve.tensor_tensor(k.actT[:, g, :], k.ps[:, 4 + g % 4, :], k.gelu[:, g % 4, :], ALU.mult).then_inc(s.ffn_val_out, 1)
    for half in range(2):
        for tt in range(TT):
            dve.wait_ge(s.down_done, 4 * half + tt + 1)
            xs = k.x[:, tt, half * 512:(half + 1) * 512]
            dve.tensor_tensor(xs, xs, k.ps[:, 4 * half + tt, :], ALU.add).then_inc(s.x2_ready, 1)



QKV_JOBS = 24


def qkv_tensor(pe, k, a):
    for j in range(QKV_JOBS):
        n = a.first_piece + j // 4
        if j % 4 == 0:
            a.stream.wait(pe, n)
        if j == 0:
            hT_ready(pe, a.norm)
        if j >= 4:
            pe.wait_ge(a.proj_dve if j % 2 else a.proj_act, (j - 4) // 2 + 1)
        bank = k.ps[:, j % 4, :]
        if j < 16:
            mm = features(pe, bank, a.stream.view(n), slice(j % 4 * P, (j % 4 + 1) * P), k.hT)
        else:
            mm = tokens(pe, bank, k.hT, j % 4, a.stream.view(n))
        mm.then_inc(a.proj, 1)


def qkv_out(k, j):
    if j < 8:
        return k.q[:, j, :]
    if j < 16:
        return k.k[:, j - 8, :]
    return k.v[:, j % 4, (j - 16) // 4 * 512:((j - 16) // 4 + 1) * 512]


def qkv_scale(a, j):
    return a.q_scale[j] if j < 8 else 1.0


def qkv_scalar(act, k, a):
    for j in range(0, QKV_JOBS, 2):
        act.wait_ge(a.proj, j + 1)
        act.mul(qkv_out(k, j), k.ps[:, j % 4, :], qkv_scale(a, j)).then_inc(a.proj_act, 1)


def qkv_vector(dve, k, a):
    for j in range(1, QKV_JOBS, 2):
        dve.wait_ge(a.proj, j + 1)
        dve.tensor_scalar(qkv_out(k, j), k.ps[:, j % 4, :], qkv_scale(a, j), None, ALU.mult).then_inc(a.proj_dve, 1)


def out_proj_tensor(pe, k, a):
    for half in range(2):
        n = a.first_piece + 6 + half
        a.stream.wait(pe, n)
        for tt in range(TT):
            tokens(pe, k.ps[:, 4 * half + tt, :], k.oT, tt, a.stream.view(n)).then_inc(a.out, 1)


def out_proj_vector(dve, k, a, gate, tmp):
    dve.wait_ge(a.gate_ready, 1)
    for half in range(2):
        for tt in range(TT):
            j = 4 * half + tt
            dve.wait_ge(a.out, j + 1)
            cols = slice(half * 512, (half + 1) * 512)
            dve.tensor_tensor(tmp[:, j % 2, :], k.ps[:, j, :], gate[:, cols], ALU.mult).then_inc(a.gated, 1)
            dve.wait_ge(a.gated, j + 1)
            dve.tensor_tensor(k.x[:, tt, cols], k.x[:, tt, cols], tmp[:, j % 2, :], ALU.add).then_inc(a.x_ready, 1)



DIFF_UNITS = DIFF_HEADS * TT


def diff_tensor(pe, k, a):
    def scores(i):
        h, qt = divmod(i, TT)
        if i >= 2:
            pe.wait_ge(a.biased, 2 * i - 2)
        for m in range(2):
            r = slice(m * HEAD, (m + 1) * HEAD)
            mm = pe.matmul(k.ps[:, 2 * (i % 2) + m, 0:(qt + 1) * P], k.q[r, h, qt * P:(qt + 1) * P],
                           k.k[r, h, 0:(qt + 1) * P], start=True, stop=True)
        mm.then_inc(a.scored, 1)

    def turn(i):
        pe.wait_ge(a.weighed, i + 1)
        if i >= 2:
            pe.wait_ge(a.turned_out, i - 1)
        for kt in range(i % TT + 1):
            cols = slice(kt * P, (kt + 1) * P)
            mm = pe.transpose(k.ps[:, 4 + i % 2, cols], k.sm[i % 3][:, 0, cols], k.ident[:, :])
        mm.then_inc(a.turned, 1)

    def values(i):
        h, qt = divmod(i, TT)
        pe.wait_ge(a.turned_out, i + 1)
        if h >= 2 and qt == 0:
            pe.wait_ge(a.oT_out, h - 1)
        for kt in range(qt + 1):
            mm = pe.matmul(k.ps[:, 6 + h % 2, qt * P:(qt + 1) * P], k.aT[:, i % 2, kt * P:(kt + 1) * P],
                           k.v[:, kt, h * P:(h + 1) * P], start=(kt == 0), stop=(kt == qt))
        mm.then_inc(a.valued, 1)

    def turn_head(h):
        pe.wait_ge(a.head_normed, h + 1)
        for tt in range(TT):
            mm = pe.transpose(k.ps[:, 6 + h % 2, tt * P:(tt + 1) * P], k.hd[:, tt * P:(tt + 1) * P], k.ident[:, :])
        mm.then_inc(a.head_turned, 1)

    pe.wait_ge(a.proj_act, QKV_JOBS // 2)
    pe.wait_ge(a.proj_dve, QKV_JOBS // 2)
    for i in range(DIFF_UNITS + 5):
        if i < DIFF_UNITS:
            scores(i)
        if 2 <= i <= DIFF_UNITS + 1:
            turn(i - 2)
        if 3 <= i <= DIFF_UNITS + 2:
            values(i - 3)
        if i >= 8 and (i - 8) % TT == 0:
            turn_head((i - 8) // TT)
    pe.wait_ge(a.oT_out, DIFF_HEADS)


def diff_scalar(act, k, a):
    slopes = head_slopes()
    for i in range(DIFF_UNITS + 5):
        if i < DIFF_UNITS:
            kw = (i % TT + 1) * P
            act.wait_ge(a.maxed, i + 1)
            for m in range(2):
                buf = k.sm[i % 3][:, m, 0:kw]
                act.activation(buf, buf, ACT.Exp, bias=k.nmax[:, i % 2, m:m + 1], scale=slopes[i // TT],
                               accum_out=k.esum[:, i % 2, m:m + 1]).then_inc(a.exped, 1)
        if 1 <= i <= DIFF_UNITS:
            u = i - 1
            kw = (u % TT + 1) * P
            act.wait_ge(a.turned, u + 1)
            if u >= 2:
                act.wait_ge(a.valued, u - 1)
            act.copy(k.aT[:, u % 2, 0:kw], k.ps[:, 4 + u % 2, 0:kw]).then_inc(a.turned_out, 1)
        if i >= 6 and (i - 6) % TT == 0 and (i - 6) // TT < DIFF_HEADS:
            h = (i - 6) // TT
            act.wait_ge(a.valued, TT * h + TT)
            if h:
                act.wait_ge(a.head_turned, h)
            act.activation(k.hd[:, :], k.ps[:, 6 + h % 2, :], ACT.Square).then_inc(a.squared, 1)
            act.wait_ge(a.var, h + 1)
            act.activation(k.hsmall[:, 2, :], k.hsmall[:, 1, :], ACT.Sqrt).then_inc(a.rooted, 1)
        if i >= 8 and (i - 8) % TT == 0:
            h = (i - 8) // TT
            act.wait_ge(a.head_turned, h + 1)
            act.activation(k.oT[:, h, :], k.ps[:, 6 + h % 2, :], ACT.Copy, scale=k.subln[:, 0:1]).then_inc(a.oT_out, 1)


def diff_vector(dve, k, a, ch):
    slopes = head_slopes()

    def front(i):
        h, qt = divmod(i, TT)
        kw = (qt + 1) * P
        dve.wait_ge(a.scored, i + 1)
        if i >= 3:
            dve.wait_ge(a.turned, i - 2)
        for m in range(2):
            dve.tensor_tensor_reduce(k.sm[i % 3][:, m, 0:kw], k.ps[:, 2 * (i % 2) + m, 0:kw],
                                     k.dist[:, (TT - 1 - qt) * P:TT * P], 1.0, LEAST, ALU.subtract, ALU.max,
                                     k.nmax[:, i % 2, 2 + m:3 + m]).then_inc(a.biased, 1)
        dve.wait_ge(a.biased, 2 * i + 2)
        dve.tensor_scalar(k.nmax[:, i % 2, 0:2], k.nmax[:, i % 2, 2:4], -slopes[h], None, ALU.mult).then_inc(a.maxed, 1)

    def back(i):
        kw = (i % TT + 1) * P
        dve.wait_ge(a.exped, 2 * i + 2)
        r = k.esum[:, i % 2, 2:4]
        ch.link(dve.reciprocal(r, k.esum[:, i % 2, 0:2]))
        m = ch.mark(dve.tensor_scalar(k.esum[:, i % 2, 4:5], r[:, 1:2], k.lam_neg[:, 0:1], None, ALU.mult))
        p0, p1 = k.sm[i % 3][:, 0, 0:kw], k.sm[i % 3][:, 1, 0:kw]
        ch.link(dve.tensor_scalar(p0, p0, r[:, 0:1], None, ALU.mult))
        dve.scalar_tensor_tensor(out=p0, in0=p1, scalar=k.esum[:, i % 2, 4:5], in1=p0,
                                 op0=ALU.mult, op1=ALU.add).then_inc(a.weighed, 1)

    def head_norm(h):
        sm = k.hsmall
        dve.wait_ge(a.squared, h + 1)
        hd = k.hd[:, :].rearrange("p (t d) -> p t d", t=TT)
        ch.link(dve.tensor_reduce(sm[:, 0, :], hd, AX_X, ALU.add))
        dve.tensor_scalar(sm[:, 1, :], sm[:, 0, :], 1.0 / P, SUBLN_EPS, ALU.mult, ALU.add).then_inc(a.var, 1)
        dve.wait_ge(a.rooted, h + 1)
        ch.link(dve.reciprocal(sm[:, 3, :], sm[:, 2, :]))
        dve.tensor_tensor(hd, k.ps[:, 6 + h % 2, :].rearrange("p (t d) -> p t d", t=TT),
                          sm[:, 3, :].unsqueeze(2).to_broadcast([P, TT, P]), ALU.mult).then_inc(a.head_normed, 1)

    dve.wait_ge(k.s.dist_ready, 1)
    for i in range(DIFF_UNITS + 3):
        if i < DIFF_UNITS:
            front(i)
        if 1 <= i <= DIFF_UNITS:
            back(i - 1)
        if i >= 6 and (i - 6) % TT == 0:
            head_norm((i - 6) // TT)



SB_AT = (0, 512, 1024, 896)
SB_W = 1280


def sb_cols(kt, frm=None):
    frm = kt if frm is None else frm
    return slice(SB_AT[kt] + (frm - kt) * P, SB_AT[kt] + (TT - kt) * P)


def sb_scores(k, h):
    return k.ps[:, 3 * (h % 2):3 * (h % 2) + 3, :].rearrange("p b n -> p (b n)")


def sb_tensor(pe, k, a):
    def scores(h):
        if h >= 2:
            pe.wait_ge(a.exped, h - 1)
        r = slice(h % 2 * HEAD, (h % 2 + 1) * HEAD)
        for kt in range(TT):
            pe.matmul(sb_scores(k, h)[:, sb_cols(kt)], k.k[r, h // 2, kt * P:(kt + 1) * P],
                      k.q[r, h // 2, kt * P:T], start=(kt < TT - 1), stop=False, skip_group_check=True)
        for kt in range(TT):
            mm = pe.matmul(sb_scores(k, h)[:, SB_AT[kt]:SB_AT[kt] + P], k.ident[:, :], k.far,
                           start=False, stop=True, skip_group_check=True)
        mm.then_inc(a.scored, 1)

    def sums(h):
        pe.wait_ge(a.softplus, h + 1)
        for kt in range(TT):
            for st in range(kt, TT):
                lhs = k.minus_later if st == kt else k.minus_ones
                mm = pe.matmul(sb_scores(k, h)[:, sb_cols(kt, st)], lhs, k.sp[:, sb_cols(st)],
                               start=False, stop=True, skip_group_check=True)
        mm.then_inc(a.summed, 1)

    def values(h):
        pe.wait_ge(a.exped, h + 1)
        if h % 2 == 0 and h >= 4:
            pe.wait_ge(a.oT_out, h // 2 - 1)
        out = k.ps[h % 2 * HEAD:(h % 2 + 1) * HEAD, 6 + h // 2 % 2, :]
        for kt in range(TT):
            mm = pe.matmul(out[:, kt * P:T], k.v[:, kt, h * HEAD:(h + 1) * HEAD], k.tt[:, h % 2, sb_cols(kt)],
                           start=(kt == 0), stop=(kt == TT - 1))
        mm.then_inc(a.valued, 1)

    pe.wait_ge(a.proj_act, QKV_JOBS // 2)
    pe.wait_ge(a.proj_dve, QKV_JOBS // 2)
    for h in range(SB_HEADS + 2):
        if h < SB_HEADS:
            scores(h)
        if 1 <= h <= SB_HEADS:
            sums(h - 1)
        if h >= 2:
            values(h - 2)
    pe.wait_ge(a.oT_out, SB_HEADS // 2)


def sb_scalar(act, k, a):
    for h in range(SB_HEADS + 2):
        if h < SB_HEADS:
            act.wait_ge(a.scored, h + 1)
            if h:
                act.wait_ge(a.softplus, h)
            act.activation(k.ln[:, :], sb_scores(k, h)[:, 0:SB_W], ACT.Abs).then_inc(a.steps, 1)
            act.wait_ge(a.steps, 2 * h + 1)
            act.activation(k.ln[:, :], k.ln[:, :], ACT.Exp, scale=-1.0).then_inc(a.steps, 1)
            act.wait_ge(a.steps, 2 * h + 2)
            act.activation(k.ln[:, :], k.ln[:, :], ACT.Ln, bias=k.one_col, scale=1.0).then_inc(a.logged, 1)
        if 1 <= h <= SB_HEADS:
            act.wait_ge(a.summed, h)
            if h >= 3:
                act.wait_ge(a.valued, h - 2)
            act.activation(k.tt[:, (h - 1) % 2, :], sb_scores(k, h - 1)[:, 0:SB_W], ACT.Exp).then_inc(a.exped, 1)
        if h >= 3 and h % 2 == 1:
            pair = (h - 3) // 2
            act.wait_ge(a.valued, 2 * pair + 2)
            act.copy(k.oT[:, pair, :], k.ps[:, 6 + pair % 2, :]).then_inc(a.oT_out, 1)


def sb_vector(dve, k, a):
    for h in range(SB_HEADS):
        dve.wait_ge(a.logged, h + 1)
        if h:
            dve.wait_ge(a.summed, h)
        dve.scalar_tensor_tensor(out=k.sp[:, :], in0=sb_scores(k, h)[:, 0:SB_W], scalar=0.0, in1=k.ln[:, :],
                                 op0=ALU.max, op1=ALU.add).then_inc(a.softplus, 1)




def router_tensor(pe, k, m):
    hT_ready(pe, m.norm)
    pe.wait_ge(m.router_landed, 64)
    for tt in range(TT):
        for c in range(KD):
            mm = pe.matmul(k.ps[:, 0, tt * 36:(tt + 1) * 36], k.hT[:, c, tt * P:(tt + 1) * P], k.rw[:, c, :],
                           start=(c == 0), stop=(c == KD - 1))
    mm.then_inc(m.logits, 1)
    pe.wait_ge(m.chosen, 1)
    for tt in range(TT):
        for src in range(tt + 1):
            lhs = k.before if src == tt else k.ones
            pe.matmul(k.ps[:, 1, tt * E:(tt + 1) * E], lhs[:, :], k.sel[:, src, :], start=(src == 0), stop=(src == tt))
    for src in range(TT):
        mm = pe.matmul(k.ps[:, 2, 0:E], k.ones[:, :], k.sel[:, src, :], start=(src == 0), stop=(src == TT - 1))
    mm.then_inc(m.ranked, 1)


def router_vector(dve, k, m, ch):
    f = k.route

    def first_of(out, values, top, order, n, scratch):
        ch.link(dve.tensor_tensor(scratch, values, top.to_broadcast([P, TT, n]), ALU.is_equal))
        ch.link(dve.tensor_tensor(scratch, scratch, order.unsqueeze(1).to_broadcast([P, TT, n]), ALU.mult))
        ch.link(dve.tensor_reduce(f("top_order")[:, :, 0], scratch, AX_X, ALU.max))
        ch.link(dve.tensor_tensor(out, scratch, f("top_order").to_broadcast([P, TT, n]), ALU.is_equal))

    dve.wait_ge(m.logits, 1)
    lg = f("logits")
    ch.link(dve.tensor_tensor(lg, k.ps[:, 0, 0:TT * 36].rearrange("p (t n) -> p t n", t=TT),
                              k.rb[:, :].unsqueeze(1).to_broadcast([P, TT, 36]), ALU.add))
    g, e = lg[:, :, 0:GROUPS], lg[:, :, GROUPS:36]
    gm = f("g_max")
    ch.link(dve.tensor_reduce(gm[:, :, 0], g, AX_X, ALU.max))
    dve.tensor_tensor(f("g_exp"), g, gm.to_broadcast([P, TT, GROUPS]), ALU.subtract).then_inc(m.g_diff, 1)
    first_of(f("g_hot"), g, gm, k.iota[:, 0:GROUPS], GROUPS, f("g_tmp"))
    hot = f("g_hot")
    ch.link(dve.tensor_scalar(f("g_tmp"), hot, -1.0, 1e30, ALU.add, ALU.mult))
    em = f("e_mask")
    shape = [P, TT, GROUPS, PER_GROUP]
    by_group = em.rearrange("p t (g e) -> p t g e", g=GROUPS)
    ch.link(dve.tensor_tensor(by_group, e.rearrange("p t (g e) -> p t g e", g=GROUPS),
                              hot.unsqueeze(3).to_broadcast(shape), ALU.mult))
    ch.link(dve.tensor_tensor(by_group, by_group, f("g_tmp").unsqueeze(3).to_broadcast(shape), ALU.add))
    v1, v2 = f("v1"), f("v2")
    ch.link(dve.tensor_reduce(v1[:, :, 0], em, AX_X, ALU.max))
    first_of(f("hot1"), em, v1, k.iota[:, 4:36], E, f("e_tmp"))
    ch.link(dve.scalar_tensor_tensor(out=em, in0=f("hot1"), scalar=-1e38, in1=em, op0=ALU.mult, op1=ALU.add))
    ch.link(dve.tensor_reduce(v2[:, :, 0], em, AX_X, ALU.max))
    first_of(f("hot2"), em, v2, k.iota[:, 4:36], E, f("e_tmp"))
    dve.tensor_tensor(k.sel[:, :, :], f("hot1"), f("hot2"), ALU.add).then_inc(m.chosen, 1)
    dve.tensor_tensor(f("e2")[:, :, 0], v2[:, :, 0], v1[:, :, 0], ALU.subtract).then_inc(m.e_diff, 1)
    dve.wait_ge(m.ranked, 1)
    ch.link(dve.tensor_copy(f("count"), k.ps[:, 2, 0:E]))
    ch.link(dve.tensor_tensor(f("cmp"), f("count").unsqueeze(2).to_broadcast([P, E, 8]),
                              k.iota[:, 36:44].unsqueeze(1).to_broadcast([P, E, 8]), ALU.is_gt))
    ch.link(dve.tensor_reduce(f("blocks"), f("cmp"), AX_X, ALU.add))
    ch.link(dve.tensor_tensor_scan(f("end"), k.ones[:, 0:E], f("blocks"), 0.0, ALU.mult, ALU.add))
    ch.mark(dve.tensor_scalar(f("first"), k.iota[:, 68:68 + E], float(BLOCK), None, ALU.mult))
    ch.link(dve.tensor_tensor(f("start"), f("end"), f("blocks"), ALU.subtract))
    ch.link(dve.tensor_scalar(f("start"), f("start"), float(BLOCK), float(BLOCK * (E - 1)), ALU.mult, ALU.add))
    ch.link(dve.tensor_tensor(f("start"), f("start"), f("first"), ALU.subtract))
    rank = k.ps[:, 1, 0:TT * E].rearrange("p (t e) -> p t e", t=TT)
    slot, past = f("e_mask"), f("past")
    for tt in range(TT):
        n = ch.mark(dve.scalar_tensor_tensor(out=past[:, tt, :], in0=rank[:, tt, :], scalar=float(BLOCK), in1=f("start"),
                                             op0=ALU.is_ge, op1=ALU.mult))
    ch.link(dve.tensor_tensor(slot, rank, f("first").unsqueeze(1).to_broadcast([P, TT, E]), ALU.add))
    ch.link(dve.tensor_tensor(slot, slot, past, ALU.add))
    for hot in ("hot1", "hot2"):
        n = ch.mark(dve.tensor_tensor(f(hot), slot, f(hot), ALU.mult))
    ch.after(n)
    for n, hot in enumerate(("hot1", "hot2")):
        done = ch.mark(dve.tensor_reduce(f("slot_f")[:, n * TT:(n + 1) * TT], f(hot), AX_X, ALU.add))
    ch.after(done)
    ch.link(dve.tensor_copy(k.slot[:, :, :].rearrange("p n t -> p (n t)"), f("slot_f")))
    dve.tensor_copy(k.meta[0:1, 1:1 + E], k.iota[0:1, 68:68 + E]).then_inc(m.slots_set, 1)
    ends = f("end")[0:1, :].unsqueeze(1).to_broadcast([1, EXTRA, E])
    block = k.iota[0:1, 68:68 + EXTRA].unsqueeze(2).to_broadcast([1, EXTRA, E])
    ch.link(dve.tensor_tensor(k.big[0:1, :].rearrange("p (b e) -> p b e", e=E), ends, block, ALU.is_le))
    ch.link(dve.tensor_reduce(f("owner")[0:1, :], k.big[0:1, :].rearrange("p (b e) -> p b e", e=E), AX_X, ALU.add))
    ch.link(dve.tensor_scalar(f("owner")[0:1, :], f("owner")[0:1, :], float(E - 1), None, ALU.min))
    ch.link(dve.tensor_copy(k.meta[0:1, 1 + E:1 + MAX_BLOCKS], f("owner")[0:1, :]))
    ch.link(dve.tensor_scalar(f("owner")[0:1, 0:EXTRA // 2], k.iota[0:1, 44:44 + EXTRA // 2], f("end")[0:1, E - 1:E], None, ALU.is_lt))
    ch.link(dve.tensor_reduce(f("slot_f")[0:1, 0:1], f("owner")[0:1, 0:EXTRA // 2], AX_X, ALU.add))
    dve.tensor_scalar(k.meta[0:1, 0:1], f("slot_f")[0:1, 0:1], float(E // 2), None, ALU.add).then_inc(m.routed, 1)
    dve.wait_ge(m.exps, 2)
    ch.link(dve.tensor_reduce(f("g_sum")[:, :, 0], f("g_exp"), AX_X, ALU.add))
    ch.link(dve.tensor_scalar(f("w1"), f("e2"), 1.0, None, ALU.add))
    ch.link(dve.tensor_tensor(f("w1"), f("w1"), f("g_sum"), ALU.mult))
    ch.link(dve.reciprocal(f("w1"), f("w1")))
    dve.tensor_tensor(f("w2"), f("w1"), f("e2"), ALU.mult).then_inc(m.weights_ready, 1)
    dve.wait_ge(m.weights_ready, 1)


def router_scalar(act, k, m):
    act.wait_ge(m.g_diff, 1)
    act.activation(k.route("g_exp"), k.route("g_exp"), ACT.Exp).then_inc(m.exps, 1)
    act.wait_ge(m.e_diff, 1)
    act.activation(k.route("e2"), k.route("e2"), ACT.Exp).then_inc(m.exps, 1)


def pair_count(eng, k, m):
    eng.wait_ge(m.routed, 1)
    return eng.value_load(k.meta[0:1, 0:1], min_val=E // 2, max_val=PAIRS)


def moe_sync(sp, k, m, a):
    kinds = ((m.w_gate, m.gate_landed, m.gated), (m.w_up, m.up_landed, m.upped), (m.w_down, m.down_landed, m.downed))

    def weights(kind, b, expert):
        src = kinds[kind][0][bass.ds(expert, 1), :, :].rearrange("a (p k) n -> p (a k n)", p=P)
        sp.dma_start(k.ring[:, 2 * kind + b, :], src).then_inc(kinds[kind][1], 16)

    late = {(a.first_piece + 6 + half) % RING: half for half in range(2)}
    sp.wait_ge(a.proj, QKV_JOBS)
    for slot in sorted(range(RING), key=lambda n: n in late):
        if slot in late:
            sp.wait_ge(a.out, TT * (late[slot] + 1))
        weights(slot // 2, slot % 2, slot % 2)
    n = pair_count(sp, k, m)
    sp.wait_ge(m.scattered, 16 * 2 * TT)
    sp.dma_start(k.xg[:, :], k.x_slots[0:P, :]).then_inc(m.x_landed, 16)
    with sp.Fori(0, n - 1) as i:
        sp.wait_ge(m.x_turned, i + 2)
        sp.dma_start(k.xg[:, :], k.x_slots[bass.ds(i * P + P, P), :]).then_inc(m.x_landed, 16)
        experts = [sp.value_load(k.meta[0:1, bass.ds(i * 2 + 3 + b, 1)], min_val=0, max_val=E - 1) for b in range(2)]
        for kind in range(3):
            sp.wait_ge(kinds[kind][2], i + 2)
            for b in range(2):
                weights(kind, b, experts[b])
    return n, [kind[2] for kind in kinds]


def moe_tensor(pe, k, m):
    n = pair_count(pe, k, m)
    for opened in (m.x_turned, m.gated, m.upped, m.downed, m.h_turned):
        pe.sem_inc(opened, 1)
    halves = (slice(0, BLOCK), slice(BLOCK, P))
    with pe.Fori(0, n) as i:
        pe.wait_ge(m.x_landed, i * 16 + 16)
        for c in range(KD):
            mm = pe.transpose(k.ps[:, c // 4, c % 4 * P:(c % 4 + 1) * P], k.xg[:, c::KD], k.ident[:, :])
        mm.then_inc(m.x_turned, 1)
        pe.wait_ge(m.xT_act, i + 1)
        pe.wait_ge(m.xT_dve, i + 1)
        pe.wait_ge(m.hidden, i + 1)
        for kind, (landed, done) in enumerate(((m.gate_landed, m.gated), (m.up_landed, m.upped))):
            pe.wait_ge(landed, i * 32 + 32)
            for c in range(KD):
                for b, slots in enumerate(halves):
                    w = k.ring[:, 2 * kind + b, :].rearrange("p (k n) -> p k n", k=KD)
                    mm = pe.matmul(k.ps[slots, 2 + kind, :], k.xT[:, c, slots], w[:, c, :],
                                   start=(c == 0), stop=(c == KD - 1))
            mm.then_inc(done, 1)
        pe.wait_ge(m.hidden, i + 2)
        for c in range(KH):
            mm = pe.transpose(k.ps[:, 4, c * P:(c + 1) * P], k.hid[:, c::KH], k.ident[:, :])
        mm.then_inc(m.h_turned, 1)
        pe.wait_ge(m.hT_out, i + 1)
        pe.wait_ge(m.down_landed, i * 32 + 32)
        pe.wait_ge(m.y_act, i + 1)
        pe.wait_ge(m.y_dve, i + 1)
        for half in range(2):
            for c in range(KH):
                for b, slots in enumerate(halves):
                    w = k.ring[:, 4 + b, :].rearrange("p (k n) -> p k n", k=KH)
                    mm = pe.matmul(k.ps[slots, 5 + half, :], k.hTt[:, c, slots], w[:, c, half * 512:(half + 1) * 512],
                                   start=(c == 0), stop=(c == KH - 1))
        mm.then_inc(m.downed, 1)


def moe_scalar(act, k, m):
    n = pair_count(act, k, m)
    act.sem_inc(m.y_act, 1)
    act.sem_inc(m.y_stored, 1)
    with act.Fori(0, n) as i:
        act.wait_ge(m.x_turned, i + 2)
        act.wait_ge(m.upped, i + 1)
        for c in range(KD // 2):
            ins = act.activation(k.xT[:, c, :], k.ps[:, 0, c * P:(c + 1) * P], ACT.Identity,
                                 bias=m.norm.shift(c), scale=m.norm.gain(c))
        ins.then_inc(m.xT_act, 1)
        act.wait_ge(m.gated, i + 2)
        act.wait_ge(m.hidden, i + 1)
        act.activation(k.sg[:, :], k.ps[:, 2, :], ACT.Silu).then_inc(m.silu, 1)
        act.wait_ge(m.h_turned, i + 2)
        act.copy(k.hTt[:, :, :].rearrange("p c s -> p (c s)"), k.ps[:, 4, :]).then_inc(m.hT_out, 1)
        act.wait_ge(m.downed, i + 2)
        act.wait_ge(m.y_stored, i * 16 + 1)
        act.copy(k.ys[:, 0:512], k.ps[:, 5, :]).then_inc(m.y_act, 1)
        act.wait_ge(m.y_act, i + 2)
        act.wait_ge(m.y_dve, i + 2)
        act.dma_start(k.y_slots[bass.ds(i * P, P), :], k.ys[:, :]).then_inc(m.y_stored, 16)


def moe_vector(dve, k, m):
    n = pair_count(dve, k, m)
    dve.sem_inc(m.y_dve, 1)
    dve.sem_inc(m.hidden, 1)
    with dve.Fori(0, n) as i:
        dve.wait_ge(m.x_turned, i + 2)
        dve.wait_ge(m.upped, i + 1)
        for c in range(KD // 2, KD):
            ins = dve.tensor_scalar(k.xT[:, c, :], k.ps[:, 1, (c - 4) * P:(c - 3) * P], m.norm.gain(c), m.norm.shift(c),
                                    ALU.mult, ALU.add)
        ins.then_inc(m.xT_dve, 1)
        dve.wait_ge(m.upped, i + 2)
        dve.wait_ge(m.silu, i + 1)
        dve.wait_ge(m.h_turned, i + 1)
        dve.tensor_tensor(k.hid[:, :], k.ps[:, 3, :], k.sg[:, :], ALU.mult).then_inc(m.hidden, 1)
        dve.wait_ge(m.downed, i + 2)
        dve.wait_ge(m.y_stored, i * 16 + 1)
        dve.tensor_copy(k.ys[:, 512:1024], k.ps[:, 6, :]).then_inc(m.y_dve, 1)
    dve.wait_ge(m.y_stored, n * 16 + 1)
    dve.memset(k.all_stored[:, :], 0.0).then_inc(m.all_stored, 1)


def moe_gpsimd(pool, k, m):
    pool.wait_ge(m.slots_set, 1)
    m.norm.after(pool, "xn_act", 2)
    m.norm.after(pool, "xn_dve", 2)
    for tt in range(TT):
        for c in range(2):
            pool.indirect_dma_start(k.x_slots, bass.IndirectOffsetOnAxis(ap=k.slot[:, c, tt:tt + 1], axis=0),
                                    k.xn[:, tt, :], None).then_inc(m.scattered, 16)
    pool.wait_ge(m.all_stored, 1)
    pool.wait_ge(m.scattered, 16 * 2 * TT)
    for tt in range(TT):
        for c in range(2):
            pool.indirect_dma_start(k.yg[:, 2 * tt + c, :], None, k.y_slots,
                                    bass.IndirectOffsetOnAxis(ap=k.slot[:, c, tt:tt + 1], axis=0)).then_inc(m.gathered[tt], 16)


def combine_scalar(act, k, m):
    act.wait_ge(m.weights_ready, 1)
    for tt in range(TT):
        act.wait_ge(m.gathered[tt], 32)
        y1 = k.yg[:, 2 * tt, :]
        act.activation(y1, y1, ACT.Copy, scale=k.route("w1")[:, tt, :]).then_inc(m.weighed, 1)


def combine_vector(dve, k, m, ch):
    dve.wait_ge(m.gate_ready, 1)
    for tt in range(TT):
        dve.wait_ge(m.gathered[tt], 32)
        y1, y2 = k.yg[:, 2 * tt, :], k.yg[:, 2 * tt + 1, :]
        dve.wait_ge(m.weighed, tt + 1)
        ch.link(dve.scalar_tensor_tensor(out=y1, in0=y2, scalar=k.route("w2")[:, tt, :], in1=y1, op0=ALU.mult, op1=ALU.add))
        ch.link(dve.tensor_tensor(y1, y1, k.gate_m[:, :], ALU.mult))
        dve.tensor_tensor(k.x[:, tt, :], k.x[:, tt, :], y1, ALU.add).then_inc(m.x_ready, 1)




PARAM_ROWS = [("ffn_w", FFN_TAPS * FT), ("ffn_b", FT), ("rg_w", B_TAPS * B_TILES), ("rg_b", B_TILES), ("rg_b_a", B_TILES),
              ("rg_b_x", B_TILES), ("rg_lambda", B_TILES), ("lower", A_TILES), ("gla_b", 1), ("subln", 1)]
PARAM_AT = {name: sum(n for _, n in PARAM_ROWS[:i]) for i, (name, _) in enumerate(PARAM_ROWS)}
PARAMS = sum(n for _, n in PARAM_ROWS)

ROUTE = [("logits", 36), ("g_max", 1), ("g_exp", 4), ("g_hot", 4), ("g_tmp", 4), ("top_order", 1), ("e_mask", 32),
         ("e_tmp", 32), ("v1", 1), ("v2", 1), ("hot1", 32), ("hot2", 32), ("past", 32), ("e2", 1), ("g_sum", 1), ("w1", 1), ("w2", 1)]


def make_constants(pool, k, ch):
    s = k.s
    pool.memset(k.ones[:, :], 1.0)
    ch.link(pool.memset(k.ident[:, :], 0.0))
    pool.affine_select(out=k.ident[:, :], in_=k.ident[:, :], compare_op=ALU.not_equal, fill=1.0, base=0,
                       pattern=[[-1, P]], channel_multiplier=1).then_inc(s.ident_ready, 1)
    pool.wait_ge(s.ident_ready, 1)
    pool.affine_select(out=k.before[:, :], in_=k.ones[:, :], compare_op=ALU.is_gt, fill=0.0, base=0,
                       pattern=[[1, P]], channel_multiplier=-1)
    pool.memset(k.xb[:, :, 0:B_TAPS - 1], 0.0).then_inc(s.pads_ready, 1)
    ch.link(pool.memset(k.mask_f[:, :, :], 0.0))
    for i, half in enumerate(LEVELS):
        m = k.mask_f[:, i, :].rearrange("p (s h l) -> p s h l", h=2, l=half)[:, :, 1, :]
        n = P // (2 * half)
        ch.link(pool.memset(m, 1.0))
        ch.link(pool.affine_select(out=m, in_=m, compare_op=ALU.is_ge, fill=0.0, base=0,
                                   pattern=[[-2 * half, n], [0, half]], channel_multiplier=1))
        ch.link(pool.affine_select(out=m, in_=m, compare_op=ALU.is_ge, fill=0.0, base=half - 1,
                                   pattern=[[2 * half, n], [0, half]], channel_multiplier=-1))
    ch.link(pool.tensor_copy(k.mask_f[:, N_LEVELS - 1, :], k.ident[:, :]))
    pool.tensor_copy(k.masks[:, :, :], k.mask_f[:, :, :]).then_inc(s.masks_ready, 1)
    it = k.iota_i
    for c0, cn, step, base in ((0, GROUPS, -1, GROUPS), (4, E, -1, E), (36, 8, BLOCK, BLOCK), (44, PAIRS, 2, 0), (68, MAX_BLOCKS, 1, 0)):
        ins = pool.iota(it[:, c0:c0 + cn], pattern=[[step, cn]], base=base, channel_multiplier=0)
    ch.link(ins)
    pool.tensor_copy(k.iota[:, :], it[:, :]).then_inc(s.iota_ready, 1)
    pool.wait_ge(s.iota_ready, 1)
    pool.memset(k.S[:, :, :], 0.0).then_inc(s.S_clear, 1)


def parameters_vector(dve, k):
    s = k.s
    dve.wait_ge(s.ident_ready, 1)
    dve.tensor_reduce(k.four[:, :], k.ident[:, 0:P:32], AX_X, ALU.add).then_inc(s.four_ready, 1)
    dve.wait_ge(s.rows_turned, 1)
    dve.tensor_copy(k.cols[:, :], k.ps[:, 0, 0:PARAMS]).then_inc(s.cols_ready, 1)
    dve.wait_ge(s.lam_landed, 64)
    dve.tensor_tensor(k.lprod[:, :], k.lvec[:, 0:4:2], k.lvec[:, 1:4:2], ALU.mult).then_inc(s.lam_prod, 1)
    dve.wait_ge(s.lam_exp, 1)
    dve.tensor_tensor(k.lam_neg[:, :], k.lexp[:, 1:2], k.lexp[:, 0:1], ALU.subtract).then_inc(s.lam_diff, 1)
    dve.wait_ge(s.lam_diff, 1)
    dve.tensor_scalar(k.lam_neg[:, :], k.lam_neg[:, :], -LAMBDA_INIT, None, ALU.add)
    dve.wait_ge(s.cols_ready, 1)
    dve.tensor_scalar(k.subln[:, :], k.col("subln", 0), 1.0 - LAMBDA_INIT, None, ALU.mult).then_inc(s.lam_ready, 1)


def parameters_tensor(pe, k):
    s = k.s
    pe.wait_ge(s.ident_ready, 1)
    pe.wait_ge(s.rows_landed, 16 * len(PARAM_ROWS))
    pe.transpose(k.ps[:, 0, 0:PARAMS], k.rows[0:PARAMS, :], k.ident[0:PARAMS, 0:PARAMS]).then_inc(s.rows_turned, 1)
    pe.wait_ge(s.lam_prod, 1)
    pe.matmul(k.ps[:, 1, 0:2], k.ones[0:HEAD, :], k.lprod[:, :], start=True, stop=True).then_inc(s.lam_sum, 1)
    pe.wait_ge(s.cols_ready, 1)
    pe.wait_ge(s.lam_exp, 1)


def modulation_gpsimd(pool, k):
    s = k.s
    pool.wait_ge(s.row_out, 16 * ADA_PIECES)
    for l in range(2):
        for i, v in enumerate((0, 1, 3, 4)):
            pool.dma_start(k.mod[:, l, i, :], k.mod_rows[l, v, :].rearrange("(p k) -> p k", p=P)).then_inc(s.mod_landed, 16)
            pool.dma_start(k.modb[:, l, i, :], k.ada_b[l, v * D:(v + 1) * D].rearrange("(p k) -> p k", p=P)).then_inc(s.mod_landed, 16)
    pool.wait_ge(s.mod_landed, 16 * 16)
    pool.tensor_tensor(k.mod[:, :, :, :], k.mod[:, :, :, :], k.modb[:, :, :, :], ALU.add).then_inc(s.mod_steps, 1)
    pool.wait_ge(s.mod_steps, 1)
    for l in range(2):
        for i in (1, 3):
            pool.tensor_scalar(k.mod[:, l, i, :], k.mod[:, l, i, :], 1.0, None, ALU.add).then_inc(s.mod_steps, 1)
    pool.wait_ge(s.mod_steps, 5)
    pool.wait_ge(s.gains_landed, 16 * 6)
    for l in range(2):
        for i, g in ((1, 2 + 2 * l), (3, 3 + 2 * l)):
            ins = pool.tensor_tensor(k.mod[:, l, i, :], k.mod[:, l, i, :], k.gains[:, g, :], ALU.mult)
    ins.then_inc(s.mod_ready, 1)


def distances_gpsimd(pool, k):
    steps = k.s.dist_steps
    pool.iota(k.dist_i, pattern=[[1, T]], base=-(T - P), channel_multiplier=-1).then_inc(steps, 1)
    pool.wait_ge(steps, 1)
    pool.tensor_copy(k.dist, k.dist_i).then_inc(steps, 1)
    pool.wait_ge(steps, 2)
    pool.tensor_scalar(k.sm[0][:, 0, :], k.dist, -2.0, 0.0, ALU.mult, ALU.max).then_inc(steps, 1)
    pool.wait_ge(steps, 3)
    pool.tensor_tensor(k.dist, k.dist, k.sm[0][:, 0, :], ALU.add).then_inc(steps, 1)
    pool.wait_ge(steps, 4)
    pool.memset(k.dist[0:CHUNK, T - CHUNK:T], F_SLOPE_MASK).then_inc(k.s.dist_ready, 1)


def gate_rows(pool, k, l, v, out, tmp, landed, ready):
    pool.dma_start(out, k.mod_rows[l, v:v + 1, :].to_broadcast([P, D])).then_inc(landed, 16)
    pool.dma_start(tmp, k.ada_b[l:l + 1, v * D:(v + 1) * D].to_broadcast([P, D])).then_inc(landed, 16)
    pool.wait_ge(landed, 32)
    pool.tensor_tensor(out, out, tmp, ALU.add).then_inc(ready, 1)



ARENA = 18124
LEAST = -3e38
F_FAR = 1e30
F_SLOPE_MASK = 1e32


def place(k, nc, ctx):

    def sb(name, shape, dt=F32):
        return ctx.enter_context(nc.sbuf_tensor(name, shape, dt))

    k.ring = sb("ring", [P, RING, SLOT_F])
    xbuf = sb("x", [P, TT * D])
    k.x = xbuf[:, :].rearrange("p (t d) -> p t d", t=TT)
    k.hT = sb("hT", [P, KD, T])
    k.oT = k.hT
    arena = sb("arena", [P, ARENA])
    k.ps = ctx.enter_context(nc.psum_tensor("ps", [P, 8, 512], F32))

    def at(off, *shape, base=arena):
        n = 1
        for d in shape:
            n *= d
        flat = base[:, off:off + n]
        if len(shape) == 2:
            return flat.rearrange("p (a b) -> p a b", b=shape[1])
        if len(shape) == 3:
            return flat.rearrange("p (a b c) -> p a b c", b=shape[1], c=shape[2])
        return flat

    k.ident, k.ones, k.before = sb("ident", [P, P]), sb("ones", [P, P]), sb("before", [P, P])
    k.masks = sb("masks", [P, N_LEVELS, P], U8)
    k.cols = sb("cols", [P, PARAMS])
    k.col = lambda name, i: k.cols[:, PARAM_AT[name] + i:PARAM_AT[name] + i + 1]
    k.cols_of = lambda name: k.cols[:, PARAM_AT[name]:PARAM_AT[name] + dict(PARAM_ROWS)[name]]
    k.gains = sb("gains", [P, 6, KD])
    k.mod, k.modb = sb("mod", [P, 2, 4, KD]), at(16500, 8, KD).rearrange("p (l v) k -> p l v k", l=2)
    k.iota = sb("iota", [P, 68 + MAX_BLOCKS])
    k.one_col = k.ones[:, 0:1]
    k.subln, k.lam_neg, k.lvec, k.lprod, k.lexp = (sb("subln", [P, 1]), sb("lam_neg", [P, 1]), sb("lvec", [HEAD, 4]),
                                                   sb("lprod", [HEAD, 2]), sb("lexp", [P, 2]))
    k.ss, k.vr, k.rt, k.rstd = (sb(n, [P, TT]) for n in ("ss", "vr", "rt", "rstd"))
    k.all_stored = sb("all_stored", [1, 1])
    k.slot = sb("slot", [P, 2, TT], I32)
    k.meta = sb("meta", [1, 2 + MAX_BLOCKS], I32)
    k.xn = at(0, TT, D)

    k.cvec, k.cond, k.four = sb("cvec", [P, KD]), sb("cond", [P, KD, 32]), sb("four", [P, 1])
    k.gate_up, k.normw = sb("gate_up", [RANK, P]), sb("normw", [P, 512])
    k.sp_e, k.sp_x, k.sp_y, k.sp_z, k.sp8, k.sp8n = (sb(n, [P, B_TILES]) for n in ("sp_e", "sp_x", "sp_y", "sp_z", "sp8", "sp8n"))
    k.lb_e, k.lb_r, k.lb, k.lb1 = (sb(n, [P, A_TILES]) for n in ("lb_e", "lb_r", "lb", "lb1"))
    k.eL = sb("eL", [P, TT])
    k.hss, k.hvar, k.hrt, k.hrs = (sb(n, [P, 2, 16]) for n in ("hss", "hvar", "hrt", "hrs"))
    k.arg, k.qk = at(0, 2, T, base=xbuf), at(1024, 2, T, base=xbuf)
    k.kd, k.q0, k.kdT = at(2048, T, base=xbuf), at(2560, 2, T, base=xbuf), at(3584, 3, P, base=xbuf)
    k.f2 = k.qk
    k.qA, k.S_late, k.keyA, k.lfA, k.VA = at(0, 2, T), at(0, 2, T), at(1024, 2, T), at(2048, 2, T), at(3072, TT, 512)
    k.bd = at(1024, 8, P).rearrange("p (g t) c -> p g t c", g=2)
    k.ga = at(3072, B_TILES, T)
    k.qC, k.kC, k.lfC, k.VC = at(5120, T), at(5632, T), at(6144, T), at(6656, TT, 512)
    k.xb, k.xc, k.gg = at(8704, B_TILES, T + B_TAPS - 1), at(10764, B_TILES, T), at(12812, B_TILES, T)
    k.S = at(14860, 2, T)
    k.onorm, k.th, k.part = at(15884, TT, 256), at(15884, 2, T), at(16908, T)
    k.f2c = k.th[:, 0, :]
    k.lr = k.lfC[0:RANK, :]
    k.row = at(17420, 512)[0:1, :]
    k.st = lambda t, c: at(3584 + c * P, P, base=xbuf) if t < 2 else at((3584, 3840, 2048)[c], 2 * P, base=xbuf)
    k.rows, k.mask_f = at(17420, P), at(12812, N_LEVELS, P)
    k.iota_i = at(14860, 68 + MAX_BLOCKS).bitcast(I32)
    k.scores = lambda t, h: k.S[:, h % 2, :] if t < 2 or h < 2 else k.S_late[:, h - 2, :]
    k.tiles = [Tile(k, t) for t in range(3)]

    k.actT, k.gpad, k.conv, k.gelu = at(0, FT, T), at(10752, 2, T + FFN_TAPS - 1), at(11780, 2, T), at(12804, 4, T)
    k.gain_1, k.zero = at(14852, D), at(15876, 512)

    k.q, k.k, k.v = at(0, KD, T), at(4096, KD, T), at(8192, TT, D)
    k.dist, k.sm = at(12288, T), [at(12800, 2, T), at(13824, 2, T), at(16384, 2, T)]
    k.aT, k.hd = at(14848, 2, T), at(15872, T)
    k.dist_i = at(12800, T).bitcast(I32)
    k.nmax, k.esum, k.hsmall = at(17408, 2, 4), at(17416, 2, 5), at(17426, 4, TT)
    k.gate_diff, k.gate_diff_b, k.tmp_diff = at(0, D), at(D, D), at(12800, 2, 512)
    k.ln, k.sp, k.tt = at(12288, SB_W), at(13568, SB_W), at(14848, 2, SB_W)
    k.minus_ones, k.minus_later, k.far = at(17408, P), at(17536, P), at(17664, P)
    k.gate_sb, k.gate_sb_b, k.tmp_sb = at(12288, D), at(13568, D), at(14848, 2, 512)

    k.big = at(4096, EXTRA * E)
    k.xg, k.xT, k.sg, k.hid, k.hTt, k.ys = (at(8192, D), at(9216, KD, P), at(10240, HID), at(10752, HID), at(11264, KH, P),
                                            at(11776, D))
    route_at, off = {}, 12800
    for name, n in ROUTE:
        route_at[name] = at(off, TT, n)
        off += TT * n
    for name, n in (("count", E), ("blocks", E), ("end", E), ("start", E), ("first", E), ("owner", EXTRA), ("slot_f", 2 * TT)):
        route_at[name] = at(off, n)
        off += n
    route_at["cmp"] = at(off, E, 8)
    off += E * 8
    k.sel = at(off, TT, E)
    off += TT * E
    k.route = lambda name: route_at[name]
    k.rw = at(off, KD, 36)
    off += KD * 36
    k.rb = at(off, 36)
    off += 36
    k.gate_m, k.gate_m_b = at(off, D), at(off + D, D)
    off += 2 * D
    assert off + D <= ARENA, off
    k.gain_2 = at(off, D)
    k.yg = at(0, 2 * TT, D)


def semaphores(nc, prefix, names):
    return [nc.alloc_semaphore(name=prefix + n) for n in names.split()]


@contextmanager
def part(nc):
    before = nc.snapshot_sems()
    yield
    nc.all_engine_barrier()
    nc.clear_and_free_semaphores(nc.allocated_since(before))
    nc.all_engine_barrier()


def norm_group(nc, k, where, n, rows):
    norm, row = ({name: nc.alloc_semaphore(name=where + prefix + name) for name in counts}
                 for prefix, counts in (("norm_", NORM_COUNTS), ("row_norm_", ROW_NORM_COUNTS)))
    return [Norm(k, norm, NORM_COUNTS, i) for i in range(n)], [Norm(k, row, ROW_NORM_COUNTS, i) for i in range(rows)]


def piece(st, src, c0, n, at=0, width=512, chunks=KD):
    view = st.view(len(st.pieces), chunks, width)
    return view[:, :, at:at + n], src[:, :, c0:c0 + n]


def plan_first_block(k, w):
    s, st = "first", k.stream1
    k.w = st.view
    w_in = rows_strided(w["w_in"][0])
    k.w_in_piece, k.ada_piece = {}, {}
    for j in job_order():
        n = len(st.pieces)
        if j in (0, 4, 8, 12):
            st.add([piece(st, w_in, 128 * j, 512)], s, "main_done", job_count(j + 3))
            k.w_in_piece.update({j + i: n for i in range(4)})
        elif j == 16:
            st.add([piece(st, w_in, 2048, 256, 0, 272), piece(st, w_in, 2816, RANK, 256, 272)], s, "main_done", job_count(18))
            k.w_in_piece.update({j + i: n for i in range(3)})
        elif j == 19:
            st.add([piece(st, w_in, 2304, 512)], s, "main_done", job_count(22))
            k.w_in_piece.update({j + i: n for i in range(4)})
        elif j >= ADA_JOB and j % 2 == ADA_JOB % 2:
            a = (j - ADA_JOB) // 2
            l, c = divmod(a, ADA_PIECES // 2)
            st.add([piece(st, rows_strided(w["ada_w"][l]), c * 512, 512)], s, "main_done", job_count(j))
            k.ada_piece[a] = n
    k.w_out_piece = len(st.pieces)
    for n, half in enumerate((1, 0)):
        st.add([piece(st, rows_tiled(w["w_out"][0]), half * 512, 512)], s, "w_out_done", TT * (n + 1))
    k.ffn_piece = len(st.pieces)
    for c in range(FFN_PIECES):
        tiles = gate_tiles(c)
        n = len(tiles) * P
        for name, used in (("ffn_w_gate", "ffn_gate"), ("ffn_w_val", "ffn_val")):
            st.add([piece(st, rows_strided(w[name][0]), c * 512, n, 0, n)], s, used, tiles[-1] + 1)
    k.down_piece = len(st.pieces)
    down = rows_tiled(w["ffn_w_down"][0])
    for half in range(2):
        for r, (c0, n) in enumerate(DOWN_CHUNKS):
            used = ("down_done", TT * (half + 1)) if r == len(DOWN_CHUNKS) - 1 else ("down_piece_used", 2 * half + r + 1)
            st.add([piece(st, down[:, c0:c0 + n, :], half * 512, 512, chunks=n)], s, *used)


def plan_attention(st, a, w_in, w_out):
    for n in range(6):
        st.add([piece(st, rows_strided(w_in), n * 512, 512)], a, "proj", 4 * (n + 1))
    for half in range(2):
        st.add([piece(st, rows_tiled(w_out), half * 512, 512)], a, "out", TT * (half + 1))


def first_block(nc, k, w):
    s = k.s = Kit()
    (s.S_clear, s.four_ready, s.ident_ready, s.pads_ready, s.masks_ready, s.iota_ready, s.pool_chain, s.dve_chain,
     s.rows_landed, s.rows_turned, s.cols_ready, s.lam_landed, s.lam_prod, s.lam_sum, s.lam_exp, s.lam_diff,
     s.lam_ready, s.gains_landed, s.cond_landed, s.small_landed, s.x_landed, s.main_done, s.main_emptied,
     s.unit_done, s.unit_emptied, s.out_done, s.out_turned, s.par_act, s.par_pool, s.sp_recip, s.lb_arg,
     s.cond_ready, s.f_ready, s.ln_ready, s.cum_ready, s.arg_ready, s.exp_ready, s.prep_ready, s.A_normed,
     s.A_emptied, s.C_normed, s.C_emptied, s.gw_ready, s.bd_clear, s.bd_landed, s.conv_ready, s.gelu_ready, s.B_tanh,
     s.B_a, s.B_square, s.B_sqrt, s.B_sqrt_used, s.B_scan, s.oT_pool, s.row_out, s.w_out_done, s.x_again, s.x1_ready,
     s.ffn_pads, s.ffn_gate, s.ffn_gate_out, s.ffn_val, s.ffn_val_out, s.ffn_conv, s.ffn_gelu, s.down_piece_used,
     s.down_done, s.x2_ready, s.zero_ready, s.slots_clear, s.mod_landed, s.mod_steps, s.mod_ready, s.gain_landed) = semaphores(
        nc, "", """S_clear four_ready ident_ready pads_ready masks_ready iota_ready pool_chain dve_chain rows_landed
        rows_turned cols_ready lam_landed lam_prod lam_sum lam_exp lam_diff lam_ready gains_landed
        cond_landed small_landed x_landed main_done main_emptied unit_done unit_emptied out_done out_turned
        par_act par_pool sp_recip lb_arg cond_ready f_ready ln_ready cum_ready arg_ready exp_ready
        prep_ready A_normed A_emptied C_normed C_emptied gw_ready bd_clear bd_landed conv_ready gelu_ready
        B_tanh B_a B_square B_sqrt B_sqrt_used B_scan oT_pool row_out w_out_done x_again x1_ready ffn_pads
        ffn_gate ffn_gate_out ffn_val ffn_val_out ffn_conv ffn_gelu down_piece_used down_done x2_ready
        zero_ready slots_clear mod_landed mod_steps mod_ready gain_landed""")
    k.used["first"] = {"main_done": s.main_done, "w_out_done": s.w_out_done, "ffn_gate": s.ffn_gate, "ffn_val": s.ffn_val,
                       "down_piece_used": s.down_piece_used, "down_done": s.down_done}
    s.osq, s.ovar, s.oroot = ([nc.alloc_semaphore(name=f"{n}{i}") for i in range(2)] for n in ("osq", "ovar", "oroot"))
    k.norms, (last,) = norm_group(nc, k, "first_", 2, 1)
    for i, n in enumerate(k.norms):
        n.gain, n.shift = (lambda c, i=i: k.gains[:, i, c:c + 1]), (lambda c: 0.0)

    def x_landed(eng):
        eng.wait_ge(s.x_landed, 16)

    def x1(eng):
        eng.wait_ge(s.x1_ready, 8)

    def x2(eng):
        eng.wait_ge(s.x2_ready, 8)

    def gains(eng):
        eng.wait_ge(s.gains_landed, 16 * 6)

    with nc.Block() as block:
        @block.sync
        def _(sp):
            sp.dma_start(k.x, w["x"][0].rearrange("(t p) d -> p t d", p=P)).then_inc(s.x_landed, 16)
            for n in range(k.diff_piece + RING):
                if n == 1:
                    sp.wait_ge(s.rows_landed, 16 * len(PARAM_ROWS))
                    sp.wait_ge(s.gains_landed, 16 * 6)
                    sp.wait_ge(s.lam_landed, 64)
                k.stream1.load(sp, n)

        @block.gpsimd
        def _(pool):
            first_block_gpsimd(pool, k)
            pool.wait_ge(s.prep_ready, 3 * PREPS)
            pool.wait_ge(s.out_done, 4)
            pool.dma_start(k.x, w["x"][0].rearrange("(t p) d -> p t d", p=P)).then_inc(s.x_again, 16)
            pool.wait_ge(s.ffn_pads, 1)
            pool.memset(k.zero, 0.0).then_inc(s.zero_ready, 1)
            pool.dma_start(k.gain_1, w["norm_final"].rearrange("(a d) -> a d", a=1).to_broadcast([P, D])).then_inc(s.gain_landed, 16)
            pool.wait_ge(s.zero_ready, 1)
            for slots in (k.x_slots, k.y_slots):
                dst = slots.rearrange("(p r) (h n) -> p (r h) n", p=P, h=2)
                pool.dma_start(dst, k.zero.unsqueeze(1).to_broadcast([P, 2 * SLOTS // P, 512])).then_inc(s.slots_clear, 16)
            modulation_gpsimd(pool, k)
            pool.wait_ge(s.slots_clear, 32)

        @block.scalar
        def _(act):
            act.dma_start(k.cvec[:, :], w["c"][0].rearrange("(p k) -> p k", p=P)).then_inc(s.cond_landed, 16)
            for name, n in PARAM_ROWS:
                r = k.rows[PARAM_AT[name]:PARAM_AT[name] + n, :]
                act.dma_start(r, w["row_" + name]).then_inc(s.rows_landed, 16)
            for i, name in enumerate(("norm_mix", "norm_ffn")):
                act.dma_start(k.gains[:, i, :], w[name][0].rearrange("(p k) -> p k", p=P)).then_inc(s.gains_landed, 16)
            for l in range(2):
                for i, name in enumerate(("norm1_g", "norm2_g")):
                    act.dma_start(k.gains[:, 2 + 2 * l + i, :], w[name][l].rearrange("(p k) -> p k", p=P)).then_inc(s.gains_landed, 16)
            for i, name in enumerate(("q1", "k1", "q2", "k2")):
                act.dma_start(k.lvec[:, i:i + 1], w["lambda_" + name][0].rearrange("(d a) -> d a", a=1)).then_inc(s.lam_landed, 16)
            act.dma_start(k.gate_up[:, :], w["gla_w_gate_up"][0]).then_inc(s.small_landed, 16)
            act.dma_start(k.normw[:, 0:256], w["hgrn_norm"].to_broadcast([P, 256])).then_inc(s.small_landed, 16)
            act.dma_start(k.normw[:, 256:512], w["gla_norm"].to_broadcast([P, 256])).then_inc(s.small_landed, 16)
            act.wait_ge(s.lam_sum, 1)
            act.activation(k.lexp[:, :], k.ps[:, 1, 0:2], ACT.Exp).then_inc(s.lam_exp, 1)
            gains(act)
            norm_scalar(act, k, k.norms[0], x_landed)
            first_block_scalar(act, k)
            norm_scalar(act, k, k.norms[1], x1)
            ffn_scalar(act, k)
            row_norm_scalar(act, k, last, x2)

        @block.tensor
        def _(pe):
            parameters_tensor(pe, k)
            norm_tensor(pe, k, k.norms[0])
            first_block_tensor(pe, k)
            norm_tensor(pe, k, k.norms[1])
            ffn_tensor(pe, k)

        @block.vector
        def _(dve):
            ch = Chain(dve, s.dve_chain)
            parameters_vector(dve, k)
            norm_vector(dve, k, k.norms[0], x_landed, gains)
            first_block_vector(dve, k, ch)
            norm_vector(dve, k, k.norms[1], x1, gains)
            ffn_vector(dve, k, ch)
            dve.wait_ge(s.gain_landed, 16)
            row_norm_vector(dve, k, last, x2, k.gain_1, k.x)


def second_block_layer(nc, k, w, out, l):
    s, a, m = Kit(), Kit(), Kit()
    a.q_scale = [HEAD ** -0.5 / (slope if l == 0 else 1.0) for slope in head_slopes()]
    k.s, a.stream, a.first_piece = s, (k.stream1, k.stream2)[l], (k.diff_piece, 0)[l]
    (s.dve_chain, s.dist_steps, s.dist_ready, s.later_ready, s.gain_landed, s.stored) = semaphores(
        nc, f"layer{l}_", """dve_chain dist_steps dist_ready later_ready gain_landed stored""")
    (a.proj, a.proj_act, a.proj_dve, a.out, a.gated, a.x_ready, a.gate_landed, a.gate_ready, a.scored, a.valued,
     a.exped, a.oT_out) = semaphores(
        nc, f"attention{l}_", """proj proj_act proj_dve out gated x_ready gate_landed gate_ready scored valued exped oT_out""")
    if l == 0:
        (a.biased, a.maxed, a.weighed, a.turned, a.turned_out, a.squared, a.var, a.rooted, a.head_normed, a.head_turned) = semaphores(
            nc, "diff_", """biased maxed weighed turned turned_out squared var rooted head_normed head_turned""")
    else:
        (a.steps, a.logged, a.softplus, a.summed) = semaphores(
            nc, "sb_", """steps logged softplus summed""")
    k.used[("diff", "sb")[l]] = {"proj": a.proj, "out": a.out}
    (m.router_landed, m.logits, m.g_diff, m.e_diff, m.exps, m.chosen, m.ranked, m.routed, m.scattered, m.x_landed,
     m.x_turned, m.xT_act, m.xT_dve, m.gate_landed, m.up_landed, m.down_landed, m.gated, m.upped, m.downed, m.hidden,
     m.silu, m.h_turned, m.hT_out, m.y_act, m.y_dve, m.y_stored, m.weights_ready, m.weighed, m.slots_set, m.all_stored, m.gate_rows, m.gate_ready, m.x_ready) = semaphores(
        nc, f"moe{l}_", """router_landed logits g_diff e_diff exps chosen ranked routed scattered x_landed x_turned xT_act
        xT_dve gate_landed up_landed down_landed gated upped downed hidden silu h_turned hT_out y_act y_dve
        y_stored weights_ready weighed slots_set all_stored gate_rows gate_ready x_ready""")
    m.gathered = [nc.alloc_semaphore(name=f"moe{l}_gathered{t}") for t in range(TT)]
    m.w_gate, m.w_up, m.w_down = (w[n][l] for n in ("expert_w_gate", "expert_w_up", "expert_w_down"))
    (norm1, m.norm), (last,) = norm_group(nc, k, f"layer{l}_", 2, 1)
    a.norm = norm1
    for v, n in enumerate((norm1, m.norm)):
        n.gain = lambda c, v=v: k.mod[:, l, 2 * v + 1, c:c + 1]
        n.shift = lambda c, v=v: k.mod[:, l, 2 * v, c:c + 1]
    gate, gate_b, tmp = (k.gate_diff, k.gate_diff_b, k.tmp_diff) if l == 0 else (k.gate_sb, k.gate_sb_b, k.tmp_sb)

    def from_before(eng):
        pass

    def after_attention(eng):
        eng.wait_ge(a.x_ready, 8)

    def after_moe(eng):
        eng.wait_ge(m.x_ready, TT)

    with nc.Block() as block:
        @block.sync
        def _(sp):
            for n in range(a.first_piece + RING, a.first_piece + 8):
                a.stream.load(sp, n)
            n_pairs, used = moe_sync(sp, k, m, a)
            if l == 0:
                for n in range(RING):
                    if n % 2 == 0:
                        sp.wait_ge(used[n // 2], n_pairs + 1)
                    k.stream2.load(sp, n)
            else:
                last.after(sp, "normed", TT)
                sp.dma_start(out[0].rearrange("(t p) d -> p t d", p=P), k.x).then_inc(s.stored, 16)
                sp.wait_ge(s.stored, 16)

        @block.gpsimd
        def _(pool):
            if l == 0:
                distances_gpsimd(pool, k)
                pool.wait_ge(a.scored, DIFF_UNITS)
                gate_rows(pool, k, l, 2, gate, gate_b, a.gate_landed, a.gate_ready)
            else:
                pool.memset(k.minus_ones, -1.0)
                pool.memset(k.far, 0.0).then_inc(s.later_ready, 1)
                pool.wait_ge(s.later_ready, 1)
                pool.affine_select(out=k.far, in_=k.far, compare_op=ALU.is_gt, fill=-F_FAR, base=0,
                                   pattern=[[1, P]], channel_multiplier=-1)
                pool.affine_select(out=k.minus_later, in_=k.minus_ones, compare_op=ALU.is_ge, fill=0.0, base=0,
                                   pattern=[[-1, P]], channel_multiplier=1).then_inc(s.later_ready, 1)
                pool.wait_ge(a.softplus, SB_HEADS)
                pool.wait_ge(a.summed, SB_HEADS)
                gate_rows(pool, k, l, 2, gate, gate_b, a.gate_landed, a.gate_ready)
            pool.wait_ge(m.routed, 1)
            gate_rows(pool, k, l, 5, k.gate_m, k.gate_m_b, m.gate_rows, m.gate_ready)
            if l == 1:
                gain = w["final_norm_g"].rearrange("(a d) -> a d", a=1).to_broadcast([P, D])
                pool.wait_ge(m.gate_ready, 1)
                pool.dma_start(k.gain_2, gain).then_inc(s.gain_landed, 16)
            moe_gpsimd(pool, k, m)

        @block.scalar
        def _(act):
            norm_scalar(act, k, norm1, from_before)
            qkv_scalar(act, k, a)
            (diff_scalar, sb_scalar)[l](act, k, a)
            after_attention(act)
            act.dma_start(k.rw[:, :, 0:GROUPS], rows_strided(w["router_group_w"][l])).then_inc(m.router_landed, 16)
            act.dma_start(k.rw[:, :, GROUPS:36], rows_strided(w["router_expert_w"][l])).then_inc(m.router_landed, 16)
            act.dma_start(k.rb[:, 0:GROUPS], w["router_group_b"][l:l + 1].to_broadcast([P, GROUPS])).then_inc(m.router_landed, 16)
            act.dma_start(k.rb[:, GROUPS:36], w["router_expert_b"][l:l + 1].rearrange("a g e -> a (g e)").to_broadcast([P, E]))                .then_inc(m.router_landed, 16)
            norm_scalar(act, k, m.norm, after_attention)
            router_scalar(act, k, m)
            moe_scalar(act, k, m)
            combine_scalar(act, k, m)
            if l == 1:
                row_norm_scalar(act, k, last, after_moe)

        @block.tensor
        def _(pe):
            norm_tensor(pe, k, norm1)
            qkv_tensor(pe, k, a)
            if l == 1:
                pe.wait_ge(s.later_ready, 2)
            (diff_tensor, sb_tensor)[l](pe, k, a)
            out_proj_tensor(pe, k, a)
            norm_tensor(pe, k, m.norm)
            router_tensor(pe, k, m)
            moe_tensor(pe, k, m)

        @block.vector
        def _(dve):
            ch = Chain(dve, s.dve_chain)
            norm_vector(dve, k, norm1, from_before, from_before)
            qkv_vector(dve, k, a)
            if l == 0:
                diff_vector(dve, k, a, ch)
            else:
                sb_vector(dve, k, a)
            out_proj_vector(dve, k, a, gate, tmp)
            norm_vector(dve, k, m.norm, after_attention, from_before)
            router_vector(dve, k, m, ch)
            moe_vector(dve, k, m)
            combine_vector(dve, k, m, ch)
            if l == 1:
                dve.wait_ge(s.gain_landed, 16)
                row_norm_vector(dve, k, last, after_moe, k.gain_2, k.x)


def two_block_kernel(nc, w, out):
    with ExitStack() as ctx:
        k = Kit()
        place(k, nc, ctx)
        k.mod_dram = nc.dram_tensor("modulation", [ADA_PIECES, 512], F32).ap()
        k.mod_rows = k.mod_dram.rearrange("(l v h) n -> l v (h n)", l=2, v=6)
        k.x_slots = nc.dram_tensor("token_slots", [SLOTS, D], F32).ap()
        k.y_slots = nc.dram_tensor("output_slots", [SLOTS, D], F32).ap()
        k.ada_b, k.rg_w_a, k.rg_w_x = w["ada_b"], w["rg_w_a"], w["rg_w_x"]
        k.used = {}
        k.stream1, k.stream2 = (Stream(k, [ctx.enter_context(nc.semaphore(f"ring{i}_{n}")) for n in range(RING)]) for i in range(2))
        plan_first_block(k, w)
        k.diff_piece = len(k.stream1.pieces)
        plan_attention(k.stream1, "diff", w["diff_w_in"][0], w["diff_w_out"][0])
        plan_attention(k.stream2, "sb", w["sb_w_in"][0], w["sb_w_out"][0])
        with part(nc):
            first_block(nc, k, w)
        for l in range(2):
            with part(nc):
                second_block_layer(nc, k, w, out, l)


_INS = {
    "x": ("x", None), "norm_mix": ("norm_mix", None), "w_in": ("w_in", None), "hgrn_norm": ("hgrn_norm", None),
    "rg_w_a": ("rg_w_a", None), "rg_w_x": ("rg_w_x", None), "gla_w_gate_up": ("gla_w_gate_up", None),
    "gla_norm": ("gla_norm", None), "w_out": ("w_out", None), "norm_ffn": ("norm_ffn", None),
    "ffn_w_gate": ("ffn_w_gate", None), "ffn_w_val": ("ffn_w_val", None), "ffn_w_down": ("ffn_w_down", None),
    "norm_final": ("norm_final", None),
    "row_ffn_w": ("ffn_conv_w", (-1, P)), "row_ffn_b": ("ffn_conv_b", (-1, P)), "row_rg_w": ("rg_conv_w", (-1, P)),
    "row_rg_b": ("rg_conv_b", (-1, P)), "row_rg_b_a": ("rg_b_a", (-1, P)), "row_rg_b_x": ("rg_b_x", (-1, P)),
    "row_rg_lambda": ("rg_lambda", (-1, P)), "row_lower": ("hgrn_lower_bounds", (-1, P)),
    "row_gla_b": ("gla_b_gate", (-1, P)), "row_subln": ("diff_subln_g_2", (-1, P)),
    "c": ("c_2", None), "norm1_g": ("norm1_g_2", None), "norm2_g": ("norm2_g_2", None), "ada_w": ("ada_w_2", None),
    "ada_b": ("ada_b_2", None), "diff_w_in": ("diff_w_in_2", None), "diff_w_out": ("diff_w_out_2", None),
    "lambda_q1": ("diff_lambda_q1_2", None), "lambda_k1": ("diff_lambda_k1_2", None),
    "lambda_q2": ("diff_lambda_q2_2", None), "lambda_k2": ("diff_lambda_k2_2", None),
    "sb_w_in": ("sb_w_in_2", None), "sb_w_out": ("sb_w_out_2", None), "router_group_w": ("router_group_w_2", None),
    "router_group_b": ("router_group_b_2", None), "router_expert_w": ("router_expert_w_2", None),
    "router_expert_b": ("router_expert_b_2", None), "expert_w_gate": ("expert_w_gate_2", None),
    "expert_w_up": ("expert_w_up_2", None), "expert_w_down": ("expert_w_down_2", None),
    "final_norm_g": ("final_norm_g_2", None),
}


def kernel(**inputs):
    import numpy as _np
    import concourse.bacc as _bacc
    from concourse.bass_utils import run_bass_kernel_spmd as _run

    nc = _bacc.Bacc("TRN2", target_bir_lowering=False, num_devices=1)
    arrays, w = {}, {}
    for name, (source, shape) in _INS.items():
        a = _np.ascontiguousarray(inputs[source])
        if shape:
            a = a.reshape(shape)
        arrays[f"in_{name}"] = a
        w[name] = nc.dram_tensor(f"in_{name}", a.shape, mybir.dt.from_np(a.dtype), kind="ExternalInput").ap()
    out = nc.dram_tensor("out", (1, T, D), F32, kind="ExternalOutput").ap()
    two_block_kernel(nc, w, out)
    r = _run(nc, [arrays], core_ids=[0])
    return r.results[0]["out"]
```
